# Optimizing a Trainium2 kernel written in Bass

```python
import jax, jax.numpy as jnp
from jax import lax
import numpy as np
import math

D_MODEL = 1024
BATCH = 1
SEQ = 256
DEPTH = 1

MLA_HEADS = 8
MLA_NOPE_DIM = 64
MLA_ROPE_DIM = 32
MLA_V_DIM = 64
MLA_Q_RANK = 256
MLA_KV_RANK = 128
MLA_WIDTH = MLA_HEADS * MLA_V_DIM
MOBA_HEADS = 8
MOBA_HEAD_DIM = 64
MOBA_WIDTH = MOBA_HEADS * MOBA_HEAD_DIM
MOBA_BLOCK = 256
MOBA_TOPK = 3
MOBA_Q_CHUNK = 16
ATTN_Q_BLOCK = 128
ROPE_THETA = 10000.0
EPS = 1e-6
N_BRANCHES = 2
IN_SIZES = (MLA_Q_RANK, MLA_KV_RANK, MLA_ROPE_DIM, MLA_WIDTH,
            MOBA_WIDTH, MOBA_WIDTH, MOBA_WIDTH, MOBA_WIDTH, N_BRANCHES * D_MODEL)
D_IN = MLA_Q_RANK + MLA_KV_RANK + MLA_ROPE_DIM + MLA_WIDTH + 4 * MOBA_WIDTH + N_BRANCHES * D_MODEL


def rms_norm(t, g):
    tf = t.astype(jnp.float32)
    tf = tf * lax.rsqrt(jnp.mean(tf * tf, axis=-1, keepdims=True) + EPS)
    return (tf * g.astype(jnp.float32)).astype(t.dtype)

def apply_rope(t, positions):
    half = t.shape[-1] // 2
    inv_freq = ROPE_THETA ** (-jnp.arange(half, dtype=jnp.float32) / half)
    ang = positions.astype(jnp.float32)[:, :, None, None] * inv_freq
    cos, sin = jnp.cos(ang), jnp.sin(ang)
    tf = t.astype(jnp.float32)
    t1, t2 = tf[..., :half], tf[..., half:]
    return jnp.concatenate([t1 * cos - t2 * sin, t2 * cos + t1 * sin], axis=-1).astype(t.dtype)

def split_cols(t, sizes):
    outs, start = [], 0
    for n in sizes:
        outs.append(t[..., start:start + n])
        start += n
    return outs

def causal_dense_attention(q, k, v, scale):
    B, S, H, _ = q.shape
    kpos = jnp.arange(S)

    def one_block(i):
        start = i * ATTN_Q_BLOCK
        qb = lax.dynamic_slice_in_dim(q, start, ATTN_Q_BLOCK, axis=1)
        s = jnp.einsum('bqhd,bkhd->bhqk', qb, k).astype(jnp.float32) * scale
        qpos = start + jnp.arange(ATTN_Q_BLOCK)
        s = jnp.where(kpos[None, :] <= qpos[:, None], s, -jnp.inf)
        p = jax.nn.softmax(s, axis=-1).astype(v.dtype)
        return jnp.einsum('bhqk,bkhd->bqhd', p, v)

    out = lax.map(one_block, jnp.arange(S // ATTN_Q_BLOCK))
    return out.transpose(1, 0, 2, 3, 4).reshape(B, S, H, v.shape[-1])

def moba_attention(q, k, v):
    B, S, H, dh = q.shape
    nb = -(-S // MOBA_BLOCK)
    n_top = min(MOBA_TOPK, nb)
    pad = nb * MOBA_BLOCK - S
    kp = jnp.pad(k, ((0, 0), (0, pad), (0, 0), (0, 0)))
    vp = jnp.pad(v, ((0, 0), (0, pad), (0, 0), (0, 0)))
    kb = kp.reshape(B, nb, MOBA_BLOCK, H, dh).transpose(0, 3, 1, 2, 4)
    vb = vp.reshape(B, nb, MOBA_BLOCK, H, dh).transpose(0, 3, 1, 2, 4)
    kmean = jnp.mean(kb.astype(jnp.float32), axis=3)
    scale = dh ** -0.5
    bi = jnp.arange(B)[:, None, None, None]
    hi = jnp.arange(H)[None, :, None, None]
    in_blk = jnp.arange(MOBA_BLOCK)
    blk_ids = jnp.arange(nb)
    n_sel = n_top * MOBA_BLOCK

    def one_chunk(i):
        start = i * MOBA_Q_CHUNK
        qc = lax.dynamic_slice_in_dim(q, start, MOBA_Q_CHUNK, axis=1)
        qpos = start + jnp.arange(MOBA_Q_CHUNK)
        own = start // MOBA_BLOCK
        gate = jnp.einsum('bqhd,bhnd->bhqn', qc.astype(jnp.float32), kmean)
        gate = jnp.where(blk_ids < own, gate, -jnp.inf)
        _, idx = lax.top_k(gate, n_top)
        valid = jnp.arange(n_top) < own
        k_sel = kb[bi, hi, idx]
        v_sel = vb[bi, hi, idx]
        s_sel = jnp.einsum('bqhd,bhqnkd->bhqnk', qc, k_sel).astype(jnp.float32) * scale
        s_sel = jnp.where(valid[:, None], s_sel, -jnp.inf)
        k_own = lax.dynamic_index_in_dim(kb, own, axis=2, keepdims=False)
        v_own = lax.dynamic_index_in_dim(vb, own, axis=2, keepdims=False)
        s_own = jnp.einsum('bqhd,bhkd->bhqk', qc, k_own).astype(jnp.float32) * scale
        kpos_own = own * MOBA_BLOCK + in_blk
        s_own = jnp.where(kpos_own[None, :] <= qpos[:, None], s_own, -jnp.inf)
        s = jnp.concatenate([s_sel.reshape(B, H, MOBA_Q_CHUNK, n_sel), s_own], axis=-1)
        p = jax.nn.softmax(s, axis=-1).astype(v.dtype)
        p_sel = p[..., :n_sel].reshape(B, H, MOBA_Q_CHUNK, n_top, MOBA_BLOCK)
        p_own = p[..., n_sel:]
        return (jnp.einsum('bhqnk,bhqnkd->bqhd', p_sel, v_sel)
                + jnp.einsum('bhqk,bhkd->bqhd', p_own, v_own))

    out = lax.map(one_chunk, jnp.arange(S // MOBA_Q_CHUNK))
    return out.transpose(1, 0, 2, 3, 4).reshape(B, S, H, dh)

def first_inputs(seed: int = 0) -> dict:
    key = jax.random.key(seed)
    ks = jax.random.split(key, 20)

    def w(k, shape, fan_in, mult=1.0):
        return jax.random.normal(k, shape, jnp.float32) * (mult * fan_in ** -0.5)

    def gain(k, n):
        return 1.0 + 0.05 * jax.random.normal(k, (DEPTH, n), jnp.float32)

    x = jax.random.normal(ks[0], (BATCH, SEQ, D_MODEL), jnp.float32)
    c = jax.random.normal(ks[1], (BATCH, D_MODEL), jnp.float32)
    offset = jax.random.randint(ks[2], (BATCH, 1), 0, 1024, dtype=jnp.int32)
    positions = (offset + jnp.arange(SEQ, dtype=jnp.int32)[None, :]).astype(jnp.int32)
    return {
        "x": x,
        "c": c,
        "positions": positions,
        "w_ada": w(ks[3], (DEPTH, D_MODEL, 3 * D_MODEL), D_MODEL, 0.5),
        "b_ada": 0.01 * jax.random.normal(ks[4], (DEPTH, 3 * D_MODEL), jnp.float32),
        "g_pre": gain(ks[5], D_MODEL),
        "g_post": gain(ks[6], D_MODEL),
        "w_in": w(ks[7], (DEPTH, D_MODEL, D_IN), D_MODEL),
        "g_q_lat": gain(ks[8], MLA_Q_RANK),
        "w_uq": w(ks[9], (DEPTH, MLA_Q_RANK, MLA_HEADS * (MLA_NOPE_DIM + MLA_ROPE_DIM)), MLA_Q_RANK),
        "g_kv_lat": gain(ks[10], MLA_KV_RANK),
        "w_ukv": w(ks[11], (DEPTH, MLA_KV_RANK, MLA_HEADS * (MLA_NOPE_DIM + MLA_V_DIM)), MLA_KV_RANK),
        "w_o_mla": w(ks[12], (DEPTH, MLA_WIDTH, D_MODEL), MLA_WIDTH),
        "w_o_moba": w(ks[13], (DEPTH, MOBA_WIDTH, D_MODEL), MOBA_WIDTH),
        "b_merge": 0.01 * jax.random.normal(ks[14], (DEPTH, N_BRANCHES * D_MODEL), jnp.float32),
        "w_out": w(ks[15], (DEPTH, D_MODEL, D_MODEL), D_MODEL),
    }

def first_block(x, c, positions, w_ada, b_ada, g_pre, g_post, w_in, g_q_lat, w_uq,
              g_kv_lat, w_ukv, w_o_mla, w_o_moba, b_merge, w_out):
    B, S, D = x.shape
    for l in range(DEPTH):
        mod = jax.nn.silu(c) @ w_ada[l] + b_ada[l]
        shift, scale, gate = jnp.split(mod, 3, axis=-1)
        h = rms_norm(x, g_pre[l]) * (1 + scale[:, None, :]) + shift[:, None, :]

        proj = h @ w_in[l]
        (q_lat, kv_lat, k_rope, z_mla, q_mb, k_mb, v_mb, z_mb,
         merge_logits) = split_cols(proj, IN_SIZES)

        q = (rms_norm(q_lat, g_q_lat[l]) @ w_uq[l]).reshape(B, S, MLA_HEADS, MLA_NOPE_DIM + MLA_ROPE_DIM)
        q_nope, q_pe = q[..., :MLA_NOPE_DIM], q[..., MLA_NOPE_DIM:]
        kv = (rms_norm(kv_lat, g_kv_lat[l]) @ w_ukv[l]).reshape(B, S, MLA_HEADS, MLA_NOPE_DIM + MLA_V_DIM)
        k_nope, v_mla = kv[..., :MLA_NOPE_DIM], kv[..., MLA_NOPE_DIM:]
        q_pe = apply_rope(q_pe, positions)
        k_pe = apply_rope(k_rope[:, :, None, :], positions)
        q_full = jnp.concatenate([q_nope, q_pe], axis=-1)
        k_full = jnp.concatenate([k_nope, jnp.broadcast_to(k_pe, (B, S, MLA_HEADS, MLA_ROPE_DIM))], axis=-1)
        o_mla = causal_dense_attention(q_full, k_full, v_mla,
                                       (MLA_NOPE_DIM + MLA_ROPE_DIM) ** -0.5).reshape(B, S, MLA_WIDTH)
        y_mla = (o_mla * jax.nn.silu(z_mla)) @ w_o_mla[l]

        qm = apply_rope(q_mb.reshape(B, S, MOBA_HEADS, MOBA_HEAD_DIM), positions)
        km = apply_rope(k_mb.reshape(B, S, MOBA_HEADS, MOBA_HEAD_DIM), positions)
        vm = v_mb.reshape(B, S, MOBA_HEADS, MOBA_HEAD_DIM)
        o_mb = moba_attention(qm, km, vm).reshape(B, S, MOBA_WIDTH)
        y_mb = (o_mb * jax.nn.silu(z_mb)) @ w_o_moba[l]

        gates = jax.nn.sigmoid(merge_logits + b_merge[l])
        g_a, g_b = jnp.split(gates, 2, axis=-1)
        y = (g_a * y_mla + g_b * y_mb) @ w_out[l]

        x = x + gate[:, None, :] * rms_norm(y, g_post[l])
    return x


DEPTH_2 = 2

N_MIXERS = 2
N_NSA_LAYERS = (DEPTH_2 + 1) // 2
N_DIFF_LAYERS = DEPTH_2 // 2
HEAD_DIM = 64
ROPE_DIM = HEAD_DIM // 4
ROPE_THETA_2 = 500000.0
NSA_HEADS = D_MODEL // HEAD_DIM
NSA_GROUPS = 4
NSA_HPG = NSA_HEADS // NSA_GROUPS
CMP_BLOCK = 32
CMP_STRIDE = 16
CMP_HIDDEN = 2 * HEAD_DIM
SEL_BLOCK = 64
SEL_TOPK = 16
WINDOW = 512
NSA_Q_CHUNK = 64
NSA_Q_W = NSA_HEADS * HEAD_DIM
NSA_KV_W = NSA_GROUPS * HEAD_DIM
NSA_IN = NSA_Q_W + 6 * NSA_KV_W + 3 * NSA_HEADS
DIFF_HEADS = D_MODEL // (2 * HEAD_DIM)
DIFF_V_DIM = 2 * HEAD_DIM
DIFF_W = DIFF_HEADS * 2 * HEAD_DIM
DIFF_IN = 3 * DIFF_W
ATT_BLOCK = 128
D_FF = 4 * D_MODEL
NEG_INF = -1e30
SEL_FORCE = 1e6


def rms_norm_2(x, g):
    xf = x.astype(jnp.float32)
    y = xf * lax.rsqrt(jnp.mean(xf * xf, axis=-1, keepdims=True) + EPS)
    return (y * g.astype(jnp.float32)).astype(x.dtype)

def rope_tables(positions):
    inv = ROPE_THETA_2 ** (-jnp.arange(0, ROPE_DIM, 2, dtype=jnp.float32) / ROPE_DIM)
    ang = positions.astype(jnp.float32)[..., None] * inv
    return jnp.cos(ang), jnp.sin(ang)

def apply_partial_rope(x, cos, sin):
    half = ROPE_DIM // 2
    shape = cos.shape[:2] + (1,) * (x.ndim - 3) + cos.shape[-1:]
    c = cos.reshape(shape)
    s = sin.reshape(shape)
    x1 = x[..., :half].astype(jnp.float32)
    x2 = x[..., half:ROPE_DIM].astype(jnp.float32)
    rot = jnp.concatenate([x1 * c - x2 * s, x2 * c + x1 * s], axis=-1).astype(x.dtype)
    return jnp.concatenate([rot, x[..., ROPE_DIM:]], axis=-1)

def masked_softmax(s, mask):
    return jax.nn.softmax(jnp.where(mask, s, NEG_INF), axis=-1) * mask

def compress_blocks(blk, pe, w1, w2):
    B, NC = blk.shape[:2]
    z = (blk + pe[:, None, :]).transpose(0, 1, 3, 2, 4).reshape(B, NC, NSA_GROUPS, CMP_BLOCK * HEAD_DIM)
    return jax.nn.silu(z @ w1) @ w2

def nsa_mixer(h, cos, sin, w_in, b_gate, q_gain, k_gain, pe_k, w_ck1, w_ck2, pe_v, w_cv1, w_cv2, w_out):
    B, S, _ = h.shape
    G, HPG, dh = NSA_GROUPS, NSA_HPG, HEAD_DIM
    scale = 1.0 / math.sqrt(dh)
    sizes = [NSA_Q_W] + [NSA_KV_W] * 6 + [3 * NSA_HEADS]
    q, kc, vc, ks, vs, kw, vw, gl = jnp.split(h @ w_in, list(np.cumsum(sizes)[:-1]), axis=-1)
    q = rms_norm_2(q.reshape(B, S, NSA_HEADS, dh), q_gain)
    q_rot = apply_partial_rope(q, cos, sin)
    q_cmp = q.reshape(B, S, G, HPG, dh).transpose(0, 2, 3, 1, 4)
    q_rot = q_rot.reshape(B, S, G, HPG, dh).transpose(0, 2, 3, 1, 4)
    gates = jax.nn.sigmoid(gl.astype(jnp.float32) + b_gate.astype(jnp.float32)).reshape(B, S, NSA_HEADS, 3)

    n_cmp = (S - CMP_BLOCK) // CMP_STRIDE + 1
    idx = jnp.arange(n_cmp)[:, None] * CMP_STRIDE + jnp.arange(CMP_BLOCK)[None, :]
    kc = kc.reshape(B, S, G, dh)
    vc = vc.reshape(B, S, G, dh)
    k_cmp = rms_norm_2(compress_blocks(kc[:, idx], pe_k, w_ck1, w_ck2), k_gain[0]).transpose(0, 2, 1, 3)
    v_cmp = compress_blocks(vc[:, idx], pe_v, w_cv1, w_cv2).transpose(0, 2, 1, 3)
    cmp_start = jnp.arange(n_cmp) * CMP_STRIDE
    cmp_end = cmp_start + CMP_BLOCK - 1
    n_sel = S // SEL_BLOCK
    top_n = min(SEL_TOPK, n_sel)
    sel_start = jnp.arange(n_sel) * SEL_BLOCK
    overlap = ((cmp_start[:, None] <= sel_start[None, :] + SEL_BLOCK - 1)
               & (cmp_end[:, None] >= sel_start[None, :])).astype(jnp.float32)

    ks = apply_partial_rope(rms_norm_2(ks.reshape(B, S, G, dh), k_gain[1]), cos, sin)
    ks_blk = ks.transpose(0, 2, 1, 3).reshape(B, G, n_sel, SEL_BLOCK, dh)
    vs_blk = vs.reshape(B, S, G, dh).transpose(0, 2, 1, 3).reshape(B, G, n_sel, SEL_BLOCK, dh)
    kw = apply_partial_rope(rms_norm_2(kw.reshape(B, S, G, dh), k_gain[2]), cos, sin)
    pad = ((0, 0), (0, 0), (WINDOW, 0), (0, 0))
    kw_pad = jnp.pad(kw.transpose(0, 2, 1, 3), pad)
    vw_pad = jnp.pad(vw.reshape(B, S, G, dh).transpose(0, 2, 1, 3), pad)
    b_idx = jnp.arange(B)[:, None, None, None]
    g_idx = jnp.arange(G)[None, :, None, None]
    blk_ids = jnp.arange(n_sel)
    QC = NSA_Q_CHUNK

    def chunk(ci):
        s0 = ci * QC
        t = s0 + jnp.arange(QC)
        qc_ = lax.dynamic_slice_in_dim(q_cmp, s0, QC, axis=3)
        qr_ = lax.dynamic_slice_in_dim(q_rot, s0, QC, axis=3)
        sc = jnp.einsum('bghqd,bgcd->bghqc', qc_, k_cmp).astype(jnp.float32) * scale
        pc = masked_softmax(sc, cmp_end[None, :] <= t[:, None])
        o_cmp = jnp.einsum('bghqc,bgcd->bghqd', pc.astype(v_cmp.dtype), v_cmp)
        imp = jnp.einsum('bghqc,cs->bgqs', pc, overlap)
        bt = (t // SEL_BLOCK)[:, None]
        valid = blk_ids[None, :] <= bt
        forced = (blk_ids[None, :] == 0) | (blk_ids[None, :] == bt) | (blk_ids[None, :] == bt - 1)
        imp = jnp.where(forced, SEL_FORCE, jnp.where(valid, imp, -1.0))
        _, sel = lax.top_k(imp, top_n)
        kg = ks_blk[b_idx, g_idx, sel]
        vg = vs_blk[b_idx, g_idx, sel]
        ss = jnp.einsum('bghqd,bgqnld->bghqnl', qr_, kg).astype(jnp.float32) * scale
        tok = sel[..., None] * SEL_BLOCK + jnp.arange(SEL_BLOCK)
        ms = (tok <= t[:, None, None])[:, :, None]
        shp = ss.shape
        ps = masked_softmax(ss.reshape(shp[:4] + (top_n * SEL_BLOCK,)),
                            ms.reshape(ms.shape[:4] + (top_n * SEL_BLOCK,))).reshape(shp)
        o_sel = jnp.einsum('bghqnl,bgqnld->bghqd', ps.astype(vg.dtype), vg)
        kw_ = lax.dynamic_slice_in_dim(kw_pad, s0, WINDOW + QC, axis=2)
        vw_ = lax.dynamic_slice_in_dim(vw_pad, s0, WINDOW + QC, axis=2)
        kpos = s0 - WINDOW + jnp.arange(WINDOW + QC)
        mw = (kpos[None, :] <= t[:, None]) & (kpos[None, :] > t[:, None] - WINDOW) & (kpos[None, :] >= 0)
        sw = jnp.einsum('bghqd,bgkd->bghqk', qr_, kw_).astype(jnp.float32) * scale
        o_win = jnp.einsum('bghqk,bgkd->bghqd', masked_softmax(sw, mw).astype(vw_.dtype), vw_)
        g = lax.dynamic_slice_in_dim(gates, s0, QC, axis=1)
        g = g.reshape(B, QC, G, HPG, 3).transpose(0, 2, 3, 1, 4).astype(o_win.dtype)
        o = g[..., 0:1] * o_cmp + g[..., 1:2] * o_sel + g[..., 2:3] * o_win
        return o.transpose(0, 3, 1, 2, 4).reshape(B, QC, NSA_Q_W)

    outs = lax.map(chunk, jnp.arange(S // QC))
    return outs.transpose(1, 0, 2, 3).reshape(B, S, NSA_Q_W) @ w_out

def diff_mixer(h, cos, sin, layer_depth, w_in, q_gain, k_gain, lq1, lk1, lq2, lk2, subln_g, w_out):
    B, S, _ = h.shape
    dh = HEAD_DIM
    scale = 1.0 / math.sqrt(dh)
    q, k, v = jnp.split(h @ w_in, [DIFF_W, 2 * DIFF_W], axis=-1)
    q = apply_partial_rope(rms_norm_2(q.reshape(B, S, DIFF_HEADS, 2, dh), q_gain), cos, sin)
    k = apply_partial_rope(rms_norm_2(k.reshape(B, S, DIFF_HEADS, 2, dh), k_gain), cos, sin)
    q = q.transpose(0, 2, 3, 1, 4)
    k = k.transpose(0, 2, 3, 1, 4)
    v = v.reshape(B, S, DIFF_HEADS, DIFF_V_DIM).transpose(0, 2, 1, 3)
    lam_init = 0.8 - 0.6 * math.exp(-0.3 * (layer_depth - 1))
    lam = (jnp.exp(jnp.sum(lq1.astype(jnp.float32) * lk1.astype(jnp.float32)))
           - jnp.exp(jnp.sum(lq2.astype(jnp.float32) * lk2.astype(jnp.float32))) + lam_init)
    kpos = jnp.arange(S)

    def block(bi):
        s0 = bi * ATT_BLOCK
        qb = lax.dynamic_slice_in_dim(q, s0, ATT_BLOCK, axis=3)
        s = jnp.einsum('bhcqd,bhckd->bhcqk', qb, k).astype(jnp.float32) * scale
        t = s0 + jnp.arange(ATT_BLOCK)
        p = masked_softmax(s, kpos[None, :] <= t[:, None])
        a = p[:, :, 0] - lam * p[:, :, 1]
        o = jnp.einsum('bhqk,bhkd->bhqd', a.astype(v.dtype), v)
        o = rms_norm_2(o, subln_g) * (1.0 - lam_init)
        return o.transpose(0, 2, 1, 3).reshape(B, ATT_BLOCK, DIFF_W)

    outs = lax.map(block, jnp.arange(S // ATT_BLOCK))
    return outs.transpose(1, 0, 2, 3).reshape(B, S, DIFF_W) @ w_out

def second_inputs(seed: int = 0) -> dict:
    key = jax.random.key(seed)
    ks = iter(jax.random.split(key, 32))
    D = D_MODEL

    def nrm(shape, scale):
        return jax.random.normal(next(ks), shape, jnp.float32) * scale

    def gain(shape):
        return 1.0 + nrm(shape, 0.02)

    x = nrm((BATCH, SEQ, D), 1.0)
    c = nrm((BATCH, D), 1.0)
    offsets = jax.random.randint(next(ks), (BATCH, 1), 0, 1024, dtype=jnp.int32)
    positions = (offsets + jnp.arange(SEQ, dtype=jnp.int32)[None, :]).astype(jnp.int32)
    NL, NDF = N_NSA_LAYERS, N_DIFF_LAYERS
    return {
        'x': x, 'c': c, 'positions': positions,
        'ln_mix_g': gain((DEPTH_2, D)), 'ln_mlp_g': gain((DEPTH_2, D)),
        'w_ada': nrm((DEPTH_2, D, 6 * D), D ** -0.5), 'b_ada': nrm((DEPTH_2, 6 * D), 0.01),
        'w_mlp_in': nrm((DEPTH_2, D, D_FF), D ** -0.5), 'w_mlp_out': nrm((DEPTH_2, D_FF, D), D_FF ** -0.5),
        'nsa_w_in': nrm((NL, D, NSA_IN), D ** -0.5), 'nsa_b_gate': nrm((NL, 3 * NSA_HEADS), 0.01),
        'nsa_q_gain': gain((NL, HEAD_DIM)), 'nsa_k_gain': gain((NL, 3, HEAD_DIM)),
        'nsa_pe_k': nrm((NL, CMP_BLOCK, HEAD_DIM), 0.1),
        'nsa_w_ck1': nrm((NL, CMP_BLOCK * HEAD_DIM, CMP_HIDDEN), (CMP_BLOCK * HEAD_DIM) ** -0.5),
        'nsa_w_ck2': nrm((NL, CMP_HIDDEN, HEAD_DIM), CMP_HIDDEN ** -0.5),
        'nsa_pe_v': nrm((NL, CMP_BLOCK, HEAD_DIM), 0.1),
        'nsa_w_cv1': nrm((NL, CMP_BLOCK * HEAD_DIM, CMP_HIDDEN), (CMP_BLOCK * HEAD_DIM) ** -0.5),
        'nsa_w_cv2': nrm((NL, CMP_HIDDEN, HEAD_DIM), CMP_HIDDEN ** -0.5),
        'nsa_w_out': nrm((NL, NSA_Q_W, D), NSA_Q_W ** -0.5),
        'diff_w_in': nrm((NDF, D, DIFF_IN), D ** -0.5),
        'diff_q_gain': gain((NDF, HEAD_DIM)), 'diff_k_gain': gain((NDF, HEAD_DIM)),
        'diff_lq1': nrm((NDF, HEAD_DIM), 0.1), 'diff_lk1': nrm((NDF, HEAD_DIM), 0.1),
        'diff_lq2': nrm((NDF, HEAD_DIM), 0.1), 'diff_lk2': nrm((NDF, HEAD_DIM), 0.1),
        'diff_subln_g': gain((NDF, DIFF_V_DIM)),
        'diff_w_out': nrm((NDF, DIFF_W, D), DIFF_W ** -0.5),
    }

def second_block(x, c, positions, ln_mix_g, ln_mlp_g, w_ada, b_ada, w_mlp_in, w_mlp_out,
              nsa_w_in, nsa_b_gate, nsa_q_gain, nsa_k_gain, nsa_pe_k, nsa_w_ck1, nsa_w_ck2,
              nsa_pe_v, nsa_w_cv1, nsa_w_cv2, nsa_w_out,
              diff_w_in, diff_q_gain, diff_k_gain, diff_lq1, diff_lk1, diff_lq2, diff_lk2,
              diff_subln_g, diff_w_out):
    cos, sin = rope_tables(positions)
    cond = jax.nn.silu(c)
    for i in range(DEPTH_2):
        mod = cond @ w_ada[i] + b_ada[i]
        sh1, sc1, g1, sh2, sc2, g2 = jnp.split(mod, 6, axis=-1)
        h = rms_norm_2(x, ln_mix_g[i]) * (1.0 + sc1[:, None, :]) + sh1[:, None, :]
        j = i // N_MIXERS
        if i % N_MIXERS == 0:
            y = nsa_mixer(h, cos, sin, nsa_w_in[j], nsa_b_gate[j], nsa_q_gain[j], nsa_k_gain[j],
                          nsa_pe_k[j], nsa_w_ck1[j], nsa_w_ck2[j], nsa_pe_v[j], nsa_w_cv1[j],
                          nsa_w_cv2[j], nsa_w_out[j])
        else:
            y = diff_mixer(h, cos, sin, i + 1, diff_w_in[j], diff_q_gain[j], diff_k_gain[j],
                           diff_lq1[j], diff_lk1[j], diff_lq2[j], diff_lk2[j], diff_subln_g[j],
                           diff_w_out[j])
        x = x + g1[:, None, :] * y
        h = rms_norm_2(x, ln_mlp_g[i]) * (1.0 + sc2[:, None, :]) + sh2[:, None, :]
        x = x + g2[:, None, :] * (jnp.square(jax.nn.relu(h @ w_mlp_in[i])) @ w_mlp_out[i])
    return x


def setup_inputs(seed=0):
    out = dict(first_inputs(seed))
    for name, value in second_inputs(seed + 1).items():
        if name != "x":
            out[name + "_2"] = value
    return out


def reference(
    x, c, positions, w_ada, b_ada, g_pre, g_post, w_in, g_q_lat, w_uq, g_kv_lat, w_ukv, w_o_mla,
    w_o_moba, b_merge, w_out, c_2, positions_2, ln_mix_g_2, ln_mlp_g_2, w_ada_2, b_ada_2,
    w_mlp_in_2, w_mlp_out_2, nsa_w_in_2, nsa_b_gate_2, nsa_q_gain_2, nsa_k_gain_2, nsa_pe_k_2,
    nsa_w_ck1_2, nsa_w_ck2_2, nsa_pe_v_2, nsa_w_cv1_2, nsa_w_cv2_2, nsa_w_out_2, diff_w_in_2,
    diff_q_gain_2, diff_k_gain_2, diff_lq1_2, diff_lk1_2, diff_lq2_2, diff_lk2_2,
    diff_subln_g_2, diff_w_out_2,
):
    x = first_block(
        x, c, positions, w_ada, b_ada, g_pre, g_post, w_in, g_q_lat, w_uq, g_kv_lat, w_ukv,
        w_o_mla, w_o_moba, b_merge, w_out,
    )
    return second_block(
        x, c_2, positions_2, ln_mix_g_2, ln_mlp_g_2, w_ada_2, b_ada_2, w_mlp_in_2, w_mlp_out_2,
        nsa_w_in_2, nsa_b_gate_2, nsa_q_gain_2, nsa_k_gain_2, nsa_pe_k_2, nsa_w_ck1_2,
        nsa_w_ck2_2, nsa_pe_v_2, nsa_w_cv1_2, nsa_w_cv2_2, nsa_w_out_2, diff_w_in_2,
        diff_q_gain_2, diff_k_gain_2, diff_lq1_2, diff_lk1_2, diff_lq2_2, diff_lk2_2,
        diff_subln_g_2, diff_w_out_2,
    )


_drawn_inputs = setup_inputs


def setup_inputs(seed=0):
    import zlib

    import numpy as np

    out = dict(_drawn_inputs(seed))
    spreads = {}
    factors = {'b_ada': 4.206,
     'g_post': 3.764,
     'g_q_lat': 8.0,
     'g_kv_lat': 4.502,
     'b_merge': 8.0,
     'ln_mix_g_2': 8.0,
     'ln_mlp_g_2': 2.907,
     'b_ada_2': 2.736,
     'nsa_b_gate_2': 8.0,
     'nsa_q_gain_2': 8.0,
     'nsa_k_gain_2': 8.0,
     'nsa_pe_k_2': 8.0,
     'nsa_pe_v_2': 3.619,
     'diff_q_gain_2': 8.0,
     'diff_k_gain_2': 8.0,
     'diff_lk1_2': 3.637,
     'diff_lq2_2': 8.0,
     'diff_lk2_2': 8.0,
     'diff_subln_g_2': 173.413}
    for name, (base, spread) in spreads.items():
        noise = np.random.default_rng([zlib.crc32(name.encode()), seed]).standard_normal(out[name].shape)
        drawn = base * np.exp(spread * noise) if base else spread * noise
        out[name] = __import__('jax').numpy.asarray(drawn.astype(out[name].dtype))
    for name, factor in factors.items():
        out[name] = (out[name] * factor).astype(out[name].dtype)
    return out
```

```python
from contextlib import ExitStack
import math
import numpy as np

import concourse.bass as bass
from concourse import mybir
from concourse.alu_op_type import AluOpType as ALU

ACT = mybir.ActivationFunctionType
AX = mybir.AxisListType
F32 = mybir.dt.float32
I32 = mybir.dt.int32

P = 128
S = 256
M = S // P
D = 1024
DT = D // P
EPS = 1e-6
NEG = -1e30
RING = 4
SLOT = 4096
ADA_RING = 2
LAM_INIT = 0.8 - 0.6 * math.exp(-0.3)
MLA_SCALE = (64 + 32) ** -0.5
HEAD_SCALE = 64 ** -0.5

DVE_JOBS = ("merge", "w_o_mla", "w_o_moba", "nsa_out", "diff_out", "mlp_out0", "mlp_out1")



class Plan:
    def __init__(self):
        self.chunks = []
        self.jobs = []
        self.job_at = {}
        self.works = {}
        self.n_works = 0
        self.n_units = 0
        self.work_free = []
        self.turned = {"act": 0, "dve": 0}
        self.turned_after = {}
        self.pt_of_unit = []
        self.copied = {"act": 0, "dve": 0}
        self.copied_after = {}
        self.job_free = []
        self.chunk_free = {}
        self.n_parts = 0

    def chunk(self, weight, k0, kt, c0, n):
        self.chunks.append((weight, k0, kt, c0, n))
        return len(self.chunks) - 1

    def job(self, stage, *key, **spec):
        self.job_at[(stage,) + key] = len(self.jobs)
        self.jobs.append(dict(spec, stage=stage, key=key))

    def work(self, stage, n, by="both"):
        self.works[stage] = self.n_works
        for i in range(n):
            w = self.n_works + i
            if by == "units":
                self.n_units += 1
                self.work_free.append(("probs_ready", self.n_units))
                continue
            who = ("act", "dve")[w % 2] if by == "both" else by
            self.turned[who] += 1
            self.work_free.append(("turned_" + who, self.turned[who]))
        self.n_works += n
        self.turned_after[stage] = dict(self.turned)


def rows_product(plan, stage, weight, kt, n_total, first=0, width=512, lhs="hT", lhs0=0):
    for c0 in range(first, n_total, width):
        n = min(width, n_total - c0)
        c = plan.chunk(weight, 0, kt, c0, n)
        for m in range(M):
            plan.job(stage, c0, m, lhs=lhs, lhs0=lhs0, parts=[(c, kt)], m=m, c0=c0, n=n, s0=0)


def make_plan():
    p = Plan()
    c = p.chunk("w_in", 0, DT, 0, 416)
    for m in range(M):
        p.job("lat", 0, m, lhs="hT", lhs0=0, parts=[(c, DT)], m=m, c0=0, n=416, s0=0)
    for i, name in enumerate(("q_mb", "k_mb", "v_mb")):
        c = p.chunk("w_in", 0, DT, 928 + 512 * i, 512)
        for m in range(M):
            p.job(name, 0, m, lhs="hT", lhs0=0, parts=[(c, DT)], m=m, c0=0, n=512, s0=0)
    c = p.chunk("w_uq", 0, 2, 0, 768)
    for n0, n in ((0, 512), (512, 256)):
        for m in range(M):
            p.job("uq", n0, m, lhs="latT", lhs0=0, parts=[(c, 2)], m=m, c0=n0, n=n, s0=n0)
    c = p.chunk("w_ukv", 0, 1, 0, 1024)
    for n0 in (0, 512):
        for m in range(M):
            p.job("ukv", n0, m, lhs="latT", lhs0=2, parts=[(c, 1)], m=m, c0=n0, n=512, s0=n0)
    for name, c0 in (("z_mla", 416), ("z_mb", 2464)):
        c = p.chunk("w_in", 0, DT, c0, 512)
        for m in range(M):
            p.job(name, 0, m, lhs="hT", lhs0=0, parts=[(c, DT)], m=m, c0=0, n=512, s0=0)
    for i in range(4):
        c = p.chunk("w_in", 0, DT, 2976 + 512 * i, 512)
        for m in range(M):
            p.job("merge", 512 * i, m, lhs="hT", lhs0=0, parts=[(c, DT)], m=m, c0=512 * i, n=512, s0=0)
    for name, lhs0 in (("w_o_mla", 0), ("w_o_moba", 4)):
        c = p.chunk(name, 0, 4, 0, 1024)
        for n0 in (0, 512):
            for m in range(M):
                p.job(name, n0, m, lhs="hT", lhs0=lhs0, parts=[(c, 4)], m=m, c0=n0, n=512, s0=n0)
    rows_product(p, "w_out", "w_out", DT, D)
    for layer, (w_first, n_first, w_mix_out) in enumerate((("nsa_in", 2608, "nsa_out"), ("diff_in", 3072, "diff_out"))):
        rows_product(p, w_first, w_first, DT, n_first)
        if layer == 0:
            p.cmp_chunk = [p.chunk(w, 0, 16, 0, 128) for w in ("ck1", "cv1")]
        rows_product(p, w_mix_out, w_mix_out, DT, D)
        for f in range(8):
            c = p.chunk("mlp_in%d" % layer, 0, DT, 512 * f, 512)
            for pair in range(2):
                p.job("mlp_in%d" % layer, f, pair, T=True, chunk=c, f=f, pair=pair)
        for n0 in (0, 512):
            parts = [(p.chunk("mlp_out%d" % layer, 8 * k, 8, n0, 512), 8) for k in range(4)]
            for m in range(M):
                p.job("mlp_out%d" % layer, n0, m, lhs="hidT", lhs0=0, parts=parts, m=m, c0=n0, n=512, s0=0)
    for stage, n, by in (
            ("cols", 1, "dve"), ("x0", 4, "both"), ("latT", 2, "both"), ("mbqT", 2, "both"), ("mbkT", 2, "both"),
            ("mb", 8, "units"), ("mlaT", 8, "both"), ("mla", 8, "units"), ("uT", 4, "both"), ("yT", 4, "both"),
            ("x1", 4, "both"), ("cmpin", 4, "dve"), ("hid", 2, "dve"), ("kv_cmp", 2, "dve"), ("kcT", 1, "dve"),
            ("qcT", 4, "both"), ("cmpS", 4, "dve"), ("cmpT", 2, "act"), ("cmpO", 4, "dve"), ("qrT", 4, "both"),
            ("kT", 4, "both"), ("sel", 16, "units"), ("win", 16, "units"), ("o1T", 4, "both"), ("x2", 4, "both"),
            ("x3", 4, "both"), ("dqT", 4, "both"), ("dkT", 4, "both"), ("diff", 16, "units"), ("o2T", 4, "both"),
            ("x4", 4, "both")):
        p.work(stage, n, by)
    p.unit0, p.pt0, u, t = {}, {}, 0, 0
    for name, n, nt in (("mb", 8, 8), ("mla", 8, 8), ("sel", 16, 16), ("win", 16, 16), ("diff", 16, 8)):
        p.unit0[name], p.pt0[name] = u, t
        p.pt_of_unit += [t + i * nt // n for i in range(n)]
        u, t = u + n, t + nt
    p.n_pt = t
    for job in p.jobs:
        who = job["by"] = "dve" if job["stage"] in DVE_JOBS else "act"
        p.copied[who] += 1
        p.job_free.append(("copied_" + who, p.copied[who]))
        p.copied_after[job["stage"]] = dict(p.copied)
    for j, job in enumerate(p.jobs):
        if job.get("T"):
            p.chunk_free[job["chunk"]] = ("job_done", j + 1)
        elif len(job["parts"]) == 1:
            p.chunk_free[job["parts"][0][0]] = ("job_done", j + 1)
        elif job["m"] == 1:
            for c, _ in job["parts"][:-1]:
                p.n_parts += 1
                p.chunk_free[c] = ("part_done", p.n_parts)
            p.chunk_free[job["parts"][-1][0]] = ("job_done", j + 1)
    for a in range(2):
        p.chunk_free[p.cmp_chunk[a]] = ("work_ready", p.works["hid"] + a + 1)
    p.pieces = [("w_ada", 0, 512 * i) for i in range(6)]
    for layer in range(2):
        p.pieces += [("w_ada_2", layer, 512 * i) for i in range(12)]
    first = p.job_at[("z_mla", 0, 0)]
    j1 = p.job_at[("w_o_mla", 0, 0)]
    p.piece_after = {}
    spots = list(range(0, first, 2)) + list(range(first, j1 + 8))
    for n in range(14):
        p.piece_after[4 + n] = spots[(n * len(spots)) // 14]
    a = p.job_at[("nsa_in", 0, 0)]
    b = p.job_at[("mlp_out0", 0, 0)]
    for n in range(12):
        p.piece_after[18 + n] = a + (n * (b - a)) // 12
    last_chunk = []
    top = -1
    for job in p.jobs:
        top = max([top] + ([job["chunk"]] if job.get("T") else [c for c, _ in job["parts"]]))
        last_chunk.append(top)
    p.loads = [("ada", n) for n in range(8)]
    after = {}
    for n in range(4, 30):
        at = 0 if n == 4 else last_chunk[p.piece_after[n - 1]] + 1 if n - 1 >= 4 else 0
        after.setdefault(min(at, len(p.chunks) - 1), []).append(n)
    for c in range(len(p.chunks)):
        p.loads.append(("w", c))
        for n in after.get(c, []):
            p.loads += [("ada", 2 * n), ("ada", 2 * n + 1)]
    p.piece_reduce = {}
    for n, j in p.piece_after.items():
        p.piece_reduce.setdefault(j + 3, []).append(n)
    return p


def build(nc, t_in, out):
    plan = make_plan()
    jobs, works = plan.jobs, plan.works
    with ExitStack() as ctx:
        def sb(name, shape, dt=F32):
            return ctx.enter_context(nc.sbuf_tensor(name, shape, dt))

        class Named(dict):
            def __missing__(self, name):
                self[name] = ctx.enter_context(nc.semaphore(name))
                return self[name]

        sem = Named()
        bank = [ctx.enter_context(nc.psum_tensor("bank%d" % i, [P, 512], F32)) for i in range(8)]

        ring = sb("ring", [P, RING, SLOT])
        ada_ring = sb("ada_ring", [P, ADA_RING, 4, 512])
        acc = sb("ada_acc", [P, 2, 512])
        x = sb("x_rows", [P, M, D])
        hT = sb("hT", [P, DT, S])
        act = sb("act", [P, 9312])
        qk = sb("qkT", [P, 24, S])
        scrA = sb("scratch_a", [P, M, D])
        scrB = sb("scratch_b", [P, 2 * D])
        gate = sb("gates", [P, 3, D])
        probs = sb("probs", [P, 4, 384])
        probsT = sb("probsT", [P, 2, 384])
        ident = sb("ident", [P, P])
        ones = sb("ones", [P, P])
        causal = sb("causal", [P, P])
        cmp_neg = sb("cmp_neg", [P, M, 15])
        cmp_keep = sb("cmp_keep", [P, M, 15])
        own = sb("own_head", [120, 8])
        vec_rows = act[0:107, 0:128]
        vec_rows2 = act[0:64, 128:256]
        cols = sb("cols", [P, 192])
        silu_c = sb("silu_c", [P, 16])
        mod = sb("mod_cols", [P, 5, 2, 8])
        gs = sb("gain_scale", [P, 5, 8])
        tiny = sb("tiny", [P, 880])
        pos_i = sb("pos_i", [P, 2, M], I32)
        pos_f = sb("pos_f", [P, 2, M])
        cs = sb("cos_sin", [P, M, 2, 56])
        trig = scrA[:, 0, 0:224].rearrange("p (m a n) -> p m a n", m=M, a=2)
        neg_max = sb("neg_max", [P, 16])
        sums = sb("prob_sums", [P, 16])
        inv = sums
        ss = sb("sum_squares", [P, 160])
        rstd = ss
        half_neg = sb("minus_half", [P, 64])
        stat = sb("stat", [P, 128])

        q_gain, k_gain = tiny[:, 0:64], tiny[:, 64:256].rearrange("p (a d) -> p a d", d=64)
        dq_gain, dk_gain, sub_gain = tiny[:, 256:320], tiny[:, 320:384], tiny[:, 384:512]
        b_gate, lqk = tiny[:, 512:560], tiny[:, 560:816].rearrange("p (a d) -> p a d", d=64)
        inv_freq = tiny[:, 816:872]
        lam_tmp = scrA[:, 0, 256:384].rearrange("p (a d) -> p a d", d=64)
        lam = tiny[:, 872:880]

        C_C, C_PRE, C_BADA, C_MIX, C_MLP, C_GQ, C_GKV, C_PEK, C_PEV, C_BADA2 = 0, 16, 24, 40, 56, 72, 74, 75, 91, 128

        lat = act[:, 0:832].rearrange("p (m n) -> p m n", m=M)
        v_mla = scrA[:, 0, :].rearrange("p (m h d) -> p m h d", m=M, h=8)
        z = {"z_mla": act[:, 832:1856].rearrange("p (m n) -> p m n", m=M),
             "z_mb": act[:, 1856:2880].rearrange("p (m n) -> p m n", m=M)}
        merge = act[:, 2880:6976].rearrange("p (m n) -> p m n", m=M)
        qk_mb = act[:, 6976:9024].rearrange("p (a m n) -> p a m n", a=2, m=M)
        y_rows = act[:, 6976:9024].rearrange("p (m n) -> p m n", m=M)
        v_mb = scrA[:, 1, :].rearrange("p (m h d) -> p m h d", m=M, h=8)
        qT_mb, kT_mb = qk[:, 0:4, :], qk[:, 4:8, :]
        qT_mla, kT_mla = qk[:, 8:16, :], qk[:, 16:24, :]
        b_merge = scrB
        latT = qk[:, 21:24, :]
        q_up = act[:, 2880:4416].rearrange("p (m n) -> p m n", m=M)
        k_up = act[:, 4416:5952].rearrange("p (m n) -> p m n", m=M)
        rope_tmp = act[:, 832:2880].rearrange("p (a n) -> p a n", a=4)
        o_blk = act[:, 6976:9024].rearrange("p (a m n) -> p a m n", a=2, m=M)

        nsa = act[:, 0:5216].rearrange("p (m n) -> p m n", m=M)
        q_rot = act[:, 5216:7264].rearrange("p (m n) -> p m n", m=M)
        k_dup = act[:, 7264:9312].rearrange("p (m a g c d) -> p m a g c d", m=M, a=2, g=4, c=2)
        kv_dup = q_rot.rearrange("p m (a g c d) -> p m a g c d", a=2, g=4, c=2)
        qcT, qrT, kselT, kwinT = qk[:, 0:8, :], qk[:, 8:16, :], qk[:, 16:20, :], qk[:, 20:24, :]
        z_blk = scrB[:, :].rearrange("p (w h g i t) -> p w h g i t", w=2, h=2, g=4, i=16)
        small = qk[:, 20:24, :].rearrange("p a s -> p (a s)")
        hid = small[:, 0:120].rearrange("p (a n) -> p a n", a=2)
        hid_rep = small[:, 128:368].rearrange("p (f g r c) -> p f g r c", f=2, g=2, r=4)
        k_cmp = small[:, 384:448]
        k_cmp2 = small[:, 448:576].rearrange("p (a d) -> p a d", a=2)
        kcT = small[:, 576:636]
        w_c2 = sb("w_c2", [P, 2, 64])
        blockV = scrB[:, 0:1024].rearrange("p (f h d) -> p f h d", f=2, h=8)
        pcT = scrB[:, 1024:1536].rearrange("p (m f q) -> p m f q", m=M, f=2)
        pc = scrB[:, 1536:2016].rearrange("p (m n) -> p m n", m=M)
        o_rows = scrA
        k_dup_tmp = scrA[:, 0, :].rearrange("p (a n) -> p a n", a=4)
        o_tmp = scrB[:, 0:256].rearrange("p (a m d) -> p a m d", a=2, m=M)

        dif = act[:, 0:6144].rearrange("p (m n) -> p m n", m=M)
        dqT, dkT = qk[:, 0:8, :], qk[:, 8:16, :]
        hidT = act[:, 0:8192].rearrange("p (f s) -> p f s", f=32)

        operand = {"hT": hT, "latT": latT, "hidT": hidT}

        def slot(c):
            w, k0, kt, c0, n = plan.chunks[c]
            return ring[:, c % RING, 0:kt * n].rearrange("p (k n) -> p k n", k=kt)

        weights = {k: t_in[k][0].rearrange("(t p) n -> p t n", p=P) for k in
                   ("w_in", "w_uq", "w_ukv", "w_o_mla", "w_o_moba", "w_out", "w_ada")}
        for name, src, i in (("nsa_in", "nsa_w_in_2", 0), ("nsa_out", "nsa_w_out_2", 0), ("diff_in", "diff_w_in_2", 0),
                             ("diff_out", "diff_w_out_2", 0), ("ck1", "nsa_w_ck1_2", 0), ("cv1", "nsa_w_cv1_2", 0),
                             ("mlp_in0", "w_mlp_in_2", 0), ("mlp_in1", "w_mlp_in_2", 1),
                             ("mlp_out0", "w_mlp_out_2", 0), ("mlp_out1", "w_mlp_out_2", 1)):
            weights[name] = t_in[src][i].rearrange("(t p) n -> p t n", p=P)
        ada2 = [t_in["w_ada_2"][i].rearrange("(t p) n -> p t n", p=P) for i in range(2)]

        def piece_source(n):
            w, layer, c0 = plan.pieces[n]
            return (weights["w_ada"] if w == "w_ada" else ada2[layer]), c0

        def piece_use(n):
            if n < 6:
                part, half = n // 2, n % 2
                return ("gate", 0, 512 * half) if part == 2 else ("col", 0, part, 4 * half, C_BADA + 4 * n)
            layer, q = (n - 6) // 12, (n - 6) % 12
            part, half = q // 2, q % 2
            if part in (2, 5):
                return "gate", (1 + 2 * layer + part // 5) % 3, 512 * half
            norm = 1 + 2 * layer + part // 3
            return "col", norm, part % 3, 4 * half, C_BADA2 + 32 * layer + 16 * (part // 3) + 4 * (q % 6)

        class Chain:
            def __init__(self, eng, name):
                self.eng, self.sem, self.n = eng, sem[name], 0

            def __call__(self, ins):
                self.n += 1
                ins.then_inc(self.sem, 1)
                self.eng.wait_ge(self.sem, self.n)

        def head_rows(ap, d):
            return ap.rearrange("p m (h d) -> p m h d", d=d)

        def spread(ap, shape):
            return ap.to_broadcast(shape)

        def turned(eng, stage):
            for who in ("act", "dve"):
                eng.wait_ge(sem["turned_" + who], plan.turned_after[stage][who])

        def copied(eng, stage):
            for who in ("act", "dve"):
                if plan.copied_after[stage][who]:
                    eng.wait_ge(sem["copied_" + who], plan.copied_after[stage][who])

        NORM_X = ["x0", "x1", "x2", "x3", "x4"]
        block = ctx.enter_context(nc.Block())

        @block.sync
        def _(sp):
            for kind, n in plan.loads:
                if kind == "w":
                    w, k0, kt, c0, cn = plan.chunks[n]
                    if n >= RING:
                        name, value = plan.chunk_free[n - RING]
                        sp.wait_ge(sem[name], value)
                    sp.dma_start(slot(n), weights[w][:, k0:k0 + kt, c0:c0 + cn]).then_inc(
                        sem["chunk_in%d" % (n % RING)], 16)
                else:
                    src, c0 = piece_source(n // 2)
                    if n >= ADA_RING:
                        sp.wait_ge(sem[("ada_used0", "acc_ready")[n % 2]], n // 2)
                    k = 4 * (n % 2)
                    sp.dma_start(ada_ring[:, n % 2], src[:, k:k + 4, c0:c0 + 512]).then_inc(
                        sem["ada_in%d" % (n % 2)], 16)
            for m in range(M):
                sp.wait_ge(sem["x_done4"], m + 1)
                sp.dma_start(out[0, m * P:(m + 1) * P, :], x[:, m, :]).then_inc(sem["stored"], 16)
            sp.wait_ge(sem["stored"], 16 * M)

        @block.tensor
        def _(pe):
            used = set()

            def arrived(c):
                if c not in used:
                    used.add(c)
                    pe.wait_ge(sem["chunk_in%d" % (c % RING)], 16 * (c // RING + 1))

            def reduce_piece(n):
                pe.wait_ge(sem["acc_ready"], n + 1)
                if n >= 1:
                    pe.wait_ge(sem["mod_taken"], n)
                use = piece_use(n)
                if use[0] == "gate":
                    mm = pe.matmul(bank[3][:, :], ones[:, :], acc[:, n % 2, :], start=True, stop=True)
                else:
                    for i in range(4):
                        mm = pe.matmul(bank[3][:, i:i + 1], acc[:, n % 2, i * P:(i + 1) * P], ones[:, 0:1],
                                       start=True, stop=True)
                mm.then_inc(sem["piece_summed"], 1)

            def bank_for(j):
                if j >= 3:
                    name, value = plan.job_free[j - 3]
                    pe.wait_ge(sem[name], value)
                return bank[j % 3]

            def run_job(j):
                job = jobs[j]
                if job.get("T"):
                    c = job["chunk"]
                    arrived(c)
                    b = bank_for(j)
                    w = slot(c)
                    for i in range(2):
                        f0 = (2 * job["pair"] + i) * P
                        for k in range(DT):
                            mm = pe.matmul(b[:, i * S:(i + 1) * S], w[:, k, f0:f0 + P], hT[:, k, :],
                                           start=k == 0, stop=k == DT - 1)
                    mm.then_inc(sem["job_done"], 1)
                else:
                    act_T = operand[job["lhs"]]
                    b = bank_for(j)
                    m, n = job["m"], job["n"]
                    for i, (c, kt) in enumerate(job["parts"]):
                        arrived(c)
                        w = slot(c)
                        for k in range(kt):
                            a = job["lhs0"] + 8 * i + k
                            mm = pe.matmul(b[:, 0:n], act_T[:, a, m * P:(m + 1) * P],
                                           w[:, k, job["s0"]:job["s0"] + n],
                                           start=i == 0 and k == 0, stop=i == len(job["parts"]) - 1 and k == kt - 1)
                    mm.then_inc(sem["job_done"], 1)
                for n in plan.piece_reduce.get(j, []):
                    reduce_piece(n)

            def run_jobs(stage):
                for j, job in enumerate(jobs):
                    if job["stage"] == stage:
                        run_job(j)

            def run_accumulated(stage):
                js = [j for j, job in enumerate(jobs) if job["stage"] == stage]
                for j0 in js[::2]:
                    banks = [bank_for(j0), bank_for(j0 + 1)]
                    parts = jobs[j0]["parts"]
                    for i, (c, kt) in enumerate(parts):
                        arrived(c)
                        w = slot(c)
                        for m in range(M):
                            for k in range(kt):
                                mm = pe.matmul(banks[m][:, :], hidT[:, 8 * i + k, m * P:(m + 1) * P], w[:, k, :],
                                               start=i == 0 and k == 0, stop=i == 3 and k == 7)
                            if i == 3:
                                mm.then_inc(sem["job_done"], 1)
                        if i < 3:
                            mm.then_inc(sem["part_done"], 1)
                    for j in (j0, j0 + 1):
                        for n in plan.piece_reduce.get(j, []):
                            reduce_piece(n)

            def work_bank(w):
                if w >= 2:
                    name, value = plan.work_free[w - 2]
                    pe.wait_ge(sem[name], value)
                return bank[4 + w % 2]

            def turn(stage, src, n_tiles, ready=None, per=2, rows=P):
                for i in range(0, n_tiles, per):
                    w = works[stage] + i // per
                    b = work_bank(w)
                    for k in range(i, min(i + per, n_tiles)):
                        for m in range(M):
                            if ready is not None and m + (i > 0) * M < M and k == i:
                                pe.wait_ge(sem[ready], m + 1)
                            s = src(k, m)
                            o = (k - i) * S + m * P
                            mm = pe.transpose(b[0:s.shape[-1], o:o + P], s, ident[:, :])
                    mm.then_inc(sem["work_ready"], 1)

            def scores(name, i, q, kk):
                w = works[name] + i
                b = work_bank(w)
                pe.matmul(b[:, 0:P], q[:, 0:P], kk[:, 0:P], start=True, stop=True)
                pe.matmul(b[:, P:384], q[:, P:S], kk[:, 0:S], start=True, stop=True).then_inc(sem["work_ready"], 1)

            def turn_probs(name, i, u):
                t = plan.pt0[name] + i
                if t >= 1:
                    pe.wait_ge(sem["pt_taken"], t)
                if name == "diff":
                    pe.wait_ge(sem["diff_mixed"], i + 1)
                else:
                    pe.wait_ge(sem["probs_ready"], u + 1)
                for a in range(3):
                    mm = pe.transpose(bank[6][:, a * P:(a + 1) * P], probs[:, u % 4, a * P:(a + 1) * P], ident[:, :])
                mm.then_inc(sem["pt_ready"], 1)

            def values(name, i, v, d):
                t = plan.pt0[name] + i
                pe.wait_ge(sem["pt_taken"], t + 1)
                if t >= 1:
                    pe.wait_ge(sem["o_taken"], t)
                r = (t % 2) * 256
                pT = probsT[:, t % 2, :]
                pe.matmul(bank[7][:, r:r + d], pT[:, 0:P], v(0), start=True, stop=True)
                pe.matmul(bank[7][:, r + d:r + 2 * d], pT[:, P:2 * P], v(0), start=True, stop=False)
                pe.matmul(bank[7][:, r + d:r + 2 * d], pT[:, 2 * P:384], v(1), start=False, stop=True)\
                    .then_inc(sem["o_ready"], 1)

            def attention(name, heads, q, kk, v, d=64, beside=(), comps=1):
                beside = list(beside)
                u0 = plan.unit0[name]
                for i in range(heads + 2):
                    if i < heads:
                        for c in range(comps):
                            scores(name, comps * i + c, q(i, c), kk(i, c))
                    if beside:
                        run_job(beside.pop(0))
                    if 1 <= i <= heads:
                        turn_probs(name, i - 1, u0 + comps * (i - 1))
                    if i >= 2:
                        values(name, i - 2, v(i - 2), d)

            pe.wait_ge(sem["const_ready"], 1)
            pe.wait_ge(sem["rows_in"], 16 * 14)
            pe.transpose(bank[4][:, 0:107], vec_rows[:, :], ident[0:107, 0:107])
            pe.transpose(bank[4][:, 128:192], vec_rows2[:, :], ident[0:64, 0:64]).then_inc(sem["work_ready"], 1)
            for n in range(4):
                reduce_piece(n)

            def norm_turn(i):
                turn(NORM_X[i], lambda k, m: scrA[:, m, k * P:(k + 1) * P], DT, ready="xs_ready%d" % i)

            norm_turn(0)
            turned(pe, "x0")
            run_jobs("lat")
            run_jobs("q_mb")
            run_jobs("k_mb")
            run_jobs("v_mb")
            pe.wait_ge(sem["lat_normed"], 1)
            turn("latT", lambda k, m: lat[:, m, k * P:(k + 1) * P], 3)
            turned(pe, "latT")
            run_jobs("uq")
            run_jobs("ukv")
            for a, name in enumerate(("mbqT", "mbkT")):
                pe.wait_ge(sem["mb_roped"], a + 1)
                turn(name, lambda k, m: qk_mb[:, a, m, k * P:(k + 1) * P], 4)
            turned(pe, "mbkT")

            def half(buf, h):
                lo = 64 * (h % 2)
                return buf[lo:lo + 64, h // 2, :]

            bg = [j for j, job in enumerate(jobs) if job["stage"] in ("z_mla", "z_mb", "merge")]
            attention("mb", 8, lambda h, c: half(qT_mb, h), lambda h, c: half(kT_mb, h),
                      lambda h: (lambda a: v_mb[:, a, h, :]), beside=bg[:4])
            pe.wait_ge(sem["mla_roped"], 1)
            turn("mlaT", lambda k, m: (q_up, k_up)[k // 8][:, m, 96 * (k % 8):96 * (k % 8) + 96], 16)
            turned(pe, "mlaT")
            attention("mla", 8, lambda h, c: qT_mla[0:96, h, :], lambda h, c: kT_mla[0:96, h, :],
                      lambda h: (lambda a: v_mla[:, a, h, :]), beside=bg[4:])
            for a in range(2):
                pe.wait_ge(sem["u_ready"], a + 1)
                for i in range(2):
                    w = works["uT"] + 2 * a + i
                    b = work_bank(w)
                    for k in range(2):
                        for m in range(M):
                            mm = pe.transpose(b[:, k * S + m * P:k * S + (m + 1) * P],
                                              o_blk[:, a, m, (2 * i + k) * P:(2 * i + k + 1) * P], ident[:, :])
                    mm.then_inc(sem["work_ready"], 1)
            turned(pe, "uT")
            run_jobs("w_o_mla")
            run_jobs("w_o_moba")
            pe.wait_ge(sem["y_ready"], 4)
            turn("yT", lambda k, m: y_rows[:, m, k * P:(k + 1) * P], DT)
            turned(pe, "yT")
            run_jobs("w_out")

            norm_turn(1)
            turned(pe, "x1")
            run_jobs("nsa_in")
            for a in range(2):
                pe.wait_ge(sem["kv_doubled"], 1)
                for i in range(2):
                    w = works["cmpin"] + 2 * a + i
                    b = work_bank(w)
                    for g in range(2):
                        for m in range(M):
                            mm = pe.transpose(b[:, g * S + m * P:g * S + (m + 1) * P],
                                              kv_dup[:, m, a, 2 * i + g].rearrange("p c d -> p (c d)"), ident[:, :])
                    mm.then_inc(sem["work_ready"], 1)
            for a in range(2):
                pe.wait_ge(sem["turned_dve"], plan.work_free[works["cmpin"] + 2 * a + 1][1])
                arrived(plan.cmp_chunk[a])
                w1 = slot(plan.cmp_chunk[a])
                w = works["hid"] + a
                b = work_bank(w)
                for t in range(16):
                    h, i0 = t // 8, t // 8
                    mm = pe.matmul(b[:, 0:60], w1[:, t, :], z_blk[:, a, h, :, i0:i0 + 15, t % 8],
                                   start=t == 0, stop=t == 15)
                mm.then_inc(sem["work_ready"], 1)
            pe.wait_ge(sem["turned_dve"], plan.work_free[works["hid"]][1])
            pe.wait_ge(sem["w_c2_in"], 32)
            b = work_bank(works["kv_cmp"])
            pe.matmul(b[0:60, 0:64], hid[:, 0, :], w_c2[:, 0, :], start=True, stop=True).then_inc(sem["work_ready"], 1)
            pe.wait_ge(sem["hid_ready"], 1)
            b = work_bank(works["kv_cmp"] + 1)
            for f in range(2):
                mm = pe.matmul(b[0:120, f * 64:(f + 1) * 64], hid_rep[:, f].rearrange("p g r c -> p (g r c)"),
                               w_c2[:, 1, :], start=True, stop=True)
            mm.then_inc(sem["work_ready"], 1)
            pe.wait_ge(sem["k_cmp_ready"], 1)
            b = work_bank(works["kcT"])
            pe.transpose(b[:, 0:60], k_cmp2[0:60].rearrange("p a d -> p (a d)"), ident[0:60, 0:60])\
                .then_inc(sem["work_ready"], 1)
            pe.wait_ge(sem["q_normed"], 1)
            turn("qcT", lambda k, m: nsa[:, m, k * P:(k + 1) * P], 8)
            turned(pe, "kcT")
            turned(pe, "qcT")
            for m in range(M):
                for odd in range(2):
                    b = work_bank(works["cmpS"] + 2 * m + odd)
                    lo = 64 * odd
                    for h in range(8):
                        mm = pe.matmul(b[:, 15 * h:15 * h + 15], qcT[lo:lo + 64, h, m * P:(m + 1) * P],
                                       kcT[lo:lo + 64, 15 * (h // 2):15 * (h // 2) + 15], start=True, stop=True)
                    mm.then_inc(sem["work_ready"], 1)
            for m in range(M):
                pe.wait_ge(sem["pc_ready"], m + 1)
                b = work_bank(works["cmpT"] + m)
                for f in range(2):
                    mm = pe.transpose(b[0:120, f * P:(f + 1) * P], pc[:, m, 120 * f:120 * (f + 1)], ident[:, :])
                mm.then_inc(sem["work_ready"], 1)
            for m in range(M):
                pe.wait_ge(sem["turned_act"], plan.work_free[works["cmpT"] + m][1])
                pe.wait_ge(sem["turned_dve"], plan.work_free[works["kv_cmp"] + 1][1])
                for f in range(2):
                    b = work_bank(works["cmpO"] + 2 * m + f)
                    pe.matmul(b[:, :], pcT[0:120, m, f, :], blockV[0:120, f].rearrange("p h d -> p (h d)"),
                              start=True, stop=True).then_inc(sem["work_ready"], 1)
            pe.wait_ge(sem["q_roped"], 1)
            turn("qrT", lambda k, m: q_rot[:, m, k * P:(k + 1) * P], 8)
            pe.wait_ge(sem["k_doubled"], 1)
            turn("kT", lambda k, m: k_dup[:, m, k // 4, k % 4].rearrange("p c d -> p (c d)"), 8)
            turned(pe, "kT")
            for name, kT, v0 in (("sel", kselT, 1792), ("win", kwinT, 2304)):
                attention(name, 16, lambda h, c: half(qrT, h),
                          lambda h, c: kT[64 * (h % 2):64 * (h % 2) + 64, h // 4, :],
                          lambda h: (lambda a: nsa[:, a, v0 + 64 * (h // 4):v0 + 64 * (h // 4) + 64]))
            pe.wait_ge(sem["o_rows_done"], 1)
            turn("o1T", lambda k, m: scrA[:, m, k * P:(k + 1) * P], DT)
            turned(pe, "o1T")
            run_jobs("nsa_out")

            def mlp(layer, norm):
                norm_turn(norm)
                turned(pe, NORM_X[norm])
                run_jobs("mlp_in%d" % layer)
                pe.wait_ge(sem["hidden"], 16 * (layer + 1))
                run_accumulated("mlp_out%d" % layer)

            mlp(0, 2)
            norm_turn(3)
            turned(pe, "x3")
            run_jobs("diff_in")
            for a, name in enumerate(("dqT", "dkT")):
                pe.wait_ge(sem["dqk_roped"], a + 1)
                turn(name, lambda k, m: dif[:, m, a * D + k * P:a * D + (k + 1) * P], 8)
            turned(pe, "dkT")
            attention("diff", 8, lambda h, c: dqT[64 * c:64 * c + 64, h, :], lambda h, c: dkT[64 * c:64 * c + 64, h, :],
                      lambda h: (lambda a: dif[:, a, 2048 + h * P:2048 + (h + 1) * P]), d=P, comps=2)
            pe.wait_ge(sem["d_rows_done"], 2)
            turn("o2T", lambda k, m: scrA[:, m, k * P:(k + 1) * P], DT)
            turned(pe, "o2T")
            run_jobs("diff_out")
            mlp(1, 4)

        SS = {"x0": 0, "lat": 2, "y": 6, "x1": 8, "nsa": 10, "kc": 58, "x2": 59, "x3": 61, "diff": 63,
              "sub": 127, "x4": 143}

        def beside_jobs(name):
            bg = [j for j, job in enumerate(jobs) if job["stage"] in ("z_mla", "z_mb", "merge")]
            return {"mb": bg[:4], "mla": bg[4:]}.get(name, [])

        @block.scalar
        def _(act_e):
            e = act_e
            def rows_of(name, i=None):
                a = t_in[name]
                a = a[0] if i is None else a[i]
                return a
            r = 0
            for src in (t_in["c"][0], t_in["c_2"][0], t_in["g_pre"][0], t_in["b_ada"][0, 0:2048],
                        t_in["ln_mix_g_2"].rearrange("a n -> (a n)"), t_in["ln_mlp_g_2"].rearrange("a n -> (a n)"),
                        t_in["g_q_lat"][0], t_in["g_kv_lat"][0]):
                n = src.shape[0] // P
                e.dma_start(vec_rows[r:r + n, :], src.rearrange("(r n) -> r n", n=P)).then_inc(sem["rows_in"], 16)
                r += n
            for name in ("nsa_pe_k_2", "nsa_pe_v_2"):
                e.dma_start(vec_rows[r:r + 16, :], t_in[name][0].rearrange("(r a) d -> r (a d)", a=2))\
                    .then_inc(sem["rows_in"], 16)
                r += 16
            for layer in range(2):
                for half_ in range(2):
                    q = 32 * layer + 16 * half_
                    e.dma_start(vec_rows2[q:q + 16, :], t_in["b_ada_2"][layer, 3072 * half_:3072 * half_ + 2048]
                                .rearrange("(r n) -> r n", n=P)).then_inc(sem["rows_in"], 16)
            e.dma_start(x[:, :, :], t_in["x"][0].rearrange("(m p) n -> p m n", p=P)).then_inc(sem["x_in"], 16)
            for o, name in enumerate(("positions", "positions_2")):
                e.dma_start(pos_i[:, o, :], t_in[name][0].rearrange("(m p) -> p m", p=P), allow_slow_non_contiguous=True).then_inc(sem["tiny_in"], 16)
            for dst, src in ((q_gain, t_in["nsa_q_gain_2"][0]), (tiny[:, 64:256], t_in["nsa_k_gain_2"].rearrange("l a d -> (l a d)")),
                             (dq_gain, t_in["diff_q_gain_2"][0]), (dk_gain, t_in["diff_k_gain_2"][0]),
                             (sub_gain, t_in["diff_subln_g_2"][0]), (b_gate, t_in["nsa_b_gate_2"][0]),
                             (lqk[:, 0, :], t_in["diff_lq1_2"][0]), (lqk[:, 1, :], t_in["diff_lk1_2"][0]),
                             (lqk[:, 2, :], t_in["diff_lq2_2"][0]), (lqk[:, 3, :], t_in["diff_lk2_2"][0]),
                             (inv_freq, t_in["inv_freq"])):
                e.dma_start(dst, src.partition_broadcast(P)).then_inc(sem["tiny_in"], 16)
            e.dma_start(gate[:, 2, :], t_in["g_post"][0].partition_broadcast(P)).then_inc(sem["g_post_in"], 16)
            e.dma_start(gate[:, 0, :], t_in["b_ada"][0, 2048:3072].partition_broadcast(P)).then_inc(sem["gate_in0"], 16)
            e.dma_start(gate[:, 1, :], t_in["b_ada_2"][0, 2048:3072].partition_broadcast(P)).then_inc(sem["gate_in1"], 16)
            e.dma_start(b_merge[:, :], t_in["b_merge"][0].partition_broadcast(P)).then_inc(sem["b_merge_in"], 16)
            for a, name in enumerate(("nsa_w_ck2_2", "nsa_w_cv2_2")):
                e.dma_start(w_c2[:, a, :], t_in[name][0]).then_inc(sem["w_c2_in"], 16)

            e.wait_ge(sem["angles"], 1)
            e.activation(cs[:, :, :, :], trig[:, :, :, :], ACT.Sin).then_inc(sem["cos_sin"], 1)
            e.wait_ge(sem["lam_sums"], 1)
            e.activation(lam[:, 2:4], lam[:, 0:2], ACT.Exp).then_inc(sem["lam_exp"], 1)
            e.wait_ge(sem["turned_dve"], 1)
            e.activation(stat[:, 0:16], cols[:, 0:16], ACT.Sigmoid).then_inc(sem["sig_c"], 1)

            def turn_out(stage, i, put):
                w = works[stage] + i
                if w % 2 == 0:
                    e.wait_ge(sem["work_ready"], w + 1)
                    put(i, bank[4 + w % 2]).then_inc(sem["turned_act"], 1)

            def plain(dst, rows=P):
                def put(i, b):
                    return e.activation(dst[0:rows, 2 * i:2 * i + 2, :].rearrange("p a s -> p (a s)"),
                                        b[0:rows, :], ACT.Copy)
                return put

            def norm_stage(i, ready):
                for m in range(M):
                    e.wait_ge(sem[ready], (16 if ready == "x_in" else m + 1))
                    c = SS["x%d" % i] + m
                    e.activation(scrA[:, m, :], x[:, m, :], ACT.Square, accum_out=ss[:, c:c + 1])\
                        .then_inc(sem["ss_x%d" % i], 1)
                e.wait_ge(sem["gs_ready"], i + 1)

                def put(t, b):
                    for k in range(2):
                        f = 2 * t + k
                        ins = e.activation(hT[:, f, :], b[:, k * S:(k + 1) * S], ACT.Identity,
                                           scale=gs[:, i, f:f + 1], bias=mod[:, i, 0, f:f + 1])
                    return ins
                for t in range(4):
                    turn_out("x%d" % i, t, put)

            def take_job(j):
                job = jobs[j]
                if job["by"] != "act":
                    return
                e.wait_ge(sem["job_done"], j + 1)
                b, m, c0, stage = bank[j % 3], job.get("m"), job.get("c0"), job["stage"]
                n = job.get("n")
                if stage == "lat":
                    ins = e.activation(lat[:, m, :], b[:, 0:416], ACT.Copy)
                elif stage in ("q_mb", "k_mb"):
                    ins = e.activation(qk_mb[:, int(stage == "k_mb"), m, :], b[:, :], ACT.Copy,
                                       scale=HEAD_SCALE if stage == "q_mb" else 1.0)
                elif stage == "v_mb":
                    ins = e.activation(v_mb[:, m, :, :].rearrange("p h d -> p (h d)"), b[:, :], ACT.Copy)
                elif stage == "uq":
                    ins = e.activation(q_up[:, m, c0:c0 + n], b[:, 0:n], ACT.Copy, scale=MLA_SCALE)
                elif stage == "ukv":
                    h0 = c0 // P
                    src = b[:, :].rearrange("p (h d) -> p h d", d=P)
                    dst = k_up[:, m, :].rearrange("p (h d) -> p h d", d=96)
                    e.activation(dst[:, h0:h0 + 4, 0:64], src[:, :, 0:64], ACT.Copy)
                    ins = e.activation(v_mla[:, m, h0:h0 + 4, :], src[:, :, 64:128], ACT.Copy)
                elif stage in ("z_mla", "z_mb"):
                    ins = e.activation(z[stage][:, m, :], b[:, :], ACT.Copy)
                elif stage == "w_out":
                    ins = e.activation(scrA[:, m, c0:c0 + n], b[:, 0:n], ACT.Copy)
                elif stage == "nsa_in":
                    ins = e.activation(nsa[:, m, c0:c0 + n], b[:, 0:n], ACT.Copy)
                elif stage == "diff_in":
                    ins = e.activation(dif[:, m, c0:c0 + n], b[:, 0:n], ACT.Copy)
                else:
                    f = 4 * job["f"] + 2 * job["pair"]
                    ins = e.activation(hidT[:, f:f + 2, :].rearrange("p a s -> p (a s)"), b[:, :], ACT.Relu)
                ins.then_inc(sem["copied_act"], 1)

            def take_jobs(stage):
                for j, job in enumerate(jobs):
                    if job["stage"] == stage:
                        take_job(j)

            def exps(name, i):
                u, w = plan.unit0[name] + i, works[name] + i
                e.wait_ge(sem["neg_max"], u + 1)
                if u >= 4:
                    e.wait_ge(sem["pt_ready"], plan.pt_of_unit[u - 4] + 1)
                b = bank[4 + w % 2]
                e.activation(probs[:, u % 4, 0:P], b[:, 0:P], ACT.Exp, bias=neg_max[:, 2 * (u % 8):2 * (u % 8) + 1],
                             accum_out=sums[:, 2 * (u % 8):2 * (u % 8) + 1])
                e.activation(probs[:, u % 4, P:384], b[:, P:384], ACT.Exp, bias=neg_max[:, 2 * (u % 8) + 1:2 * (u % 8) + 2],
                             accum_out=sums[:, 2 * (u % 8) + 1:2 * (u % 8) + 2]).then_inc(sem["probs_ready"], 1)

            def attention(name, heads, comps=1):
                beside = beside_jobs(name)
                for i in range(heads + 2):
                    if i < heads:
                        for c in range(comps):
                            exps(name, comps * i + c)
                    if beside:
                        take_job(beside.pop(0))
                    if 1 <= i <= heads:
                        t = plan.pt0[name] + i - 1
                        e.wait_ge(sem["pt_ready"], t + 1)
                        if t >= 2:
                            e.wait_ge(sem["o_ready"], t - 1)
                        e.activation(probsT[:, t % 2, :], bank[6][:, 0:384], ACT.Copy).then_inc(sem["pt_taken"], 1)

            norm_stage(0, "x_in")
            take_jobs("lat")
            copied(e, "lat")
            for m in range(M):
                c = SS["lat"] + m
                e.activation(scrA[:, 0, 512 * m:512 * m + 256], lat[:, m, 0:256], ACT.Square, accum_out=ss[:, c:c + 1])\
                    .then_inc(sem["ss_lat"], 1)
                e.activation(scrA[:, 0, 512 * m + 256:512 * m + 384], lat[:, m, 256:384], ACT.Square, accum_out=ss[:, c + 2:c + 3])\
                    .then_inc(sem["ss_lat"], 1)
            for stage in ("q_mb", "k_mb", "v_mb"):
                take_jobs(stage)

            def put_latent(i, b):
                for k in range(2):
                    ins = e.activation(latT[:, k, :], b[:, k * S:(k + 1) * S], ACT.Copy,
                                       scale=cols[:, C_GQ + k:C_GQ + k + 1])
                return ins
            assert works["latT"] % 2 == 1
            turn_out("latT", 1, lambda i, b: e.activation(latT[:, 2, :], b[:, 0:S], ACT.Copy,
                                                          scale=cols[:, C_GKV:C_GKV + 1]))
            take_jobs("uq")
            take_jobs("ukv")
            for name, dst in (("mbqT", qT_mb), ("mbkT", kT_mb)):
                for i in range(2):
                    turn_out(name, i, plain(dst))
            attention("mb", 8)
            for i in range(8):
                turn_out("mlaT", i, plain(qk[:, 8:24, :], 96))
            attention("mla", 8)
            copied(e, "merge")
            e.wait_ge(sem["o_ready"], plan.pt0["sel"])
            e.activation(scrA[:, :, :].rearrange("p m n -> p (m n)"), act[:, 832:2880], ACT.Sigmoid)\
                .then_inc(sem["z_sig"], 1)
            e.activation(merge[:, :, :].rearrange("p m n -> p (m n)"), merge[:, :, :].rearrange("p m n -> p (m n)"),
                         ACT.Sigmoid).then_inc(sem["merge_sig"], 1)
            for i in range(4):
                turn_out("uT", i, plain(hT))
            for i in range(4):
                turn_out("yT", i, plain(hT))
            take_jobs("w_out")
            copied(e, "w_out")
            for m in range(M):
                c = SS["y"] + m
                e.activation(scrB[:, m * D:(m + 1) * D], scrA[:, m, :], ACT.Square, accum_out=ss[:, c:c + 1])\
                    .then_inc(sem["ss_y"], 1)

            norm_stage(1, "x_done0")
            take_jobs("nsa_in")
            copied(e, "nsa_in")
            for m in range(M):
                e.activation(scrA[:, m, :], nsa[:, m, 0:D], ACT.Square).then_inc(sem["nsa_sq"], 1)
                src = nsa[:, m, 1536:2560].rearrange("p (a n) -> p a n", a=2)[:, :, 0:256]
                e.activation(act[:, 7264 + 512 * m:7776 + 512 * m].rearrange("p (a n) -> p a n", a=2), src,
                             ACT.Square).then_inc(sem["nsa_sq"], 1)
            e.wait_ge(sem["gl_biased"], 2)
            e.activation(nsa[:, :, 2560:2608], nsa[:, :, 2560:2608], ACT.Sigmoid).then_inc(sem["gl_ready"], 1)
            for a in range(2):
                e.wait_ge(sem["work_ready"], works["hid"] + a + 1)
                if a:
                    e.wait_ge(sem["turned_dve"], plan.work_free[works["hid"]][1])
                e.activation(stat[:, 64:124], bank[4 + (works["hid"] + a) % 2][:, 0:60], ACT.Sigmoid)\
                    .then_inc(sem["hid_sig"], 1)
            for i in range(4):
                turn_out("qcT", i, plain(qcT))
            for m in range(M):
                e.wait_ge(sem["pc_shifted"], m + 1)
                e.activation(pc[:, m, :], pc[:, m, :], ACT.Exp).then_inc(sem["pc_exp"], 1)
            for m in range(M):
                w = works["cmpT"] + m
                e.wait_ge(sem["work_ready"], w + 1)
                e.activation(pcT[0:120, m].rearrange("p f q -> p (f q)"), bank[4 + w % 2][0:120, 0:256], ACT.Copy)\
                    .then_inc(sem["turned_act"], 1)
            for i in range(4):
                turn_out("qrT", i, plain(qrT))
            for i in range(4):
                turn_out("kT", i, plain(qk[:, 16:24, :]))
            attention("sel", 16)
            attention("win", 16)
            for i in range(4):
                turn_out("o1T", i, plain(hT))
            take_jobs("nsa_out")
            norm_stage(2, "x_done1")
            take_jobs("mlp_in0")
            norm_stage(3, "x_done2")
            take_jobs("diff_in")
            copied(e, "diff_in")
            for m in range(M):
                e.activation(scrA[:, m, :], dif[:, m, 0:D], ACT.Square).then_inc(sem["diff_sq"], 1)
                e.activation(scrB[:, m * D:(m + 1) * D], dif[:, m, D:2 * D], ACT.Square).then_inc(sem["diff_sq"], 1)
            for name, dst in (("dqT", dqT), ("dkT", dkT)):
                for i in range(4):
                    turn_out(name, i, plain(dst))
            attention("diff", 8, comps=2)
            e.wait_ge(sem["o_taken"], plan.n_pt)
            for m in range(M):
                e.activation(scrB[:, m * D:(m + 1) * D], scrA[:, m, :], ACT.Square).then_inc(sem["sub_sq"], 1)
            for i in range(4):
                turn_out("o2T", i, plain(hT))
            norm_stage(4, "x_done3")
            take_jobs("mlp_in1")

        @block.gpsimd
        def _(pool):
            e = pool
            chain = Chain(e, "pool_chain")
            chain(e.memset(ident[:, :], 0.0))
            chain(e.affine_select(out=ident[:, :], in_=ident[:, :], compare_op=ALU.not_equal, fill=1.0, base=0,
                                  pattern=[[-1, P]], channel_multiplier=1))
            e.memset(ones[:, :], 1.0).then_inc(sem["const_ready"], 1)
            chain(e.memset(half_neg[:, :], -0.5))
            chain(e.memset(causal[:, :], 0.0))
            chain(e.affine_select(out=causal[:, :], in_=causal[:, :], compare_op=ALU.is_ge, fill=NEG, base=0,
                                  pattern=[[-1, P]], channel_multiplier=1))
            for buf, inside, outside in ((cmp_neg, 0.0, NEG), (cmp_keep, 1.0, 0.0)):
                chain(e.memset(buf[:, :, :], inside))
                chain(e.affine_select(out=buf[:, :, :], in_=buf[:, :, :], compare_op=ALU.is_ge, fill=outside,
                                      base=-31, pattern=[[P, M], [-16, 15]], channel_multiplier=1))
            chain(e.memset(own[:, :], 1.0))
            chain(e.affine_select(out=own[:, :], in_=own[:, :], compare_op=ALU.is_ge, fill=0.0, base=0,
                                  pattern=[[-15, 8]], channel_multiplier=1))
            chain(e.affine_select(out=own[:, :], in_=own[:, :], compare_op=ALU.is_ge, fill=0.0, base=14,
                                  pattern=[[15, 8]], channel_multiplier=-1))
            e.memset(stat[:, 127:128], 0.0).then_inc(sem["masks_ready"], 1)

            def root(name, groups, count, p=P):
                e.wait_ge(sem["ss_" + name], count)
                for c, n, elements in groups:
                    chain(e.tensor_scalar(rstd[0:p, c:c + n], ss[0:p, c:c + n], 1.0 / elements, EPS, ALU.mult, ALU.add))
                for g, (c, n, _) in enumerate(groups):
                    e.tensor_tensor(rstd[0:p, c:c + n], rstd[0:p, c:c + n], half_neg[0:p, 0:n], ALU.pow)\
                        .then_inc(sem["rs_" + name], 1)

            root("x0", [(SS["x0"], 2, D)], 2)
            root("lat", [(SS["lat"], 2, 256), (SS["lat"] + 2, 2, 128)], 4)
            e.wait_ge(sem["gg_ready"], 1)
            e.dma_start(gate[:, 2, :], t_in["b_ada_2"][0, 5120:6144].partition_broadcast(P)).then_inc(sem["gate_in2"], 16)
            root("y", [(SS["y"], 2, D)], 2)
            e.wait_ge(sem["x_done0"], 2)
            e.dma_start(gate[:, 0, :], t_in["b_ada_2"][1, 2048:3072].partition_broadcast(P)).then_inc(sem["gate_in3"], 16)
            root("x1", [(SS["x1"], 2, D)], 2)
            root("nsa", [(SS["nsa"], 48, 64)], 4)
            root("kc", [(SS["kc"], 1, 64)], 1, 60)
            e.wait_ge(sem["x_done1"], 2)
            e.dma_start(gate[:, 1, :], t_in["b_ada_2"][1, 5120:6144].partition_broadcast(P)).then_inc(sem["gate_in4"], 16)

            def square_hidden(layer):
                for f in range(8):
                    for pair in range(2):
                        j = plan.job_at[("mlp_in%d" % layer, f, pair)]
                        e.wait_ge(sem["copied_act"], plan.job_free[j][1])
                        h = hidT[:, 4 * f + 2 * pair:4 * f + 2 * pair + 2, :].rearrange("p a s -> p (a s)")
                        e.tensor_tensor(h, h, h, ALU.mult).then_inc(sem["hidden"], 1)

            root("x2", [(SS["x2"], 2, D)], 2)
            square_hidden(0)
            root("x3", [(SS["x3"], 2, D)], 2)
            root("diff", [(SS["diff"], 64, 64)], 4)
            root("sub", [(SS["sub"], 16, P)], 2)
            root("x4", [(SS["x4"], 2, D)], 2)
            square_hidden(1)

        @block.vector
        def _(dve):
            e = dve
            chain = Chain(e, "dve_chain")
            flat = lambda ap: ap

            e.wait_ge(sem["tiny_in"], 16 * 13)
            chain(e.tensor_copy(pos_f[:, :, :], pos_i[:, :, :]))
            for m in range(M):
                for o, (a, b) in enumerate(((0, 48), (48, 56))):
                    for kind in range(2):
                        chain(e.tensor_scalar(trig[:, m, kind, a:b], inv_freq[:, a:b], pos_f[:, o, m:m + 1], None, ALU.mult))
            TURN = 2 * math.pi
            C1, C2 = 6.28125, 2029 / 2 ** 20
            C3 = TURN - C1 - C2
            MAGIC = 1.5 * 2 ** 23
            turns = cs
            for kind, quarter in ((0, 0.25), (1, 0.0)):
                chain(e.tensor_scalar(turns[:, :, kind, :], trig[:, :, kind, :], 1 / TURN, quarter, ALU.mult, ALU.add))
            chain(e.tensor_scalar(turns[:, :, :, :], turns[:, :, :, :], MAGIC, None, ALU.add))
            chain(e.tensor_scalar(turns[:, :, :, :], turns[:, :, :, :], -MAGIC, None, ALU.add))
            for c in (C1, C2, C3):
                chain(e.scalar_tensor_tensor(out=trig[:, :, :, :], in0=turns[:, :, :, :], scalar=-c,
                                             in1=trig[:, :, :, :], op0=ALU.mult, op1=ALU.add))
            chain(e.tensor_scalar(trig[:, :, 0, :], trig[:, :, 0, :], math.pi / 2, None, ALU.add))
            LIMIT = 3.1415925
            e.tensor_scalar(trig[:, :, :, :], trig[:, :, :, :], LIMIT, -LIMIT, ALU.min, ALU.max)\
                .then_inc(sem["angles"], 1)
            chain(e.tensor_tensor(lam_tmp[:, :, :], lqk[:, 0:4:2, :], lqk[:, 1:4:2, :], ALU.mult))
            e.tensor_reduce(lam[:, 0:2], lam_tmp[:, :, :], AX.X, ALU.add).then_inc(sem["lam_sums"], 1)
            chain(e.tensor_scalar(q_gain, q_gain, HEAD_SCALE, None, ALU.mult))
            chain(e.tensor_scalar(dq_gain, dq_gain, HEAD_SCALE, None, ALU.mult))
            chain(e.tensor_scalar(sub_gain, sub_gain, 1.0 - LAM_INIT, None, ALU.mult))
            e.wait_ge(sem["lam_exp"], 1)
            chain(e.tensor_tensor(lam[:, 4:5], lam[:, 2:3], lam[:, 3:4], ALU.subtract))
            chain(e.tensor_scalar(lam[:, 5:6], lam[:, 4:5], LAM_INIT, -1.0, ALU.add, ALU.mult))
            e.wait_ge(sem["work_ready"], 1)
            e.tensor_copy(cols[:, 0:107], bank[4][:, 0:107])
            e.tensor_copy(cols[:, 128:192], bank[4][:, 128:192]).then_inc(sem["turned_dve"], 1)
            e.wait_ge(sem["turned_dve"], 1)
            e.wait_ge(sem["sig_c"], 1)
            chain(e.tensor_tensor(silu_c[:, :], stat[:, 0:16], cols[:, 0:16], ALU.mult))

            def piece(n):
                c = 0 if n < 6 else 8
                for k in range(DT):
                    half_load = 2 * n + k // 4
                    if k % 4 == 0:
                        e.wait_ge(sem["ada_in%d" % (k // 4)], 16 * (n + 1))
                    w = ada_ring[:, k // 4, k % 4, :]
                    s = silu_c[:, c + k:c + k + 1]
                    if k == 0:
                        if n >= 2:
                            e.wait_ge(sem["piece_summed"], n - 1)
                        ins = e.tensor_scalar(acc[:, n % 2, :], w, s, None, ALU.mult)
                    else:
                        ins = e.scalar_tensor_tensor(out=acc[:, n % 2, :], in0=w, scalar=s, in1=acc[:, n % 2, :],
                                                     op0=ALU.mult, op1=ALU.add)
                    if k == 3:
                        ins.then_inc(sem["ada_used0"], 1)
                        e.wait_ge(sem["ada_used0"], n + 1)
                    elif k == 7:
                        ins.then_inc(sem["acc_ready"], 1)
                    else:
                        chain(ins)

            def piece_end(n):
                e.wait_ge(sem["piece_summed"], n + 1)
                use = piece_use(n)
                if use[0] == "col":
                    _, norm, part, c0, b0 = use
                    e.tensor_tensor(mod[:, norm, part, c0:c0 + 4], bank[3][:, 0:4], cols[:, b0:b0 + 4], ALU.add)\
                        .then_inc(sem["mod_taken"], 1)
                else:
                    g = 0 if n < 6 else 1 + (n - 6) // 12 * 2 + ((n - 6) % 12) // 6
                    e.wait_ge(sem["gate_in%d" % g], 16)
                    dst = gate[:, use[1], use[2]:use[2] + 512]
                    e.tensor_tensor(dst, bank[3][:, :], dst, ALU.add).then_inc(sem["mod_taken"], 1)
                if n == 5:
                    e.wait_ge(sem["mod_taken"], 6)
                    e.wait_ge(sem["g_post_in"], 16)
                    e.tensor_tensor(gate[:, 0, :], gate[:, 0, :], gate[:, 2, :], ALU.mult).then_inc(sem["gg_ready"], 1)

            def after_job(j):
                for n, at in plan.piece_after.items():
                    if at == j:
                        piece(n)
                for n in plan.piece_reduce.get(j, []):
                    piece_end(n)

            def turn_out(stage, i, put):
                w = works[stage] + i
                if w % 2 == 1:
                    e.wait_ge(sem["work_ready"], w + 1)
                    put(i, bank[5]).then_inc(sem["turned_dve"], 1)

            def plain(dst, rows=P):
                def put(i, b):
                    return e.tensor_copy(dst[0:rows, 2 * i:2 * i + 2, :].rearrange("p a s -> p (a s)"), b[0:rows, :])
                return put

            GAIN = [C_PRE, C_MIX, C_MLP, C_MIX + 8, C_MLP + 8]
            LAST_PIECE = [4, 10, 16, 22, 28]

            def norm_stage(i):
                e.wait_ge(sem["mod_taken"], LAST_PIECE[i])
                e.scalar_tensor_tensor(out=gs[:, i, :], in0=mod[:, i, 1, :], scalar=1.0,
                                       in1=cols[:, GAIN[i]:GAIN[i] + 8], op0=ALU.add, op1=ALU.mult)\
                    .then_inc(sem["gs_ready"], 1)
                e.wait_ge(sem["rs_x%d" % i], 1)
                for m in range(M):
                    c = SS["x%d" % i] + m
                    e.tensor_scalar(scrA[:, m, :], x[:, m, :], rstd[:, c:c + 1], None, ALU.mult)\
                        .then_inc(sem["xs_ready%d" % i], 1)
                e.wait_ge(sem["gs_ready"], i + 1)

                def put(t, b):
                    for k in range(2):
                        f = 2 * t + k
                        ins = e.tensor_scalar(hT[:, f, :], b[:, k * S:(k + 1) * S], gs[:, i, f:f + 1],
                                              mod[:, i, 0, f:f + 1], ALU.mult, ALU.add)
                    return ins
                for t in range(4):
                    turn_out("x%d" % i, t, put)

            def rope(x1, x2, c, s, o1, o2, tmp):
                e.tensor_tensor(tmp[0], x1, c, ALU.mult)
                e.tensor_tensor(tmp[1], x2, s, ALU.mult)
                e.tensor_tensor(tmp[2], x2, c, ALU.mult)
                chain(e.tensor_tensor(tmp[3], x1, s, ALU.mult))
                e.tensor_tensor(o1, tmp[0], tmp[1], ALU.subtract)
                return e.tensor_tensor(o2, tmp[2], tmp[3], ALU.add)

            def angles(kind, a, b, heads):
                return cs[:, :, kind, a:b].unsqueeze(2).to_broadcast([P, M, heads, b - a])

            def take_job(j):
                job = jobs[j]
                if job["by"] == "dve":
                    b, m, c0, stage = bank[j % 3], job["m"], job["c0"], job["stage"]
                    e.wait_ge(sem["job_done"], j + 1)
                    t = scrB[:, (j % 2) * 512:(j % 2) * 512 + 512]
                    if stage == "merge":
                        e.wait_ge(sem["b_merge_in"], 16)
                        e.tensor_tensor(merge[:, m, c0:c0 + 512], b[:, :], b_merge[:, c0:c0 + 512], ALU.add)\
                            .then_inc(sem["copied_dve"], 1)
                    elif stage == "w_o_mla":
                        e.wait_ge(sem["merge_sig"], 1)
                        e.tensor_tensor(y_rows[:, m, c0:c0 + 512], b[:, :], merge[:, m, c0:c0 + 512], ALU.mult)\
                            .then_inc(sem["copied_dve"], 1)
                    elif stage == "w_o_moba":
                        e.tensor_tensor(t, b[:, :], merge[:, m, D + c0:D + c0 + 512], ALU.mult)\
                            .then_inc(sem["copied_dve"], 1)
                        e.wait_ge(sem["copied_dve"], plan.job_free[j][1])
                        y = y_rows[:, m, c0:c0 + 512]
                        e.tensor_tensor(y, y, t, ALU.add).then_inc(sem["y_ready"], 1)
                    else:
                        k = {"nsa_out": 1, "mlp_out0": 2, "diff_out": 3, "mlp_out1": 4}[stage]
                        g = gate[:, k % 3, c0:c0 + 512]
                        e.tensor_tensor(t, b[:, :], g, ALU.mult).then_inc(sem["copied_dve"], 1)
                        e.wait_ge(sem["copied_dve"], plan.job_free[j][1])
                        r = x[:, m, c0:c0 + 512]
                        ins = e.tensor_tensor(r, r, t, ALU.add)
                        if c0 == 512:
                            ins.then_inc(sem["x_done%d" % k], 1)
                after_job(j)

            def take_jobs(stage):
                for j, job in enumerate(jobs):
                    if job["stage"] == stage:
                        take_job(j)

            def maxima(name, i):
                u, w = plan.unit0[name] + i, works[name] + i
                b = bank[4 + w % 2]
                e.wait_ge(sem["work_ready"], w + 1)
                for lo in (0, 256):
                    ins = e.tensor_tensor(b[:, lo:lo + P], b[:, lo:lo + P], causal[:, :], ALU.add)
                chain(ins)
                e.tensor_reduce(neg_max[:, 2 * (u % 8):2 * (u % 8) + 1], b[:, 0:P], AX.X, ALU.max, negate=True)
                e.tensor_reduce(neg_max[:, 2 * (u % 8) + 1:2 * (u % 8) + 2], b[:, P:384], AX.X, ALU.max, negate=True)\
                    .then_inc(sem["neg_max"], 1)

            def outputs(name, i):
                t = plan.pt0[name] + i
                u = plan.unit0[name] + i
                r = (t % 2) * 256
                if name == "diff":
                    e.wait_ge(sem["o_ready"], t + 1)
                    o = bank[7][:, r:r + 256].rearrange("p (m d) -> p m d", m=M)
                    e.tensor_copy(scrA[:, :, i * P:(i + 1) * P], o).then_inc(sem["o_taken"], 1)
                    return
                e.wait_ge(sem["probs_ready"], u + 1)
                chain(e.reciprocal(inv[:, 2 * (u % 8):2 * (u % 8) + 2], sums[:, 2 * (u % 8):2 * (u % 8) + 2]))
                if name in ("sel", "win"):
                    g = nsa[:, :, 2560 + 3 * i + (1 if name == "sel" else 2)]
                    chain(e.tensor_tensor(inv[:, 2 * (u % 8):2 * (u % 8) + 2], inv[:, 2 * (u % 8):2 * (u % 8) + 2], g, ALU.mult))
                e.wait_ge(sem["o_ready"], t + 1)
                o = bank[7][:, r:r + P].rearrange("p (m d) -> p m d", m=M)
                w = inv[:, 2 * (u % 8):2 * (u % 8) + 2].unsqueeze(2).to_broadcast([P, M, 64])
                if name in ("mb", "mla"):
                    dst = o_blk[:, int(name == "mb"), :, 64 * i:64 * i + 64]
                    e.tensor_tensor(dst, o, w, ALU.mult).then_inc(sem["o_taken"], 1)
                else:
                    tmp = o_tmp[:, t % 2, :, :]
                    e.tensor_tensor(tmp, o, w, ALU.mult).then_inc(sem["o_taken"], 1)
                    e.wait_ge(sem["o_taken"], t + 1)
                    dst = scrA[:, :, 64 * i:64 * i + 64]
                    chain(e.tensor_tensor(dst, dst, tmp, ALU.add))

            def mix(i):
                u = plan.unit0["diff"] + 2 * i
                e.wait_ge(sem["probs_ready"], u + 2)
                chain(e.reciprocal(inv[:, 2 * (u % 8):2 * (u % 8) + 4], sums[:, 2 * (u % 8):2 * (u % 8) + 4]))
                chain(e.tensor_scalar(inv[:, 2 * (u % 8) + 2:2 * (u % 8) + 4], inv[:, 2 * (u % 8) + 2:2 * (u % 8) + 4], lam[:, 5:6], None, ALU.mult))
                for m, (a, b) in enumerate(((0, P), (P, 384))):
                    p1 = probs[:, (u + 1) % 4, a:b]
                    ins = e.tensor_scalar(p1, p1, inv[:, 2 * (u % 8) + 2 + m:2 * (u % 8) + 3 + m], None, ALU.mult)
                chain(ins)
                for m, (a, b) in enumerate(((0, P), (P, 384))):
                    p0 = probs[:, u % 4, a:b]
                    ins = e.scalar_tensor_tensor(out=p0, in0=p0, scalar=inv[:, 2 * (u % 8) + m:2 * (u % 8) + m + 1],
                                                 in1=probs[:, (u + 1) % 4, a:b], op0=ALU.mult, op1=ALU.add)
                ins.then_inc(sem["diff_mixed"], 1)

            def attention(name, heads, comps=1):
                beside = beside_jobs(name)
                for i in range(heads + 2):
                    if i < heads:
                        for c in range(comps):
                            maxima(name, comps * i + c)
                        if comps == 2:
                            mix(i)
                    if beside:
                        take_job(beside.pop(0))
                    if i >= 2:
                        outputs(name, i - 2)

            e.wait_ge(sem["masks_ready"], 1)
            for n in range(4):
                piece(n)
                if n:
                    piece_end(n - 1)
            piece_end(3)
            norm_stage(0)
            take_jobs("lat")
            e.wait_ge(sem["rs_lat"], 2)
            for m in range(M):
                c = SS["lat"] + m
                chain(e.tensor_scalar(lat[:, m, 0:256], lat[:, m, 0:256], rstd[:, c:c + 1], None, ALU.mult))
                ins = e.tensor_scalar(lat[:, m, 256:384], lat[:, m, 256:384], rstd[:, c + 2:c + 3], None, ALU.mult)
                if m:
                    ins.then_inc(sem["lat_normed"], 1)
                else:
                    chain(ins)
            take_jobs("q_mb")
            take_jobs("k_mb")
            e.wait_ge(sem["cos_sin"], 1)
            for a, stage in enumerate(("q_mb", "k_mb")):
                copied(e, stage)
                v = qk_mb[:, a].rearrange("p m (h d) -> p m h d", d=64)
                tmp = [rope_tmp[:, i, :].rearrange("p (m h d) -> p m h d", m=M, h=8) for i in range(4)]
                rope(v[:, :, :, 0:32], v[:, :, :, 32:64], angles(0, 16, 48, 8), angles(1, 16, 48, 8),
                     v[:, :, :, 0:32], v[:, :, :, 32:64], tmp).then_inc(sem["mb_roped"], 1)
                e.wait_ge(sem["mb_roped"], a + 1)
            take_jobs("v_mb")

            def put_latent(i, b):
                for k in range(2):
                    ins = e.tensor_scalar(latT[:, k, :], b[:, k * S:(k + 1) * S], cols[:, C_GQ + k:C_GQ + k + 1],
                                          None, ALU.mult)
                return ins
            turn_out("latT", 0, put_latent)
            take_jobs("uq")
            take_jobs("ukv")
            copied(e, "uq")
            tmp = [rope_tmp[:, i, 0:256].rearrange("p (m h d) -> p m h d", m=M, h=8) for i in range(4)]
            v = q_up.rearrange("p m (h d) -> p m h d", d=96)
            chain(rope(v[:, :, :, 64:80], v[:, :, :, 80:96], angles(0, 0, 16, 8), angles(1, 0, 16, 8),
                       v[:, :, :, 64:80], v[:, :, :, 80:96], tmp))
            tmp = [rope_tmp[:, i, 0:32].rearrange("p (m d) -> p m d", m=M) for i in range(4)]
            r1, r2, c_, s_ = lat[:, :, 384:400], lat[:, :, 400:416], cs[:, :, 0, 0:16], cs[:, :, 1, 0:16]
            for t_, (a_, b_) in zip(tmp, ((r1, c_), (r2, s_), (r2, c_), (r1, s_))):
                chain(e.tensor_tensor(t_, a_, b_, ALU.mult))
            wide = [t_.unsqueeze(2).to_broadcast([P, M, 8, 16]) for t_ in tmp]
            v = k_up.rearrange("p m (h d) -> p m h d", d=96)
            chain(e.tensor_tensor(v[:, :, :, 64:80], wide[0], wide[1], ALU.subtract))
            copied(e, "ukv")
            e.tensor_tensor(v[:, :, :, 80:96], wide[2], wide[3], ALU.add).then_inc(sem["mla_roped"], 1)
            for name, dst in (("mbqT", qT_mb), ("mbkT", kT_mb)):
                for i in range(2):
                    turn_out(name, i, plain(dst))
            attention("mb", 8)
            for i in range(8):
                turn_out("mlaT", i, plain(qk[:, 8:24, :], 96))
            attention("mla", 8)
            e.wait_ge(sem["z_sig"], 1)
            zz = act[:, 832:2880]
            chain(e.tensor_tensor(zz, zz, scrA[:, :, :].rearrange("p m n -> p (m n)"), ALU.mult))
            e.wait_ge(sem["o_taken"], plan.pt0["sel"])
            for a, name in enumerate(("z_mla", "z_mb")):
                o = o_blk[:, a]
                e.tensor_tensor(o, o, z[name], ALU.mult).then_inc(sem["u_ready"], 1)
            for i in range(4):
                turn_out("uT", i, plain(hT))
            take_jobs("w_o_mla")
            take_jobs("w_o_moba")
            for i in range(4):
                turn_out("yT", i, plain(hT))
            take_jobs("w_out")
            e.wait_ge(sem["rs_y"], 1)
            e.wait_ge(sem["x_in"], 16)
            for m in range(M):
                c = SS["y"] + m
                chain(e.scalar_tensor_tensor(out=scrA[:, m, :], in0=scrA[:, m, :], scalar=rstd[:, c:c + 1],
                                             in1=gate[:, 0, :], op0=ALU.mult, op1=ALU.mult))
                e.tensor_tensor(x[:, m, :], x[:, m, :], scrA[:, m, :], ALU.add).then_inc(sem["x_done0"], 1)

            norm_stage(1)
            take_jobs("nsa_in")
            copied(e, "nsa_in")
            for m in range(M):
                for c in range(2):
                    ins = e.tensor_copy(kv_dup[:, m, :, :, c, :].rearrange("p a g d -> p (a g) d"),
                                        nsa[:, m, 1024:1536].rearrange("p (b d) -> p b d", d=64))
            ins.then_inc(sem["kv_doubled"], 1)
            for m in range(M):
                gl = nsa[:, m, 2560:2608]
                e.tensor_tensor(gl, gl, b_gate, ALU.add).then_inc(sem["gl_biased"], 1)
            for m in range(M):
                e.wait_ge(sem["nsa_sq"], 2 * m + 2)
                c = SS["nsa"] + 16 * m
                e.tensor_reduce(ss[:, c:c + 16], scrA[:, m, :].rearrange("p (h d) -> p h d", d=64), AX.X, ALU.add)\
                    .then_inc(sem["ss_nsa"], 1)
                c = SS["nsa"] + 32 + 8 * m
                e.tensor_reduce(ss[:, c:c + 8], act[:, 7264 + 512 * m:7776 + 512 * m].rearrange("p (h d) -> p h d", d=64),
                                AX.X, ALU.add).then_inc(sem["ss_nsa"], 1)
            for i in range(4):
                w = works["cmpin"] + i
                a, g0 = i // 2, 2 * (i % 2)
                e.wait_ge(sem["work_ready"], w + 1)
                for half_ in range(2):
                    lo = 64 * half_
                    src = bank[4 + w % 2][lo:lo + 64, :].rearrange("p (g i t c) -> p g i t c", g=2, i=16, c=2)[:, :, :, :, half_]
                    for h in range(2):
                        for g in range(2):
                            pe0 = (C_PEK, C_PEV)[a] + 8 * h
                            pos = cols[lo:lo + 64, pe0:pe0 + 8].unsqueeze(1).to_broadcast([64, 16, 8])
                            ins = e.tensor_tensor(z_blk[lo:lo + 64, a, h, g0 + g], src[:, g], pos, ALU.add)
                ins.then_inc(sem["turned_dve"], 1)
            e.wait_ge(sem["rs_nsa"], 1)

            def scale_heads(v, c, heads, gain):
                r = rstd[:, c:c + heads].unsqueeze(2).to_broadcast([P, heads, 64])
                chain(e.tensor_tensor(v, v, r, ALU.mult))
                return e.tensor_tensor(v, v, gain.unsqueeze(1).to_broadcast([P, heads, 64]), ALU.mult)

            def hidden_cmp(a):
                w = works["hid"] + a
                e.wait_ge(sem["hid_sig"], a + 1)
                e.tensor_tensor(hid[:, a, :], bank[4 + w % 2][:, 0:60], stat[:, 64:124], ALU.mult)\
                    .then_inc(sem["turned_dve"], 1)
                e.wait_ge(sem["turned_dve"], plan.work_free[w][1])

            hidden_cmp(0)
            hidden_cmp(1)
            for f in range(2):
                src = hid[:, 1, 30 * f:30 * f + 30].rearrange("p (g c) -> p g c", g=2)
                ins = e.tensor_copy(hid_rep[:, f], src.unsqueeze(2).to_broadcast([P, 2, 4, 15]))
            ins.then_inc(sem["hid_ready"], 1)
            w = works["kv_cmp"]
            e.wait_ge(sem["work_ready"], w + 1)
            e.tensor_copy(k_cmp[0:60, :], bank[4 + w % 2][0:60, 0:64]).then_inc(sem["turned_dve"], 1)
            e.wait_ge(sem["turned_dve"], plan.work_free[w][1])
            chain(e.tensor_tensor(k_cmp2[0:60, 0, :], k_cmp[0:60, :], k_cmp[0:60, :], ALU.mult))
            c = SS["kc"]
            e.tensor_reduce(ss[0:60, c:c + 1], k_cmp2[0:60, 0, :], AX.X, ALU.add).then_inc(sem["ss_kc"], 1)
            w = works["kv_cmp"] + 1
            e.wait_ge(sem["work_ready"], w + 1)
            for f in range(2):
                src = bank[4 + w % 2][0:120, 64 * f:64 * f + 64].unsqueeze(1).to_broadcast([120, 8, 64])
                ins = e.tensor_tensor(blockV[0:120, f], src, own[:, :].unsqueeze(2).to_broadcast([120, 8, 64]), ALU.mult)
            ins.then_inc(sem["turned_dve"], 1)
            for m in range(M):
                ins = scale_heads(nsa[:, m, 0:D].rearrange("p (h d) -> p h d", d=64), SS["nsa"] + 16 * m, 16, q_gain)
                if m:
                    ins.then_inc(sem["q_normed"], 1)
                else:
                    chain(ins)
            e.wait_ge(sem["rs_kc"], 1)
            for a in range(2):
                ins = e.scalar_tensor_tensor(out=k_cmp2[0:60, a, :], in0=k_cmp[0:60, :], scalar=rstd[0:60, c:c + 1],
                                             in1=k_gain[0:60, 0, :], op0=ALU.mult, op1=ALU.mult)
            ins.then_inc(sem["k_cmp_ready"], 1)
            w = works["kcT"]
            e.wait_ge(sem["work_ready"], w + 1)
            e.tensor_copy(kcT[:, :], bank[4 + w % 2][:, 0:60]).then_inc(sem["turned_dve"], 1)
            for i in range(4):
                turn_out("qcT", i, plain(qcT))
            e.wait_ge(sem["gl_ready"], 1)
            wide_h = lambda ap, n: ap.unsqueeze(2).to_broadcast([P, 16, n])
            for m in range(M):
                p3 = pc[:, m, :].rearrange("p (h c) -> p h c", c=15)
                for odd in range(2):
                    w = works["cmpS"] + 2 * m + odd
                    e.wait_ge(sem["work_ready"], w + 1)
                    e.tensor_tensor(p3[:, odd:16:2], bank[4 + w % 2][:, 0:120].rearrange("p (h c) -> p h c", c=15),
                                    cmp_neg[:, m, :].unsqueeze(1).to_broadcast([P, 8, 15]), ALU.add)\
                        .then_inc(sem["turned_dve"], 1)
                    e.wait_ge(sem["turned_dve"], plan.work_free[w][1])
                chain(e.tensor_reduce(stat[:, 16 * m:16 * m + 16], p3, AX.X, ALU.max, negate=True))
                e.tensor_tensor(p3, p3, wide_h(stat[:, 16 * m:16 * m + 16], 15), ALU.add).then_inc(sem["pc_shifted"], 1)
            for m in range(M):
                p3 = pc[:, m, :].rearrange("p (h c) -> p h c", c=15)
                s_ = stat[:, 32 + 16 * m:48 + 16 * m]
                e.wait_ge(sem["pc_exp"], m + 1)
                chain(e.tensor_reduce(s_, p3, AX.X, ALU.add))
                e.tensor_tensor(p3, p3, cmp_keep[:, m, :].unsqueeze(1).to_broadcast([P, 16, 15]), ALU.mult)\
                    .then_inc(sem["pc_ready"], 1)
                chain(e.reciprocal(s_, s_))
                g = nsa[:, m, 2560:2608].rearrange("p (h b) -> p h b", b=3)[:, :, 0]
                chain(e.tensor_tensor(s_, s_, g, ALU.mult))
            chain(e.tensor_copy(q_rot[:, :, :], nsa[:, :, 0:D]))
            v = q_rot.rearrange("p m (h d) -> p m h d", d=64)
            tmp = [k_dup_tmp[:, i, :].rearrange("p (m h d) -> p m h d", m=M, h=16) for i in range(4)]
            rope(v[:, :, :, 0:8], v[:, :, :, 8:16], angles(0, 48, 56, 16), angles(1, 48, 56, 16),
                 v[:, :, :, 0:8], v[:, :, :, 8:16], tmp).then_inc(sem["q_roped"], 1)
            e.wait_ge(sem["q_roped"], 1)
            for b_, k0 in enumerate((1536, 2048)):
                for m in range(M):
                    v = nsa[:, m, k0:k0 + 256].rearrange("p (h d) -> p h d", d=64)
                    chain(scale_heads(v, SS["nsa"] + 32 + 8 * m + 4 * b_, 4, k_gain[:, 1 + b_, :]))
                v = nsa[:, :, k0:k0 + 256].rearrange("p m (h d) -> p m h d", d=64)
                tmp = [k_dup_tmp[:, i, 0:64].rearrange("p (m h d) -> p m h d", m=M, h=4) for i in range(4)]
                chain(rope(v[:, :, :, 0:8], v[:, :, :, 8:16], angles(0, 48, 56, 4), angles(1, 48, 56, 4),
                           v[:, :, :, 0:8], v[:, :, :, 8:16], tmp))
            for b_, k0 in enumerate((1536, 2048)):
                for m in range(M):
                    for c_ in range(2):
                        ins = e.tensor_copy(k_dup[:, m, b_, :, c_, :],
                                            nsa[:, m, k0:k0 + 256].rearrange("p (h d) -> p h d", d=64))
            ins.then_inc(sem["k_doubled"], 1)
            for m in range(M):
                for f in range(2):
                    w = works["cmpO"] + 2 * m + f
                    e.wait_ge(sem["work_ready"], w + 1)
                    s_ = stat[:, 32 + 16 * m + 8 * f:40 + 16 * m + 8 * f].unsqueeze(2).to_broadcast([P, 8, 64])
                    e.tensor_tensor(o_rows[:, m, 512 * f:512 * f + 512].rearrange("p (h d) -> p h d", d=64),
                                    bank[4 + w % 2][:, :].rearrange("p (h d) -> p h d", d=64), s_, ALU.mult)\
                        .then_inc(sem["turned_dve"], 1)
            for i in range(4):
                turn_out("qrT", i, plain(qrT))
            for i in range(4):
                turn_out("kT", i, plain(qk[:, 16:24, :]))
            attention("sel", 16)
            attention("win", 16)
            e.memset(stat[:, 126:127], 0.0).then_inc(sem["o_rows_done"], 1)
            for i in range(4):
                turn_out("o1T", i, plain(hT))
            take_jobs("nsa_out")
            norm_stage(2)
            take_jobs("mlp_in0")
            take_jobs("mlp_out0")

            norm_stage(3)
            take_jobs("diff_in")
            for m in range(M):
                for a in range(2):
                    e.wait_ge(sem["diff_sq"], 2 * m + a + 1)
                    src = scrA[:, m, :] if a == 0 else scrB[:, m * D:(m + 1) * D]
                    c = SS["diff"] + 32 * a + 16 * m
                    e.tensor_reduce(ss[:, c:c + 16], src.rearrange("p (h d) -> p h d", d=64), AX.X, ALU.add)\
                        .then_inc(sem["ss_diff"], 1)
            e.wait_ge(sem["rs_diff"], 1)
            tmp = [scrB[:, 256 * i:256 * i + 256].rearrange("p (m h d) -> p m h d", m=M, h=16) for i in range(4)]
            for a in range(2):
                for m in range(M):
                    v = dif[:, m, a * D:(a + 1) * D].rearrange("p (h d) -> p h d", d=64)
                    chain(scale_heads(v, SS["diff"] + 32 * a + 16 * m, 16, (dq_gain, dk_gain)[a]))
                v = dif[:, :, a * D:(a + 1) * D].rearrange("p m (h d) -> p m h d", d=64)
                rope(v[:, :, :, 0:8], v[:, :, :, 8:16], angles(0, 48, 56, 16), angles(1, 48, 56, 16),
                     v[:, :, :, 0:8], v[:, :, :, 8:16], tmp).then_inc(sem["dqk_roped"], 1)
                e.wait_ge(sem["dqk_roped"], a + 1)
            for name, dst in (("dqT", dqT), ("dkT", dkT)):
                for i in range(4):
                    turn_out(name, i, plain(dst))
            attention("diff", 8, comps=2)
            e.wait_ge(sem["o_taken"], plan.n_pt)
            for m in range(M):
                e.wait_ge(sem["sub_sq"], m + 1)
                c = SS["sub"] + 8 * m
                e.tensor_reduce(ss[:, c:c + 8], scrB[:, m * D:(m + 1) * D].rearrange("p (h d) -> p h d", d=P),
                                AX.X, ALU.add).then_inc(sem["ss_sub"], 1)
            e.wait_ge(sem["rs_sub"], 1)
            for m in range(M):
                c = SS["sub"] + 8 * m
                v = scrA[:, m, :].rearrange("p (h d) -> p h d", d=P)
                chain(e.tensor_tensor(v, v, rstd[:, c:c + 8].unsqueeze(2).to_broadcast([P, 8, P]), ALU.mult))
                e.tensor_tensor(v, v, sub_gain.unsqueeze(1).to_broadcast([P, 8, P]), ALU.mult)\
                    .then_inc(sem["d_rows_done"], 1)
            for i in range(4):
                turn_out("o2T", i, plain(hT))
            take_jobs("diff_out")
            norm_stage(4)
            take_jobs("mlp_in1")
            take_jobs("mlp_out1")
    return nc


NAMES = ["x", "c", "positions", "w_ada", "b_ada", "g_pre", "g_post", "w_in", "g_q_lat", "w_uq", "g_kv_lat", "w_ukv",
         "w_o_mla", "w_o_moba", "b_merge", "w_out", "c_2", "positions_2", "ln_mix_g_2", "ln_mlp_g_2", "w_ada_2",
         "b_ada_2", "w_mlp_in_2", "w_mlp_out_2", "nsa_w_in_2", "nsa_b_gate_2", "nsa_q_gain_2", "nsa_k_gain_2",
         "nsa_pe_k_2", "nsa_w_ck1_2", "nsa_w_ck2_2", "nsa_pe_v_2", "nsa_w_cv1_2", "nsa_w_cv2_2", "nsa_w_out_2",
         "diff_w_in_2", "diff_q_gain_2", "diff_k_gain_2", "diff_lq1_2", "diff_lk1_2", "diff_lq2_2", "diff_lk2_2",
         "diff_subln_g_2", "diff_w_out_2"]


def kernel(**inputs):
    import concourse.bacc as bacc
    from concourse.bass_utils import run_bass_kernel_spmd

    freq = [np.float32(10000.0) ** (-np.arange(h, dtype=np.float32) / np.float32(h)) for h in (16, 32)]
    freq.append(np.float32(500000.0) ** (-np.arange(0, 16, 2, dtype=np.float32) / np.float32(16)))
    arrays = {"inv_freq": np.concatenate(freq).astype(np.float32)}
    for name in NAMES:
        arrays[name] = np.ascontiguousarray(inputs[name])
    nc = bacc.Bacc("TRN2", target_bir_lowering=False, num_devices=1)
    t_in = {name: nc.dram_tensor("in_" + name, a.shape, mybir.dt.from_np(a.dtype), kind="ExternalInput").ap()
            for name, a in arrays.items()}
    out = nc.dram_tensor("out_x", (1, S, D), F32, kind="ExternalOutput").ap()
    build(nc, t_in, out)
    r = run_bass_kernel_spmd(nc, [{"in_" + k: v for k, v in arrays.items()}], core_ids=[0])
    return r.results[0]["out_x"]
```

```python
from contextlib import ExitStack
import math
import numpy as np

import concourse.bass as bass
from concourse import mybir
from concourse.alu_op_type import AluOpType as ALU

ACT = mybir.ActivationFunctionType
AX = mybir.AxisListType
F32 = mybir.dt.float32
F32R = mybir.dt.float32r
I32 = mybir.dt.int32

P = 128
S = 256
M = S // P
D = 1024
DT = D // P
EPS = 1e-6
NEG = -1e30
RING = 4
SLOT = 2048
PART = 1024
PARTS = 3
ADA_RING = 2
ADA_FIRST = 6
LAM_INIT = 0.8 - 0.6 * math.exp(-0.3)
MLA_SCALE = (64 + 32) ** -0.5
HEAD_SCALE = 64 ** -0.5

DVE_JOBS = ("merge", "w_o_mla", "w_o_moba", "nsa_out", "diff_out", "mlp_out0", "mlp_out1")



class Plan:
    def __init__(self):
        self.chunks = []
        self.jobs = []
        self.parts = []
        self.last_part = []
        self.pair_at = {}
        self.works = {}
        self.n_works = 0
        self.n_units = 0
        self.work_free = []
        self.turned = {"act": 0, "dve": 0}
        self.turned_after = {}
        self.pt_of_unit = []
        self.copied = {"act": 0, "dve": 0}
        self.copied_after = {}
        self.job_free = []
        self.job_done = []
        self.chunk_free = {}
        self.low_by, self.low_count = [], []

    def chunk(self, weight, k0, kt, c0, n):
        self.chunks.append((weight, k0, kt, c0, n))
        return len(self.chunks) - 1

    def pair(self, stage, weight, kt, c0, n, lhs="hT", lhs0=0, T=False, key=None):
        spec = dict(stage=stage, lhs=lhs, lhs0=lhs0, n=n, T=T, key=c0 if key is None else key, parts=[])
        for k0 in range(0, kt, 4):
            c = self.chunk(weight, k0, min(4, kt - k0), c0, n)
            for k in range(0, min(4, kt - k0), 2):
                spec["parts"].append(len(self.parts))
                self.parts.append((c, k, min(2, min(4, kt - k0) - k), k0 + k))
        self.last_part.append(len(self.parts) - 1)
        for half in range(2):
            self.jobs.append(dict(spec, half=half, m=half, c0=spec["key"]))
        self.pair_at[(stage, spec["key"])] = len(self.last_part) - 1

    def work(self, stage, n, by="both"):
        self.works[stage] = self.n_works
        for i in range(n):
            w = self.n_works + i
            if by == "units":
                self.n_units += 1
                self.work_free.append(("probs_ready", self.n_units))
                continue
            who = ("act", "dve")[w % 2] if by == "both" else by
            self.turned[who] += 1
            self.work_free.append(("turned_" + who, self.turned[who]))
        self.n_works += n
        self.turned_after[stage] = dict(self.turned)


def make_plan():
    p = Plan()
    p.pair("lat", "w_in", DT, 0, 416)
    for i, name in enumerate(("q_mb", "k_mb", "v_mb")):
        p.pair(name, "w_in", DT, 928 + 512 * i, 512, key=0)
    for n0, n in ((0, 512), (512, 256)):
        p.pair("uq", "w_uq", 2, n0, n, lhs="latT")
    for n0 in (0, 512):
        p.pair("ukv", "w_ukv", 1, n0, 512, lhs="latT", lhs0=2)
    for name, c0 in (("z_mla", 416), ("z_mb", 2464)):
        p.pair(name, "w_in", DT, c0, 512, key=0)
    for i in range(4):
        p.pair("merge", "w_in", DT, 2976 + 512 * i, 512, key=512 * i)
    for name, lhs0 in (("w_o_mla", 0), ("w_o_moba", 4)):
        for n0 in (0, 512):
            p.pair(name, name, 4, n0, 512, lhs0=lhs0)
    for n0 in (0, 512):
        p.pair("w_out", "w_out", DT, n0, 512)
    for layer, (first, n_first, mix_out) in enumerate((("nsa_in", 2608, "nsa_out"), ("diff_in", 3072, "diff_out"))):
        for n0 in range(0, n_first, 512):
            p.pair(first, first, DT, n0, min(512, n_first - n0))
        if layer == 0:
            p.cmp_chunk = [p.chunk(w, 0, 16, 0, 128) for w in ("ck1", "cv1")]
        for n0 in (0, 512):
            p.pair(mix_out, mix_out, DT, n0, 512)
        for f in range(8):
            p.pair("mlp_in%d" % layer, "mlp_in%d" % layer, DT, 512 * f, 512, T=True)
        for n0 in (0, 512):
            p.pair("mlp_out%d" % layer, "mlp_out%d" % layer, 32, n0, 512, lhs="hidT")
    for stage, n, by in (
            ("cols", 1, "dve"), ("x0", 4, "act"), ("latT", 2, "dve"), ("mbqT", 2, "both"), ("mbkT", 2, "both"),
            ("mb", 8, "units"), ("mlaT", 8, "both"), ("mla", 8, "units"), ("uT", 4, "dve"), ("yT", 4, "dve"),
            ("x1", 4, "act"), ("cmpin", 4, "dve"), ("hid", 2, "dve"), ("kv_cmp", 2, "dve"), ("kcT", 1, "dve"),
            ("qcT", 4, "both"), ("cmpS", 4, "dve"), ("cmpT", 2, "act"), ("cmpO", 4, "dve"), ("qrT", 4, "both"),
            ("kT", 4, "both"), ("sel", 16, "units"), ("win", 16, "units"), ("o1T", 4, "dve"), ("x2", 4, "act"),
            ("x3", 4, "act"), ("dqT", 4, "both"), ("dkT", 4, "both"), ("diff", 16, "units"), ("o2T", 4, "dve"),
            ("x4", 4, "act")):
        p.work(stage, n, by)
    p.unit0, p.pt0, u, t = {}, {}, 0, 0
    for name, n, nt in (("mb", 8, 8), ("mla", 8, 8), ("sel", 16, 16), ("win", 16, 16), ("diff", 16, 8)):
        p.unit0[name], p.pt0[name] = u, t
        p.pt_of_unit += [t + i * nt // n for i in range(n)]
        u, t = u + n, t + nt
    p.n_pt = t
    for job in p.jobs:
        who = job["by"] = "dve" if job["stage"] in DVE_JOBS else "act"
        p.copied[who] += 1
        p.job_free.append(("copied_" + who, p.copied[who]))
        p.copied_after[job["stage"]] = dict(p.copied)
    for j in range(len(p.jobs)):
        p.job_done.append(("first_done", j // 2 + 1) if j % 2 == 0 else ("part_done", p.last_part[j // 2] + 1))
    n_low = {"dve": 0, "pool": 0}
    for q, (c, k, nk, k_w) in enumerate(p.parts):
        stage = next(p.jobs[2 * i]["stage"] for i, last in enumerate(p.last_part) if q <= last)
        who = "pool" if q % 2 and not stage.startswith("mlp_in") else "dve"
        n_low[who] += 1
        p.low_by.append(who)
        p.low_count.append(n_low[who])
        p.chunk_free.setdefault(c, {})["low_ready_" + who] = n_low[who]
    for a in range(2):
        p.chunk_free[p.cmp_chunk[a]] = {"work_ready": p.works["hid"] + a + 1}
    p.pieces = [("w_ada", 0, 512 * i) for i in range(6)]
    for layer in range(2):
        p.pieces += [("w_ada_2", layer, 512 * i) for i in range(12)]
    def spread(pieces, a, b):
        halves = [2 * n + h for n in pieces for h in range(2)]
        for i, h in enumerate(halves):
            p.half_after[h] = a + i * (b - a) // len(halves)

    def first_part(stage, key=0):
        q = p.pair_at[(stage, key)]
        return p.last_part[q - 1] + 1 if q else 0
    p.half_after = {}
    spread(range(4, 14), 5, first_part("w_out"))
    spread(range(14, 18), first_part("nsa_in"), first_part("nsa_out") - 4)
    spread(range(18, 26), first_part("mlp_in0"), first_part("diff_in") - 4)
    spread(range(26, 30), first_part("diff_in"), first_part("diff_out") - 4)
    p.piece_sum = {}
    for n in range(4, 30):
        p.piece_sum.setdefault(p.half_after[2 * n + 1] + 2, []).append(n)
    last_of = {c: q for q, (c, _, _, _) in enumerate(p.parts)}
    after = {}
    for h in range(8, 60):
        taken = p.half_after.get(h - ADA_RING, 0)
        fit = [c for c in sorted(last_of) if c - RING in last_of and last_of[c - RING] <= p.half_after[h] + PARTS]
        late = [c for c in fit if last_of[c - RING] >= taken + PARTS]
        after.setdefault(late[0] if late else max(fit, default=0), []).append(h)
    at, moved = 0, {}
    for h in range(8, 60):
        at = max(at, next(c for c, hs in after.items() if h in hs))
        moved.setdefault(at, []).append(h)
    after = moved
    p.loads = [("ada", h) for h in range(8)]
    for c in range(len(p.chunks)):
        p.loads.append(("w", c))
        p.loads += [("ada", h) for h in after.get(c, [])]
    return p


def build(nc, t_in, out):
    plan = make_plan()
    jobs, works = plan.jobs, plan.works
    with ExitStack() as ctx:
        def sb(name, shape, dt=F32):
            return ctx.enter_context(nc.sbuf_tensor(name, shape, dt))

        class Named(dict):
            def __missing__(self, name):
                self[name] = ctx.enter_context(nc.semaphore(name))
                return self[name]

        sem = Named()
        bank = [ctx.enter_context(nc.psum_tensor("bank%d" % i, [P, 512], F32)) for i in range(8)]

        ring = sb("ring", [P, RING, SLOT])
        high = sb("weight_high", [P, PARTS, PART], F32R)
        low = sb("weight_low", [P, PARTS, PART], F32R)
        ada_ring = sb("ada_ring", [P, ADA_RING, 4, 512])
        acc = sb("ada_acc", [P, 2, 512])
        x = sb("x_rows", [P, M, D])
        hT = [sb("hT_" + part, [P, DT, S], F32R) for part in ("high", "low")]
        A_ACT, A_QK, A_B = 9312, 24 * S, 2 * D
        base = nc.sbuf_base
        region = sb("region", [P, A_ACT + A_QK + A_B])
        act = region[:, 0:A_ACT]
        qk = region[:, A_ACT:A_ACT + A_QK].rearrange("p (a s) -> p a s", s=S)
        scrB = region[:, A_ACT + A_QK:]

        def over(name, shape, first):
            return nc.alloc_sbuf_tensor_at(name, shape, F32R, offset=base + 4 * first)
        hidT = [over("hidT_" + part, [P, 32, S], 32 * S * i) for i, part in enumerate(("high", "low"))]
        latT = [over("latT_" + part, [P, 3, S], A_ACT + (18 + 3 * i) * S) for i, part in enumerate(("high", "low"))]
        scrA = sb("scratch_a", [P, M, D])
        gate = sb("gates", [P, 3, D])
        probs = sb("probs", [P, 4, 384])
        probsT = sb("probsT", [P, 2, 384])
        ident = sb("ident", [P, P])
        ones = sb("ones", [P, P])
        causal = sb("causal", [P, P])
        cmp_neg = sb("cmp_neg", [P, M, 15])
        cmp_keep = sb("cmp_keep", [P, M, 15])
        own = sb("own_head", [120, 8])
        vec_rows = act[0:107, 0:128]
        vec_rows2 = act[0:64, 128:256]
        cols = sb("cols", [P, 192])
        silu_c = sb("silu_c", [P, 16])
        mod = sb("mod_cols", [P, 5, 2, 8])
        gs = sb("gain_scale", [P, 5, 8])
        tiny = sb("tiny", [P, 880])
        pos_i = sb("pos_i", [P, 2, M], I32)
        pos_f = sb("pos_f", [P, 2, M])
        cs = sb("cos_sin", [P, M, 2, 56])
        trig = scrA[:, 1, 0:224].rearrange("p (m a n) -> p m a n", m=M, a=2)
        neg_max = sb("neg_max", [P, 16])
        sums = sb("prob_sums", [P, 16])
        inv = sums
        ss = sb("sum_squares", [P, 160])
        rstd = ss
        half_neg = sb("minus_half", [P, 64])
        stat = sb("stat", [P, 128])

        q_gain, k_gain = tiny[:, 0:64], tiny[:, 64:256].rearrange("p (a d) -> p a d", d=64)
        dq_gain, dk_gain, sub_gain = tiny[:, 256:320], tiny[:, 320:384], tiny[:, 384:512]
        b_gate, lqk = tiny[:, 512:560], tiny[:, 560:816].rearrange("p (a d) -> p a d", d=64)
        inv_freq = tiny[:, 816:872]
        lam_tmp = scrA[:, 1, 256:384].rearrange("p (a d) -> p a d", d=64)
        lam = tiny[:, 872:880]

        C_C, C_PRE, C_BADA, C_MIX, C_MLP, C_GQ, C_GKV, C_PEK, C_PEV, C_BADA2 = 0, 16, 24, 40, 56, 72, 74, 75, 91, 128

        lat = act[:, 0:832].rearrange("p (m n) -> p m n", m=M)
        v_mla = scrA[:, 0, :].rearrange("p (m h d) -> p m h d", m=M, h=8)
        z = {"z_mla": act[:, 832:1856].rearrange("p (m n) -> p m n", m=M),
             "z_mb": act[:, 1856:2880].rearrange("p (m n) -> p m n", m=M)}
        merge = act[:, 2880:6976].rearrange("p (m n) -> p m n", m=M)
        qk_mb = act[:, 6976:9024].rearrange("p (a m n) -> p a m n", a=2, m=M)
        y_rows = act[:, 6976:9024].rearrange("p (m n) -> p m n", m=M)
        v_mb = scrA[:, 1, :].rearrange("p (m h d) -> p m h d", m=M, h=8)
        qT_mb, kT_mb = qk[:, 0:4, :], qk[:, 4:8, :]
        qT_mla, kT_mla = qk[:, 8:16, :], qk[:, 16:24, :]
        b_merge = scrB
        q_up = act[:, 2880:4416].rearrange("p (m n) -> p m n", m=M)
        k_up = act[:, 4416:5952].rearrange("p (m n) -> p m n", m=M)
        rope_tmp = act[:, 832:2880].rearrange("p (a n) -> p a n", a=4)
        o_blk = act[:, 6976:9024].rearrange("p (a m n) -> p a m n", a=2, m=M)

        nsa = act[:, 0:5216].rearrange("p (m n) -> p m n", m=M)
        q_rot = act[:, 5216:7264].rearrange("p (m n) -> p m n", m=M)
        k_dup = act[:, 7264:9312].rearrange("p (m a g c d) -> p m a g c d", m=M, a=2, g=4, c=2)
        kv_dup = q_rot.rearrange("p m (a g c d) -> p m a g c d", a=2, g=4, c=2)
        qcT, qrT, kselT, kwinT = qk[:, 0:8, :], qk[:, 8:16, :], qk[:, 16:20, :], qk[:, 20:24, :]
        z_blk = scrB[:, :].rearrange("p (w h g i t) -> p w h g i t", w=2, h=2, g=4, i=16)
        small = qk[:, 20:24, :].rearrange("p a s -> p (a s)")
        hid = small[:, 0:120].rearrange("p (a n) -> p a n", a=2)
        hid_rep = small[:, 128:368].rearrange("p (f g r c) -> p f g r c", f=2, g=2, r=4)
        k_cmp = small[:, 384:448]
        k_cmp2 = small[:, 448:576].rearrange("p (a d) -> p a d", a=2)
        kcT = small[:, 576:636]
        w_c2 = sb("w_c2", [P, 2, 64])
        blockV = scrB[:, 0:1024].rearrange("p (f h d) -> p f h d", f=2, h=8)
        pcT = scrB[:, 1024:1536].rearrange("p (m f q) -> p m f q", m=M, f=2)
        pc = scrB[:, 1536:2016].rearrange("p (m n) -> p m n", m=M)
        o_rows = scrA
        k_dup_tmp = scrA[:, 0, :].rearrange("p (a n) -> p a n", a=4)
        o_tmp = scrB[:, 0:256].rearrange("p (a m d) -> p a m d", a=2, m=M)

        dif = act[:, 0:6144].rearrange("p (m n) -> p m n", m=M)
        dqT, dkT = qk[:, 0:8, :], qk[:, 8:16, :]

        whole = probs[:, :, :].rearrange("p a n -> p (a n)").rearrange("p (a n) -> p a n", n=512)
        operand = {"hT": hT, "latT": latT, "hidT": hidT}

        def slot(c):
            w, k0, kt, c0, n = plan.chunks[c]
            return ring[:, c % RING, 0:kt * n].rearrange("p (k n) -> p k n", k=kt)

        def part_words(q):
            c, k, nk, _ = plan.parts[q]
            n = plan.chunks[c][4]
            return ring[:, c % RING, k * n:(k + nk) * n], nk * n

        weights = {k: t_in[k][0].rearrange("(t p) n -> p t n", p=P) for k in
                   ("w_in", "w_uq", "w_ukv", "w_o_mla", "w_o_moba", "w_out", "w_ada")}
        for name, src, i in (("nsa_in", "nsa_w_in_2", 0), ("nsa_out", "nsa_w_out_2", 0), ("diff_in", "diff_w_in_2", 0),
                             ("diff_out", "diff_w_out_2", 0), ("ck1", "nsa_w_ck1_2", 0), ("cv1", "nsa_w_cv1_2", 0),
                             ("mlp_in0", "w_mlp_in_2", 0), ("mlp_in1", "w_mlp_in_2", 1),
                             ("mlp_out0", "w_mlp_out_2", 0), ("mlp_out1", "w_mlp_out_2", 1)):
            weights[name] = t_in[src][i].rearrange("(t p) n -> p t n", p=P)
        ada2 = [t_in["w_ada_2"][i].rearrange("(t p) n -> p t n", p=P) for i in range(2)]

        def ada_slot(h):
            if h < ADA_FIRST:
                return region[:, 1024 + SLOT * h:1024 + SLOT * (h + 1)].rearrange("p (k n) -> p k n", k=4)
            return ada_ring[:, h % 2]

        def ada_arrived(h):
            return ("ada_first%d" % h, 16) if h < ADA_FIRST else ("ada_in%d" % (h % 2), 16 * ((h - ADA_FIRST) // 2 + 1))

        def piece_source(n):
            w, layer, c0 = plan.pieces[n]
            return (weights["w_ada"] if w == "w_ada" else ada2[layer]), c0

        def piece_use(n):
            if n < 6:
                part, half = n // 2, n % 2
                return ("gate", 0, 512 * half) if part == 2 else ("col", 0, part, 4 * half, C_BADA + 4 * n)
            layer, q = (n - 6) // 12, (n - 6) % 12
            part, half = q // 2, q % 2
            if part in (2, 5):
                return "gate", (1 + 2 * layer + part // 5) % 3, 512 * half
            norm = 1 + 2 * layer + part // 3
            return "col", norm, part % 3, 4 * half, C_BADA2 + 32 * layer + 16 * (part // 3) + 4 * (q % 6)

        class Chain:
            def __init__(self, eng, name):
                self.eng, self.sem, self.n = eng, sem[name], 0

            def __call__(self, ins):
                self.n += 1
                ins.then_inc(self.sem, 1)
                self.eng.wait_ge(self.sem, self.n)

        def head_rows(ap, d):
            return ap.rearrange("p m (h d) -> p m h d", d=d)

        def spread(ap, shape):
            return ap.to_broadcast(shape)

        def turned(eng, stage):
            for who in ("act", "dve"):
                eng.wait_ge(sem["turned_" + who], plan.turned_after[stage][who])

        def copied(eng, stage):
            for who in ("act", "dve"):
                if plan.copied_after[stage][who]:
                    eng.wait_ge(sem["copied_" + who], plan.copied_after[stage][who])

        pair_of = [p for p, q in enumerate(plan.last_part) for _ in range(q - (plan.last_part[p - 1] if p else -1))]

        def stage_parts(stage):
            return [q for q, p in enumerate(pair_of) if jobs[2 * p]["stage"] == stage]

        def beside_parts(name, step):
            parts = {"mb": stage_parts("z_mla") + stage_parts("z_mb"), "mla": stage_parts("merge")}.get(name, [])
            per = -(-len(parts) // 10)
            mine = parts[per * step:per * (step + 1)]
            return mine[:1], mine[1:]

        NORM_X = ["x0", "x1", "x2", "x3", "x4"]
        block = ctx.enter_context(nc.Block())

        @block.sync
        def _(sp):
            r = 0
            for src in (t_in["c"][0], t_in["c_2"][0], t_in["g_pre"][0], t_in["b_ada"][0, 0:2048],
                        t_in["ln_mix_g_2"].rearrange("a n -> (a n)"), t_in["ln_mlp_g_2"].rearrange("a n -> (a n)"),
                        t_in["g_q_lat"][0], t_in["g_kv_lat"][0]):
                n = src.shape[0] // P
                sp.dma_start(vec_rows[r:r + n, :], src.rearrange("(r n) -> r n", n=P)).then_inc(sem["rows_in"], 16)
                r += n
            for name in ("nsa_pe_k_2", "nsa_pe_v_2"):
                sp.dma_start(vec_rows[r:r + 16, :], t_in[name][0].rearrange("(r a) d -> r (a d)", a=2))\
                    .then_inc(sem["rows_in"], 16)
                r += 16
            for layer in range(2):
                for half_ in range(2):
                    q = 32 * layer + 16 * half_
                    sp.dma_start(vec_rows2[q:q + 16, :], t_in["b_ada_2"][layer, 3072 * half_:3072 * half_ + 2048]
                                .rearrange("(r n) -> r n", n=P)).then_inc(sem["rows_in"], 16)
            for kind, n in plan.loads:
                if kind == "w":
                    w, k0, kt, c0, cn = plan.chunks[n]
                    if n >= RING:
                        for name, value in plan.chunk_free[n - RING].items():
                            sp.wait_ge(sem[name], value)
                    sp.dma_start(slot(n), weights[w][:, k0:k0 + kt, c0:c0 + cn]).then_inc(
                        sem["chunk_in%d" % (n % RING)], 16)
                else:
                    if n == 4:
                        sp.dma_start(x[:, :, :], t_in["x"][0].rearrange("(m p) n -> p m n", p=P))\
                            .then_inc(sem["x_in"], 16)
                    src, c0 = piece_source(n // 2)
                    if n >= ADA_FIRST + ADA_RING:
                        sp.wait_ge(sem["ada_used"], n - ADA_RING + 1)
                    k = 4 * (n % 2)
                    sp.dma_start(ada_slot(n), src[:, k:k + 4, c0:c0 + 512]).then_inc(sem[ada_arrived(n)[0]], 16)
            for m in range(M):
                sp.wait_ge(sem["x_done4"], m + 1)
                sp.dma_start(out[0, m * P:(m + 1) * P, :], x[:, m, :]).then_inc(sem["stored"], 16)
            sp.wait_ge(sem["stored"], 16 * M)

        @block.tensor
        def _(pe):
            def reduce_piece(n):
                pe.wait_ge(sem["ada_used"], 2 * n + 2)
                if n >= 1:
                    pe.wait_ge(sem["mod_taken"], n)
                use = piece_use(n)
                if use[0] == "gate":
                    mm = pe.matmul(bank[3][:, :], ones[:, :], acc[:, n % 2, :], start=True, stop=True)
                else:
                    for i in range(4):
                        mm = pe.matmul(bank[3][:, i:i + 1], acc[:, n % 2, i * P:(i + 1) * P], ones[:, 0:1],
                                       start=True, stop=True)
                mm.then_inc(sem["piece_summed"], 1)

            def bank_for(j):
                if j >= 3:
                    name, value = plan.job_free[j - 3]
                    pe.wait_ge(sem[name], value)
                return bank[j % 3]

            def run_part(q):
                c, _, nk, k_w = plan.parts[q]
                p = pair_of[q]
                first, last = q == 0 or pair_of[q - 1] != p, q == plan.last_part[p]
                job = jobs[2 * p]
                n = job["n"]
                pe.wait_ge(sem["low_ready_" + plan.low_by[q]], plan.low_count[q])
                wh, wl = [buf[:, q % PARTS, 0:nk * n].rearrange("p (k n) -> p k n", k=nk) for buf in (high, low)]
                ah, al = operand[job["lhs"]]
                for half in range(2):
                    j = 2 * p + half
                    b = bank_for(j) if first else bank[j % 3]
                    for k in range(nk):
                        a = job["lhs0"] + k_w + k
                        begin, end = first and k == 0, last and k == nk - 1
                        if job["T"]:
                            for i in range(2):
                                f = (2 * half + i) * P
                                for s_, (w, v) in enumerate(((wh, ah), (wh, al), (wl, ah))):
                                    mm = pe.matmul(b[:, i * S:(i + 1) * S], w[:, k, f:f + P], v[:, a, :],
                                                   start=begin and i == 0 and s_ == 0, stop=end and s_ == 2,
                                                   skip_group_check=True)
                        else:
                            t = slice(half * P, (half + 1) * P)
                            for s_, (v, w) in enumerate(((ah, wh), (ah, wl), (al, wh))):
                                mm = pe.matmul(b[:, 0:n], v[:, a, t], w[:, k, :],
                                               start=begin and s_ == 0, stop=end and s_ == 2)
                    if half == 0 and last:
                        mm.then_inc(sem["first_done"], 1)
                mm.then_inc(sem["part_done"], 1)
                for n_ in plan.piece_sum.get(q, []):
                    reduce_piece(n_)

            def run_stage(stage):
                for q in stage_parts(stage):
                    run_part(q)

            def work_bank(w):
                if w >= 2:
                    name, value = plan.work_free[w - 2]
                    pe.wait_ge(sem[name], value)
                return bank[4 + w % 2]

            def turn(stage, src, n_tiles, ready=None, per=2, rows=P):
                for i in range(0, n_tiles, per):
                    w = works[stage] + i // per
                    b = work_bank(w)
                    for k in range(i, min(i + per, n_tiles)):
                        for m in range(M):
                            if ready is not None and m + (i > 0) * M < M and k == i:
                                pe.wait_ge(sem[ready], m + 1)
                            s = src(k, m)
                            o = (k - i) * S + m * P
                            mm = pe.transpose(b[0:s.shape[-1], o:o + P], s, ident[:, :])
                    mm.then_inc(sem["work_ready"], 1)

            def scores(name, i, q, kk):
                w = works[name] + i
                b = work_bank(w)
                pe.matmul(b[:, 0:P], q[:, 0:P], kk[:, 0:P], start=True, stop=True)
                pe.matmul(b[:, P:384], q[:, P:S], kk[:, 0:S], start=True, stop=True).then_inc(sem["work_ready"], 1)

            def turn_probs(name, i, u):
                t = plan.pt0[name] + i
                if t >= 1:
                    pe.wait_ge(sem["pt_taken"], t)
                if name == "diff":
                    pe.wait_ge(sem["diff_mixed"], i + 1)
                else:
                    pe.wait_ge(sem["probs_ready"], u + 1)
                for a in range(3):
                    mm = pe.transpose(bank[6][:, a * P:(a + 1) * P], probs[:, u % 4, a * P:(a + 1) * P], ident[:, :])
                mm.then_inc(sem["pt_ready"], 1)

            def values(name, i, v, d):
                t = plan.pt0[name] + i
                pe.wait_ge(sem["pt_taken"], t + 1)
                if t >= 1:
                    pe.wait_ge(sem["o_taken"], t)
                r = (t % 2) * 256
                pT = probsT[:, t % 2, :]
                pe.matmul(bank[7][:, r:r + d], pT[:, 0:P], v(0), start=True, stop=True)
                pe.matmul(bank[7][:, r + d:r + 2 * d], pT[:, P:2 * P], v(0), start=True, stop=False)
                pe.matmul(bank[7][:, r + d:r + 2 * d], pT[:, 2 * P:384], v(1), start=False, stop=True)\
                    .then_inc(sem["o_ready"], 1)

            def attention(name, heads, q, kk, v, d=64, comps=1):
                u0 = plan.unit0[name]
                for i in range(heads + 2):
                    if i < heads:
                        for c in range(comps):
                            scores(name, comps * i + c, q(i, c), kk(i, c))
                    one, two = beside_parts(name, i)
                    for q_ in one:
                        run_part(q_)
                    if 1 <= i <= heads:
                        turn_probs(name, i - 1, u0 + comps * (i - 1))
                    for q_ in two:
                        run_part(q_)
                    if i >= 2:
                        values(name, i - 2, v(i - 2), d)

            pe.wait_ge(sem["const_ready"], 1)
            pe.wait_ge(sem["rows_in"], 16 * 14)
            pe.transpose(bank[4][:, 0:107], vec_rows[:, :], ident[0:107, 0:107])
            pe.transpose(bank[4][:, 128:192], vec_rows2[:, :], ident[0:64, 0:64]).then_inc(sem["work_ready"], 1)
            for n in range(4):
                reduce_piece(n)

            def norm_turn(i):
                turn(NORM_X[i], lambda k, m: scrA[:, m, k * P:(k + 1) * P], DT, ready="xs_ready%d" % i)

            norm_turn(0)
            pe.wait_ge(sem["x_split"], 4)
            run_stage("lat")
            run_stage("q_mb")
            run_stage("k_mb")
            run_stage("v_mb")
            pe.wait_ge(sem["lat_normed"], 1)
            turn("latT", lambda k, m: lat[:, m, k * P:(k + 1) * P], 3)
            turned(pe, "latT")
            run_stage("uq")
            run_stage("ukv")
            for a, name in enumerate(("mbqT", "mbkT")):
                pe.wait_ge(sem["mb_roped"], a + 1)
                turn(name, lambda k, m: qk_mb[:, a, m, k * P:(k + 1) * P], 4)
            turned(pe, "mbkT")

            def half(buf, h):
                lo = 64 * (h % 2)
                return buf[lo:lo + 64, h // 2, :]

            attention("mb", 8, lambda h, c: half(qT_mb, h), lambda h, c: half(kT_mb, h),
                      lambda h: (lambda a: v_mb[:, a, h, :]))
            pe.wait_ge(sem["mla_roped"], 1)
            turn("mlaT", lambda k, m: (q_up, k_up)[k // 8][:, m, 96 * (k % 8):96 * (k % 8) + 96], 16)
            turned(pe, "mlaT")
            attention("mla", 8, lambda h, c: qT_mla[0:96, h, :], lambda h, c: kT_mla[0:96, h, :],
                      lambda h: (lambda a: v_mla[:, a, h, :]))
            for a in range(2):
                pe.wait_ge(sem["u_ready"], a + 1)
                for i in range(2):
                    w = works["uT"] + 2 * a + i
                    b = work_bank(w)
                    for k in range(2):
                        for m in range(M):
                            mm = pe.transpose(b[:, k * S + m * P:k * S + (m + 1) * P],
                                              o_blk[:, a, m, (2 * i + k) * P:(2 * i + k + 1) * P], ident[:, :])
                    mm.then_inc(sem["work_ready"], 1)
            turned(pe, "uT")
            run_stage("w_o_mla")
            run_stage("w_o_moba")
            pe.wait_ge(sem["y_ready"], 4)
            turn("yT", lambda k, m: y_rows[:, m, k * P:(k + 1) * P], DT)
            turned(pe, "yT")
            run_stage("w_out")

            norm_turn(1)
            pe.wait_ge(sem["x_split"], 8)
            run_stage("nsa_in")
            for a in range(2):
                pe.wait_ge(sem["kv_doubled"], 1)
                for i in range(2):
                    w = works["cmpin"] + 2 * a + i
                    b = work_bank(w)
                    for g in range(2):
                        for m in range(M):
                            mm = pe.transpose(b[:, g * S + m * P:g * S + (m + 1) * P],
                                              kv_dup[:, m, a, 2 * i + g].rearrange("p c d -> p (c d)"), ident[:, :])
                    mm.then_inc(sem["work_ready"], 1)
            for a in range(2):
                pe.wait_ge(sem["turned_dve"], plan.work_free[works["cmpin"] + 2 * a + 1][1])
                c = plan.cmp_chunk[a]
                pe.wait_ge(sem["chunk_in%d" % (c % RING)], 16 * (c // RING + 1))
                w1 = slot(c)
                w = works["hid"] + a
                b = work_bank(w)
                for t in range(16):
                    h, i0 = t // 8, t // 8
                    mm = pe.matmul(b[:, 0:60], w1[:, t, :], z_blk[:, a, h, :, i0:i0 + 15, t % 8],
                                   start=t == 0, stop=t == 15)
                mm.then_inc(sem["work_ready"], 1)
            pe.wait_ge(sem["turned_dve"], plan.work_free[works["hid"]][1])
            pe.wait_ge(sem["w_c2_in"], 32)
            b = work_bank(works["kv_cmp"])
            pe.matmul(b[0:60, 0:64], hid[:, 0, :], w_c2[:, 0, :], start=True, stop=True).then_inc(sem["work_ready"], 1)
            pe.wait_ge(sem["hid_ready"], 1)
            b = work_bank(works["kv_cmp"] + 1)
            for f in range(2):
                mm = pe.matmul(b[0:120, f * 64:(f + 1) * 64], hid_rep[:, f].rearrange("p g r c -> p (g r c)"),
                               w_c2[:, 1, :], start=True, stop=True)
            mm.then_inc(sem["work_ready"], 1)
            pe.wait_ge(sem["k_cmp_ready"], 1)
            b = work_bank(works["kcT"])
            pe.transpose(b[:, 0:60], k_cmp2[0:60].rearrange("p a d -> p (a d)"), ident[0:60, 0:60])\
                .then_inc(sem["work_ready"], 1)
            pe.wait_ge(sem["q_normed"], 1)
            turn("qcT", lambda k, m: nsa[:, m, k * P:(k + 1) * P], 8)
            turned(pe, "kcT")
            turned(pe, "qcT")
            for m in range(M):
                for odd in range(2):
                    b = work_bank(works["cmpS"] + 2 * m + odd)
                    lo = 64 * odd
                    for h in range(8):
                        mm = pe.matmul(b[:, 15 * h:15 * h + 15], qcT[lo:lo + 64, h, m * P:(m + 1) * P],
                                       kcT[lo:lo + 64, 15 * (h // 2):15 * (h // 2) + 15], start=True, stop=True)
                    mm.then_inc(sem["work_ready"], 1)
            for m in range(M):
                pe.wait_ge(sem["pc_ready"], m + 1)
                b = work_bank(works["cmpT"] + m)
                for f in range(2):
                    mm = pe.transpose(b[0:120, f * P:(f + 1) * P], pc[:, m, 120 * f:120 * (f + 1)], ident[:, :])
                mm.then_inc(sem["work_ready"], 1)
            for m in range(M):
                pe.wait_ge(sem["turned_act"], plan.work_free[works["cmpT"] + m][1])
                pe.wait_ge(sem["turned_dve"], plan.work_free[works["kv_cmp"] + 1][1])
                for f in range(2):
                    b = work_bank(works["cmpO"] + 2 * m + f)
                    pe.matmul(b[:, :], pcT[0:120, m, f, :], blockV[0:120, f].rearrange("p h d -> p (h d)"),
                              start=True, stop=True).then_inc(sem["work_ready"], 1)
            pe.wait_ge(sem["q_roped"], 1)
            turn("qrT", lambda k, m: q_rot[:, m, k * P:(k + 1) * P], 8)
            pe.wait_ge(sem["k_doubled"], 1)
            turn("kT", lambda k, m: k_dup[:, m, k // 4, k % 4].rearrange("p c d -> p (c d)"), 8)
            turned(pe, "kT")
            for name, kT, v0 in (("sel", kselT, 1792), ("win", kwinT, 2304)):
                attention(name, 16, lambda h, c: half(qrT, h),
                          lambda h, c: kT[64 * (h % 2):64 * (h % 2) + 64, h // 4, :],
                          lambda h: (lambda a: nsa[:, a, v0 + 64 * (h // 4):v0 + 64 * (h // 4) + 64]))
            pe.wait_ge(sem["o_rows_done"], 1)
            turn("o1T", lambda k, m: scrA[:, m, k * P:(k + 1) * P], DT)
            turned(pe, "o1T")
            run_stage("nsa_out")

            def mlp(layer, norm):
                norm_turn(norm)
                pe.wait_ge(sem["x_split"], 4 * (norm + 1))
                run_stage("mlp_in%d" % layer)
                pe.wait_ge(sem["hidden"], 16 * (layer + 1))
                run_stage("mlp_out%d" % layer)

            mlp(0, 2)
            norm_turn(3)
            pe.wait_ge(sem["x_split"], 16)
            run_stage("diff_in")
            for a, name in enumerate(("dqT", "dkT")):
                pe.wait_ge(sem["dqk_roped"], a + 1)
                turn(name, lambda k, m: dif[:, m, a * D + k * P:a * D + (k + 1) * P], 8)
            turned(pe, "dkT")
            attention("diff", 8, lambda h, c: dqT[64 * c:64 * c + 64, h, :], lambda h, c: dkT[64 * c:64 * c + 64, h, :],
                      lambda h: (lambda a: dif[:, a, 2048 + h * P:2048 + (h + 1) * P]), d=P, comps=2)
            pe.wait_ge(sem["d_rows_done"], 2)
            turn("o2T", lambda k, m: scrA[:, m, k * P:(k + 1) * P], DT)
            turned(pe, "o2T")
            run_stage("diff_out")
            mlp(1, 4)

        SS = {"x0": 0, "lat": 2, "y": 6, "x1": 8, "nsa": 10, "kc": 58, "x2": 59, "x3": 61, "diff": 63,
              "sub": 127, "x4": 143}

        @block.scalar
        def _(act_e):
            e = act_e
            e.wait_ge(sem["turned_dve"], 1)
            e.activation(stat[:, 0:16], cols[:, 0:16], ACT.Sigmoid).then_inc(sem["sig_c"], 1)

            def turn_out(stage, i, put):
                w = works[stage] + i
                if w % 2 == 0:
                    e.wait_ge(sem["work_ready"], w + 1)
                    put(i, bank[4 + w % 2]).then_inc(sem["turned_act"], 1)

            def plain(dst, rows=P):
                def put(i, b):
                    return e.activation(dst[0:rows, 2 * i:2 * i + 2, :].rearrange("p a s -> p (a s)"),
                                        b[0:rows, :], ACT.Copy)
                return put

            def high_out(stage, i, dst, scale=1.0):
                w = works[stage] + i
                e.wait_ge(sem["work_ready"], w + 1)
                n = len(dst)
                b = bank[4 + w % 2]
                for k, d in enumerate(dst):
                    s_ = scale if isinstance(scale, float) else scale[:, k:k + 1]
                    wd = 512 // n if n > 1 or d.shape[-1] == 512 else S
                    ins = e.activation(d, b[:, k * wd:(k + 1) * wd], ACT.Copy, scale=s_)
                ins.then_inc(sem["turned_high"], 1)

            def high_tiles(stage):
                for i in range(4):
                    high_out(stage, i, [hT[0][:, 2 * i:2 * i + 2, :].rearrange("p a s -> p (a s)")])

            def split_high(q):
                if q >= len(plan.parts):
                    return
                c = plan.parts[q][0]
                e.wait_ge(sem["chunk_in%d" % (c % RING)], 16 * (c // RING + 1))
                if q >= PARTS:
                    e.wait_ge(sem["part_done"], q - PARTS + 1)
                src, n = part_words(q)
                e.activation(high[:, q % PARTS, 0:n], src, ACT.Copy).then_inc(sem["high_ready"], 1)

            def follow(q):
                p = pair_of[q]
                if q == plan.last_part[p]:
                    take_job(2 * p)
                    take_job(2 * p + 1)
                split_high(q + PARTS)

            def follow_stage(stage):
                for q in stage_parts(stage):
                    follow(q)

            def norm_stage(i, ready):
                for m in range(M):
                    e.wait_ge(sem[ready], (16 if ready == "x_in" else m + 1))
                    c = SS["x%d" % i] + m
                    e.activation(scrA[:, m, :], x[:, m, :], ACT.Square, accum_out=ss[:, c:c + 1])\
                        .then_inc(sem["ss_x%d" % i], 1)
                if i == 0:
                    for q in range(PARTS):
                        split_high(q)
                e.wait_ge(sem["gs_ready"], i + 1)
                for t in range(4):
                    w = works["x%d" % i] + t
                    e.wait_ge(sem["work_ready"], w + 1)
                    n = 4 * i + t
                    if n % 4 == 3:
                        e.wait_ge(sem["x_split"], n - 2)
                    for k in range(2):
                        f = 2 * t + k
                        ins = e.activation(whole[:, t % 3, k * S:(k + 1) * S], bank[4 + w % 2][:, k * S:(k + 1) * S],
                                           ACT.Identity, scale=gs[:, i, f:f + 1], bias=mod[:, i, 0, f:f + 1])
                    ins.then_inc(sem["turned_act"], 1)

            hidden = [0]

            def take_job(j):
                job = jobs[j]
                if job["by"] != "act":
                    return
                name, value = plan.job_done[j]
                e.wait_ge(sem[name], value)
                b, m, c0, stage = bank[j % 3], job["half"], job["c0"], job["stage"]
                n = job.get("n")
                if stage == "lat":
                    ins = e.activation(lat[:, m, :], b[:, 0:416], ACT.Copy)
                elif stage in ("q_mb", "k_mb"):
                    ins = e.activation(qk_mb[:, int(stage == "k_mb"), m, :], b[:, :], ACT.Copy,
                                       scale=HEAD_SCALE if stage == "q_mb" else 1.0)
                elif stage == "v_mb":
                    ins = e.activation(v_mb[:, m, :, :].rearrange("p h d -> p (h d)"), b[:, :], ACT.Copy)
                elif stage == "uq":
                    ins = e.activation(q_up[:, m, c0:c0 + n], b[:, 0:n], ACT.Copy, scale=MLA_SCALE)
                elif stage == "ukv":
                    h0 = c0 // P
                    src = b[:, :].rearrange("p (h d) -> p h d", d=P)
                    dst = k_up[:, m, :].rearrange("p (h d) -> p h d", d=96)
                    e.activation(dst[:, h0:h0 + 4, 0:64], src[:, :, 0:64], ACT.Copy)
                    ins = e.activation(v_mla[:, m, h0:h0 + 4, :], src[:, :, 64:128], ACT.Copy)
                elif stage in ("z_mla", "z_mb"):
                    ins = e.activation(z[stage][:, m, :], b[:, :], ACT.Copy)
                elif stage == "w_out":
                    ins = e.activation(scrA[:, m, c0:c0 + n], b[:, 0:n], ACT.Copy)
                elif stage == "nsa_in":
                    ins = e.activation(nsa[:, m, c0:c0 + n], b[:, 0:n], ACT.Copy)
                elif stage == "diff_in":
                    ins = e.activation(dif[:, m, c0:c0 + n], b[:, 0:n], ACT.Copy)
                else:
                    h, f = hidden[0], c0 // P + 2 * m
                    hidden[0] += 1
                    if h >= 3:
                        e.wait_ge(sem["hidden"], h - 2)
                    e.activation(whole[:, h % 3, :], b[:, :], ACT.Relu).then_inc(sem["copied_act"], 1)
                    e.wait_ge(sem["copied_act"], plan.job_free[j][1])
                    e.activation(hidT[0][:, f:f + 2, :].rearrange("p a s -> p (a s)"), whole[:, h % 3, :], ACT.Square)\
                        .then_inc(sem["hidden_high"], 1)
                    return
                ins.then_inc(sem["copied_act"], 1)

            def exps(name, i):
                u, w = plan.unit0[name] + i, works[name] + i
                e.wait_ge(sem["neg_max"], u + 1)
                if u >= 4:
                    e.wait_ge(sem["pt_ready"], plan.pt_of_unit[u - 4] + 1)
                b = bank[4 + w % 2]
                e.activation(probs[:, u % 4, 0:P], b[:, 0:P], ACT.Exp, bias=neg_max[:, 2 * (u % 8):2 * (u % 8) + 1],
                             accum_out=sums[:, 2 * (u % 8):2 * (u % 8) + 1])
                e.activation(probs[:, u % 4, P:384], b[:, P:384], ACT.Exp, bias=neg_max[:, 2 * (u % 8) + 1:2 * (u % 8) + 2],
                             accum_out=sums[:, 2 * (u % 8) + 1:2 * (u % 8) + 2]).then_inc(sem["probs_ready"], 1)

            def attention(name, heads, comps=1):
                for i in range(heads + 2):
                    if i < heads:
                        for c in range(comps):
                            exps(name, comps * i + c)
                    one, two = beside_parts(name, i)
                    for q in one:
                        follow(q)
                    if 1 <= i <= heads:
                        t = plan.pt0[name] + i - 1
                        e.wait_ge(sem["pt_ready"], t + 1)
                        if t >= 2:
                            e.wait_ge(sem["o_ready"], t - 1)
                        e.activation(probsT[:, t % 2, :], bank[6][:, 0:384], ACT.Copy).then_inc(sem["pt_taken"], 1)
                    for q in two:
                        follow(q)

            norm_stage(0, "x_in")
            follow_stage("lat")
            e.dma_start(gate[:, 2, :], t_in["g_post"][0].partition_broadcast(P)).then_inc(sem["g_post_in"], 16)
            e.dma_start(gate[:, 0, :], t_in["b_ada"][0, 2048:3072].partition_broadcast(P)).then_inc(sem["gate_in0"], 16)
            copied(e, "lat")
            for m in range(M):
                c = SS["lat"] + m
                e.activation(scrA[:, 0, 512 * m:512 * m + 256], lat[:, m, 0:256], ACT.Square, accum_out=ss[:, c:c + 1])\
                    .then_inc(sem["ss_lat"], 1)
                e.activation(scrA[:, 0, 512 * m + 256:512 * m + 384], lat[:, m, 256:384], ACT.Square, accum_out=ss[:, c + 2:c + 3])\
                    .then_inc(sem["ss_lat"], 1)
            follow_stage("q_mb")
            e.wait_ge(sem["angles"], 1)
            e.activation(cs[:, :, :, :], trig[:, :, :, :], ACT.Sin).then_inc(sem["cos_sin"], 1)
            e.wait_ge(sem["lam_sums"], 1)
            e.activation(lam[:, 2:4], lam[:, 0:2], ACT.Exp).then_inc(sem["lam_exp"], 1)
            follow_stage("k_mb")
            e.dma_start(b_merge[:, :], t_in["b_merge"][0].partition_broadcast(P)).then_inc(sem["b_merge_in"], 16)
            follow_stage("v_mb")
            e.dma_start(gate[:, 1, :], t_in["b_ada_2"][0, 2048:3072].partition_broadcast(P)).then_inc(sem["gate_in1"], 16)
            for a, name in enumerate(("nsa_w_ck2_2", "nsa_w_cv2_2")):
                e.dma_start(w_c2[:, a, :], t_in[name][0]).then_inc(sem["w_c2_in"], 16)

            high_out("latT", 0, [latT[0][:, k, :] for k in range(2)], cols[:, C_GQ:C_GQ + 2])
            high_out("latT", 1, [latT[0][:, 2, :]], cols[:, C_GKV:C_GKV + 1])
            follow_stage("uq")
            follow_stage("ukv")
            for name, dst in (("mbqT", qT_mb), ("mbkT", kT_mb)):
                for i in range(2):
                    turn_out(name, i, plain(dst))
            attention("mb", 8)
            for i in range(8):
                turn_out("mlaT", i, plain(qk[:, 8:24, :], 96))
            attention("mla", 8)
            copied(e, "merge")
            e.wait_ge(sem["o_ready"], plan.pt0["sel"])
            e.activation(scrA[:, :, :].rearrange("p m n -> p (m n)"), act[:, 832:2880], ACT.Sigmoid)\
                .then_inc(sem["z_sig"], 1)
            e.activation(merge[:, :, :].rearrange("p m n -> p (m n)"), merge[:, :, :].rearrange("p m n -> p (m n)"),
                         ACT.Sigmoid).then_inc(sem["merge_sig"], 1)
            high_tiles("uT")
            follow_stage("w_o_mla")
            follow_stage("w_o_moba")
            high_tiles("yT")
            follow_stage("w_out")
            copied(e, "w_out")
            for m in range(M):
                c = SS["y"] + m
                e.activation(scrB[:, m * D:(m + 1) * D], scrA[:, m, :], ACT.Square, accum_out=ss[:, c:c + 1])\
                    .then_inc(sem["ss_y"], 1)

            norm_stage(1, "x_done0")
            follow_stage("nsa_in")
            copied(e, "nsa_in")
            for m in range(M):
                e.activation(scrA[:, m, :], nsa[:, m, 0:D], ACT.Square).then_inc(sem["nsa_sq"], 1)
                src = nsa[:, m, 1536:2560].rearrange("p (a n) -> p a n", a=2)[:, :, 0:256]
                e.activation(act[:, 7264 + 512 * m:7776 + 512 * m].rearrange("p (a n) -> p a n", a=2), src,
                             ACT.Square).then_inc(sem["nsa_sq"], 1)
            e.wait_ge(sem["gl_biased"], 2)
            e.activation(nsa[:, :, 2560:2608], nsa[:, :, 2560:2608], ACT.Sigmoid).then_inc(sem["gl_ready"], 1)
            for a in range(2):
                e.wait_ge(sem["work_ready"], works["hid"] + a + 1)
                if a:
                    e.wait_ge(sem["turned_dve"], plan.work_free[works["hid"]][1])
                e.activation(stat[:, 64:124], bank[4 + (works["hid"] + a) % 2][:, 0:60], ACT.Sigmoid)\
                    .then_inc(sem["hid_sig"], 1)
            for i in range(4):
                turn_out("qcT", i, plain(qcT))
            for m in range(M):
                e.wait_ge(sem["pc_shifted"], m + 1)
                e.activation(pc[:, m, :], pc[:, m, :], ACT.Exp).then_inc(sem["pc_exp"], 1)
            for m in range(M):
                w = works["cmpT"] + m
                e.wait_ge(sem["work_ready"], w + 1)
                e.activation(pcT[0:120, m].rearrange("p f q -> p (f q)"), bank[4 + w % 2][0:120, 0:256], ACT.Copy)\
                    .then_inc(sem["turned_act"], 1)
            for i in range(4):
                turn_out("qrT", i, plain(qrT))
            for i in range(4):
                turn_out("kT", i, plain(qk[:, 16:24, :]))
            attention("sel", 16)
            attention("win", 16)
            high_tiles("o1T")
            follow_stage("nsa_out")
            norm_stage(2, "x_done1")
            follow_stage("mlp_in0")
            follow_stage("mlp_out0")
            norm_stage(3, "x_done2")
            follow_stage("diff_in")
            copied(e, "diff_in")
            for m in range(M):
                e.activation(scrA[:, m, :], dif[:, m, 0:D], ACT.Square).then_inc(sem["diff_sq"], 1)
                e.activation(scrB[:, m * D:(m + 1) * D], dif[:, m, D:2 * D], ACT.Square).then_inc(sem["diff_sq"], 1)
            for name, dst in (("dqT", dqT), ("dkT", dkT)):
                for i in range(4):
                    turn_out(name, i, plain(dst))
            attention("diff", 8, comps=2)
            e.wait_ge(sem["o_taken"], plan.n_pt)
            for m in range(M):
                e.activation(scrB[:, m * D:(m + 1) * D], scrA[:, m, :], ACT.Square).then_inc(sem["sub_sq"], 1)
            high_tiles("o2T")
            follow_stage("diff_out")
            norm_stage(4, "x_done3")
            follow_stage("mlp_in1")
            follow_stage("mlp_out1")

        @block.gpsimd
        def _(pool):
            e = pool
            chain = Chain(e, "pool_chain")
            chain(e.memset(ident[:, :], 0.0))
            chain(e.affine_select(out=ident[:, :], in_=ident[:, :], compare_op=ALU.not_equal, fill=1.0, base=0,
                                  pattern=[[-1, P]], channel_multiplier=1))
            e.memset(ones[:, :], 1.0).then_inc(sem["const_ready"], 1)
            chain(e.memset(half_neg[:, :], -0.5))
            chain(e.memset(causal[:, :], 0.0))
            chain(e.affine_select(out=causal[:, :], in_=causal[:, :], compare_op=ALU.is_ge, fill=NEG, base=0,
                                  pattern=[[-1, P]], channel_multiplier=1))
            for buf, inside, outside in ((cmp_neg, 0.0, NEG), (cmp_keep, 1.0, 0.0)):
                chain(e.memset(buf[:, :, :], inside))
                chain(e.affine_select(out=buf[:, :, :], in_=buf[:, :, :], compare_op=ALU.is_ge, fill=outside,
                                      base=-31, pattern=[[P, M], [-16, 15]], channel_multiplier=1))
            chain(e.memset(own[:, :], 1.0))
            chain(e.affine_select(out=own[:, :], in_=own[:, :], compare_op=ALU.is_ge, fill=0.0, base=0,
                                  pattern=[[-15, 8]], channel_multiplier=1))
            chain(e.affine_select(out=own[:, :], in_=own[:, :], compare_op=ALU.is_ge, fill=0.0, base=14,
                                  pattern=[[15, 8]], channel_multiplier=-1))
            e.memset(stat[:, 127:128], 0.0).then_inc(sem["masks_ready"], 1)
            def split_low(q):
                if q < len(plan.parts) and plan.low_by[q] == "pool":
                    e.wait_ge(sem["high_ready"], q + 1)
                    src, n = part_words(q)
                    e.tensor_tensor(low[:, q % PARTS, 0:n], src, high[:, q % PARTS, 0:n].bitcast(F32), ALU.subtract)\
                        .then_inc(sem["low_ready_pool"], 1)

            def follow_stage(*stages):
                for q in range(len(plan.parts)):
                    if jobs[2 * pair_of[q]]["stage"] in stages:
                        split_low(q + PARTS)

            def root(name, groups, count, p=P):
                e.wait_ge(sem["ss_" + name], count)
                for c, n, elements in groups:
                    chain(e.tensor_scalar(rstd[0:p, c:c + n], ss[0:p, c:c + n], 1.0 / elements, EPS, ALU.mult, ALU.add))
                for g, (c, n, _) in enumerate(groups):
                    e.tensor_tensor(rstd[0:p, c:c + n], rstd[0:p, c:c + n], half_neg[0:p, 0:n], ALU.pow)\
                        .then_inc(sem["rs_" + name], 1)

            root("x0", [(SS["x0"], 2, D)], 2)
            for o, name in enumerate(("positions", "positions_2")):
                e.dma_start(pos_i[:, o, :], t_in[name][0].rearrange("(m p) -> p m", p=P),
                            allow_slow_non_contiguous=True).then_inc(sem["tiny_in"], 16)
            for dst, src in ((q_gain, t_in["nsa_q_gain_2"][0]), (tiny[:, 64:256], t_in["nsa_k_gain_2"].rearrange("l a d -> (l a d)")),
                             (dq_gain, t_in["diff_q_gain_2"][0]), (dk_gain, t_in["diff_k_gain_2"][0]),
                             (sub_gain, t_in["diff_subln_g_2"][0]), (b_gate, t_in["nsa_b_gate_2"][0]),
                             (lqk[:, 0, :], t_in["diff_lq1_2"][0]), (lqk[:, 1, :], t_in["diff_lk1_2"][0]),
                             (lqk[:, 2, :], t_in["diff_lq2_2"][0]), (lqk[:, 3, :], t_in["diff_lk2_2"][0]),
                             (inv_freq, t_in["inv_freq"])):
                e.dma_start(dst, src.partition_broadcast(P)).then_inc(sem["tiny_in"], 16)

            for q in range(PARTS):
                split_low(q)
            follow_stage("lat")
            root("lat", [(SS["lat"], 2, 256), (SS["lat"] + 2, 2, 128)], 4)
            follow_stage("q_mb", "k_mb", "v_mb", "uq", "ukv", "z_mla", "z_mb", "merge")
            e.wait_ge(sem["gg_ready"], 1)
            e.dma_start(gate[:, 2, :], t_in["b_ada_2"][0, 5120:6144].partition_broadcast(P)).then_inc(sem["gate_in2"], 16)
            follow_stage("w_o_mla", "w_o_moba", "w_out")
            root("y", [(SS["y"], 2, D)], 2)
            e.wait_ge(sem["x_done0"], 2)
            e.dma_start(gate[:, 0, :], t_in["b_ada_2"][1, 2048:3072].partition_broadcast(P)).then_inc(sem["gate_in3"], 16)
            root("x1", [(SS["x1"], 2, D)], 2)
            follow_stage("nsa_in")
            root("nsa", [(SS["nsa"], 48, 64)], 4)
            root("kc", [(SS["kc"], 1, 64)], 1, 60)
            follow_stage("nsa_out")
            e.wait_ge(sem["x_done1"], 2)
            e.dma_start(gate[:, 1, :], t_in["b_ada_2"][1, 5120:6144].partition_broadcast(P)).then_inc(sem["gate_in4"], 16)

            def square_hidden(layer):
                for i in range(16 * layer, 16 * layer + 16):
                    f = 2 * (i % 16)
                    e.wait_ge(sem["hidden_high"], i + 1)
                    v = whole[:, i % 3, :]
                    chain(e.tensor_tensor(v, v, v, ALU.mult))
                    e.tensor_tensor(hidT[1][:, f:f + 2, :].rearrange("p a s -> p (a s)"), v,
                                    hidT[0][:, f:f + 2, :].bitcast(F32).rearrange("p a s -> p (a s)"), ALU.subtract)\
                        .then_inc(sem["hidden"], 1)

            root("x2", [(SS["x2"], 2, D)], 2)
            square_hidden(0)
            follow_stage("mlp_in0", "mlp_out0")
            root("x3", [(SS["x3"], 2, D)], 2)
            follow_stage("diff_in")
            root("diff", [(SS["diff"], 64, 64)], 4)
            root("sub", [(SS["sub"], 16, P)], 2)
            follow_stage("diff_out")
            root("x4", [(SS["x4"], 2, D)], 2)
            square_hidden(1)
            follow_stage("mlp_in1", "mlp_out1")

        @block.vector
        def _(dve):
            e = dve
            chain = Chain(e, "dve_chain")
            flat = lambda ap: ap

            e.wait_ge(sem["work_ready"], 1)
            e.tensor_copy(cols[:, 0:107], bank[4][:, 0:107])
            e.tensor_copy(cols[:, 128:192], bank[4][:, 128:192]).then_inc(sem["turned_dve"], 1)
            e.wait_ge(sem["turned_dve"], 1)
            e.wait_ge(sem["sig_c"], 1)
            chain(e.tensor_tensor(silu_c[:, :], stat[:, 0:16], cols[:, 0:16], ALU.mult))

            def half_piece(h):
                n, c = h // 2, (0 if h < 12 else 8)
                name, value = ada_arrived(h)
                e.wait_ge(sem[name], value)
                for i in range(4):
                    k = 4 * (h % 2) + i
                    w = ada_slot(h)[:, i, :]
                    s_ = silu_c[:, c + k:c + k + 1]
                    if k == 0:
                        if n >= 2:
                            e.wait_ge(sem["piece_summed"], n - 1)
                        ins = e.tensor_scalar(acc[:, n % 2, :], w, s_, None, ALU.mult)
                    else:
                        ins = e.scalar_tensor_tensor(out=acc[:, n % 2, :], in0=w, scalar=s_, in1=acc[:, n % 2, :],
                                                     op0=ALU.mult, op1=ALU.add)
                    if i < 3:
                        chain(ins)
                ins.then_inc(sem["ada_used"], 1)
                e.wait_ge(sem["ada_used"], h + 1)

            def piece_end(n):
                e.wait_ge(sem["piece_summed"], n + 1)
                use = piece_use(n)
                if use[0] == "col":
                    _, norm, part, c0, b0 = use
                    e.tensor_tensor(mod[:, norm, part, c0:c0 + 4], bank[3][:, 0:4], cols[:, b0:b0 + 4], ALU.add)\
                        .then_inc(sem["mod_taken"], 1)
                else:
                    g = 0 if n < 6 else 1 + (n - 6) // 12 * 2 + ((n - 6) % 12) // 6
                    e.wait_ge(sem["gate_in%d" % g], 16)
                    dst = gate[:, use[1], use[2]:use[2] + 512]
                    e.tensor_tensor(dst, bank[3][:, :], dst, ALU.add).then_inc(sem["mod_taken"], 1)
                if n == 5:
                    e.wait_ge(sem["mod_taken"], 6)
                    e.wait_ge(sem["g_post_in"], 16)
                    e.tensor_tensor(gate[:, 0, :], gate[:, 0, :], gate[:, 2, :], ALU.mult).then_inc(sem["gg_ready"], 1)

            def turn_out(stage, i, put):
                w = works[stage] + i
                if w % 2 == 1:
                    e.wait_ge(sem["work_ready"], w + 1)
                    put(i, bank[5]).then_inc(sem["turned_dve"], 1)

            def plain(dst, rows=P):
                def put(i, b):
                    return e.tensor_copy(dst[0:rows, 2 * i:2 * i + 2, :].rearrange("p a s -> p (a s)"), b[0:rows, :])
                return put

            GAIN = [C_PRE, C_MIX, C_MLP, C_MIX + 8, C_MLP + 8]
            LAST_PIECE = [4, 10, 16, 22, 28]

            def scale_rows(i):
                e.wait_ge(sem["rs_x%d" % i], 1)
                for m in range(M):
                    c = SS["x%d" % i] + m
                    e.tensor_scalar(scrA[:, m, :], x[:, m, :], rstd[:, c:c + 1], None, ALU.mult)\
                        .then_inc(sem["xs_ready%d" % i], 1)

            def norm_stage(i):
                e.wait_ge(sem["mod_taken"], LAST_PIECE[i])
                e.scalar_tensor_tensor(out=gs[:, i, :], in0=mod[:, i, 1, :], scalar=1.0,
                                       in1=cols[:, GAIN[i]:GAIN[i] + 8], op0=ALU.add, op1=ALU.mult)\
                    .then_inc(sem["gs_ready"], 1)
                if i:
                    scale_rows(i)
                if i == 0:
                    for q in range(PARTS):
                        split_low(q)
                for t in range(4):
                    w = works["x%d" % i] + t
                    e.wait_ge(sem["turned_act"], plan.work_free[w][1])
                    hi = hT[0][:, 2 * t:2 * t + 2, :].rearrange("p a s -> p (a s)")
                    chain(e.tensor_copy(hi, whole[:, t % 3, :]))
                    e.tensor_tensor(hT[1][:, 2 * t:2 * t + 2, :].rearrange("p a s -> p (a s)"), whole[:, t % 3, :],
                                    hT[0][:, 2 * t:2 * t + 2, :].bitcast(F32).rearrange("p a s -> p (a s)"),
                                    ALU.subtract).then_inc(sem["x_split"], 1)

            turned_low = [0]

            def low_out(stage, i, lows, highs, scale=None):
                w = works[stage] + i
                turned_low[0] += 1
                e.wait_ge(sem["turned_high"], turned_low[0])
                b = bank[4 + w % 2]
                for k, (lo, hi) in enumerate(zip(lows, highs)):
                    n = 512 if scale is None else S
                    src = b[:, k * n:(k + 1) * n]
                    if scale is None:
                        ins = e.tensor_tensor(lo, src, hi, ALU.subtract)
                    else:
                        ins = e.scalar_tensor_tensor(out=lo, in0=src, scalar=scale[:, k:k + 1], in1=hi, op0=ALU.mult,
                                                     op1=ALU.subtract)
                ins.then_inc(sem["turned_dve"], 1)

            def low_tiles(stage):
                for i in range(4):
                    flat2 = "p a s -> p (a s)"
                    low_out(stage, i, [hT[1][:, 2 * i:2 * i + 2, :].rearrange(flat2)],
                            [hT[0][:, 2 * i:2 * i + 2, :].bitcast(F32).rearrange(flat2)])

            def split_low(q):
                if q >= len(plan.parts) or plan.low_by[q] != "dve":
                    return
                e.wait_ge(sem["high_ready"], q + 1)
                src, n = part_words(q)
                e.tensor_tensor(low[:, q % PARTS, 0:n], src, high[:, q % PARTS, 0:n].bitcast(F32), ALU.subtract)\
                    .then_inc(sem["low_ready_dve"], 1)

            def follow(q):
                p = pair_of[q]
                if q == plan.last_part[p]:
                    take_job(2 * p)
                    take_job(2 * p + 1)
                split_low(q + PARTS)
                for h, at in plan.half_after.items():
                    if at == q:
                        half_piece(h)
                for n in plan.piece_sum.get(q, []):
                    piece_end(n)

            def follow_stage(stage):
                for q in stage_parts(stage):
                    follow(q)

            def rope(x1, x2, c, s, o1, o2, tmp):
                e.tensor_tensor(tmp[0], x1, c, ALU.mult)
                e.tensor_tensor(tmp[1], x2, s, ALU.mult)
                e.tensor_tensor(tmp[2], x2, c, ALU.mult)
                chain(e.tensor_tensor(tmp[3], x1, s, ALU.mult))
                e.tensor_tensor(o1, tmp[0], tmp[1], ALU.subtract)
                return e.tensor_tensor(o2, tmp[2], tmp[3], ALU.add)

            def angles(kind, a, b, heads):
                return cs[:, :, kind, a:b].unsqueeze(2).to_broadcast([P, M, heads, b - a])

            def take_job(j):
                job = jobs[j]
                if job["by"] == "dve":
                    b, m, c0, stage = bank[j % 3], job["half"], job["c0"], job["stage"]
                    name, value = plan.job_done[j]
                    e.wait_ge(sem[name], value)
                    t = scrB[:, D + (j % 2) * 512:D + (j % 2) * 512 + 512]
                    if stage == "merge":
                        e.wait_ge(sem["b_merge_in"], 16)
                        e.tensor_tensor(merge[:, m, c0:c0 + 512], b[:, :], b_merge[:, c0:c0 + 512], ALU.add)\
                            .then_inc(sem["copied_dve"], 1)
                    elif stage == "w_o_mla":
                        e.wait_ge(sem["merge_sig"], 1)
                        e.tensor_tensor(y_rows[:, m, c0:c0 + 512], b[:, :], merge[:, m, c0:c0 + 512], ALU.mult)\
                            .then_inc(sem["copied_dve"], 1)
                    elif stage == "w_o_moba":
                        e.tensor_tensor(t, b[:, :], merge[:, m, D + c0:D + c0 + 512], ALU.mult)\
                            .then_inc(sem["copied_dve"], 1)
                        e.wait_ge(sem["copied_dve"], plan.job_free[j][1])
                        y = y_rows[:, m, c0:c0 + 512]
                        e.tensor_tensor(y, y, t, ALU.add).then_inc(sem["y_ready"], 1)
                    else:
                        k = {"nsa_out": 1, "mlp_out0": 2, "diff_out": 3, "mlp_out1": 4}[stage]
                        g = gate[:, k % 3, c0:c0 + 512]
                        e.tensor_tensor(t, b[:, :], g, ALU.mult).then_inc(sem["copied_dve"], 1)
                        e.wait_ge(sem["copied_dve"], plan.job_free[j][1])
                        r = x[:, m, c0:c0 + 512]
                        ins = e.tensor_tensor(r, r, t, ALU.add)
                        if c0 == 512:
                            ins.then_inc(sem["x_done%d" % k], 1)

            def maxima(name, i):
                u, w = plan.unit0[name] + i, works[name] + i
                b = bank[4 + w % 2]
                e.wait_ge(sem["work_ready"], w + 1)
                for lo in (0, 256):
                    ins = e.tensor_tensor(b[:, lo:lo + P], b[:, lo:lo + P], causal[:, :], ALU.add)
                chain(ins)
                e.tensor_reduce(neg_max[:, 2 * (u % 8):2 * (u % 8) + 1], b[:, 0:P], AX.X, ALU.max, negate=True)
                e.tensor_reduce(neg_max[:, 2 * (u % 8) + 1:2 * (u % 8) + 2], b[:, P:384], AX.X, ALU.max, negate=True)\
                    .then_inc(sem["neg_max"], 1)

            def outputs(name, i):
                t = plan.pt0[name] + i
                u = plan.unit0[name] + i
                r = (t % 2) * 256
                if name == "diff":
                    e.wait_ge(sem["o_ready"], t + 1)
                    o = bank[7][:, r:r + 256].rearrange("p (m d) -> p m d", m=M)
                    e.tensor_copy(scrA[:, :, i * P:(i + 1) * P], o).then_inc(sem["o_taken"], 1)
                    return
                e.wait_ge(sem["probs_ready"], u + 1)
                chain(e.reciprocal(inv[:, 2 * (u % 8):2 * (u % 8) + 2], sums[:, 2 * (u % 8):2 * (u % 8) + 2]))
                if name in ("sel", "win"):
                    g = nsa[:, :, 2560 + 3 * i + (1 if name == "sel" else 2)]
                    chain(e.tensor_tensor(inv[:, 2 * (u % 8):2 * (u % 8) + 2], inv[:, 2 * (u % 8):2 * (u % 8) + 2], g, ALU.mult))
                e.wait_ge(sem["o_ready"], t + 1)
                o = bank[7][:, r:r + P].rearrange("p (m d) -> p m d", m=M)
                w = inv[:, 2 * (u % 8):2 * (u % 8) + 2].unsqueeze(2).to_broadcast([P, M, 64])
                if name in ("mb", "mla"):
                    dst = o_blk[:, int(name == "mb"), :, 64 * i:64 * i + 64]
                    e.tensor_tensor(dst, o, w, ALU.mult).then_inc(sem["o_taken"], 1)
                else:
                    tmp = o_tmp[:, t % 2, :, :]
                    e.tensor_tensor(tmp, o, w, ALU.mult).then_inc(sem["o_taken"], 1)
                    e.wait_ge(sem["o_taken"], t + 1)
                    dst = scrA[:, :, 64 * i:64 * i + 64]
                    chain(e.tensor_tensor(dst, dst, tmp, ALU.add))

            def mix(i):
                u = plan.unit0["diff"] + 2 * i
                e.wait_ge(sem["probs_ready"], u + 2)
                chain(e.reciprocal(inv[:, 2 * (u % 8):2 * (u % 8) + 4], sums[:, 2 * (u % 8):2 * (u % 8) + 4]))
                chain(e.tensor_scalar(inv[:, 2 * (u % 8) + 2:2 * (u % 8) + 4], inv[:, 2 * (u % 8) + 2:2 * (u % 8) + 4], lam[:, 5:6], None, ALU.mult))
                for m, (a, b) in enumerate(((0, P), (P, 384))):
                    p1 = probs[:, (u + 1) % 4, a:b]
                    ins = e.tensor_scalar(p1, p1, inv[:, 2 * (u % 8) + 2 + m:2 * (u % 8) + 3 + m], None, ALU.mult)
                chain(ins)
                for m, (a, b) in enumerate(((0, P), (P, 384))):
                    p0 = probs[:, u % 4, a:b]
                    ins = e.scalar_tensor_tensor(out=p0, in0=p0, scalar=inv[:, 2 * (u % 8) + m:2 * (u % 8) + m + 1],
                                                 in1=probs[:, (u + 1) % 4, a:b], op0=ALU.mult, op1=ALU.add)
                ins.then_inc(sem["diff_mixed"], 1)

            def attention(name, heads, comps=1):
                for i in range(heads + 2):
                    if i < heads:
                        for c in range(comps):
                            maxima(name, comps * i + c)
                        if comps == 2:
                            mix(i)
                    one, two = beside_parts(name, i)
                    for q in one + two:
                        follow(q)
                    if i >= 2:
                        outputs(name, i - 2)

            e.wait_ge(sem["masks_ready"], 1)
            for n in range(4):
                half_piece(2 * n)
                half_piece(2 * n + 1)
                if n == 2:
                    scale_rows(0)
                if n:
                    piece_end(n - 1)
            piece_end(3)
            norm_stage(0)
            follow_stage("lat")
            e.wait_ge(sem["rs_lat"], 2)
            for m in range(M):
                c = SS["lat"] + m
                chain(e.tensor_scalar(lat[:, m, 0:256], lat[:, m, 0:256], rstd[:, c:c + 1], None, ALU.mult))
                ins = e.tensor_scalar(lat[:, m, 256:384], lat[:, m, 256:384], rstd[:, c + 2:c + 3], None, ALU.mult)
                if m:
                    ins.then_inc(sem["lat_normed"], 1)
                else:
                    chain(ins)
            e.wait_ge(sem["tiny_in"], 16 * 13)
            chain(e.tensor_copy(pos_f[:, :, :], pos_i[:, :, :]))
            for m in range(M):
                for o, (a, b) in enumerate(((0, 48), (48, 56))):
                    for kind in range(2):
                        chain(e.tensor_scalar(trig[:, m, kind, a:b], inv_freq[:, a:b], pos_f[:, o, m:m + 1], None, ALU.mult))
            TURN = 2 * math.pi
            C1, C2 = 6.28125, 2029 / 2 ** 20
            C3 = TURN - C1 - C2
            MAGIC = 1.5 * 2 ** 23
            turns = cs
            for kind, quarter in ((0, 0.25), (1, 0.0)):
                chain(e.tensor_scalar(turns[:, :, kind, :], trig[:, :, kind, :], 1 / TURN, quarter, ALU.mult, ALU.add))
            chain(e.tensor_scalar(turns[:, :, :, :], turns[:, :, :, :], MAGIC, None, ALU.add))
            chain(e.tensor_scalar(turns[:, :, :, :], turns[:, :, :, :], -MAGIC, None, ALU.add))
            for c in (C1, C2, C3):
                chain(e.scalar_tensor_tensor(out=trig[:, :, :, :], in0=turns[:, :, :, :], scalar=-c,
                                             in1=trig[:, :, :, :], op0=ALU.mult, op1=ALU.add))
            chain(e.tensor_scalar(trig[:, :, 0, :], trig[:, :, 0, :], math.pi / 2, None, ALU.add))
            LIMIT = 3.1415925
            e.tensor_scalar(trig[:, :, :, :], trig[:, :, :, :], LIMIT, -LIMIT, ALU.min, ALU.max)\
                .then_inc(sem["angles"], 1)
            chain(e.tensor_tensor(lam_tmp[:, :, :], lqk[:, 0:4:2, :], lqk[:, 1:4:2, :], ALU.mult))
            e.tensor_reduce(lam[:, 0:2], lam_tmp[:, :, :], AX.X, ALU.add).then_inc(sem["lam_sums"], 1)
            chain(e.tensor_scalar(q_gain, q_gain, HEAD_SCALE, None, ALU.mult))
            chain(e.tensor_scalar(dq_gain, dq_gain, HEAD_SCALE, None, ALU.mult))
            chain(e.tensor_scalar(sub_gain, sub_gain, 1.0 - LAM_INIT, None, ALU.mult))
            follow_stage("q_mb")
            follow_stage("k_mb")
            e.wait_ge(sem["cos_sin"], 1)
            e.wait_ge(sem["lam_exp"], 1)
            chain(e.tensor_tensor(lam[:, 4:5], lam[:, 2:3], lam[:, 3:4], ALU.subtract))
            chain(e.tensor_scalar(lam[:, 5:6], lam[:, 4:5], LAM_INIT, -1.0, ALU.add, ALU.mult))
            for a, stage in enumerate(("q_mb", "k_mb")):
                copied(e, stage)
                v = qk_mb[:, a].rearrange("p m (h d) -> p m h d", d=64)
                tmp = [rope_tmp[:, i, :].rearrange("p (m h d) -> p m h d", m=M, h=8) for i in range(4)]
                rope(v[:, :, :, 0:32], v[:, :, :, 32:64], angles(0, 16, 48, 8), angles(1, 16, 48, 8),
                     v[:, :, :, 0:32], v[:, :, :, 32:64], tmp).then_inc(sem["mb_roped"], 1)
                e.wait_ge(sem["mb_roped"], a + 1)
            follow_stage("v_mb")

            for i, (k0, nk, g) in enumerate(((0, 2, C_GQ), (2, 1, C_GKV))):
                low_out("latT", i, [latT[1][:, k, :] for k in range(k0, k0 + nk)],
                        [latT[0][:, k, :].bitcast(F32) for k in range(k0, k0 + nk)], cols[:, g:g + nk])
            follow_stage("uq")
            follow_stage("ukv")
            copied(e, "uq")
            tmp = [rope_tmp[:, i, 0:256].rearrange("p (m h d) -> p m h d", m=M, h=8) for i in range(4)]
            v = q_up.rearrange("p m (h d) -> p m h d", d=96)
            chain(rope(v[:, :, :, 64:80], v[:, :, :, 80:96], angles(0, 0, 16, 8), angles(1, 0, 16, 8),
                       v[:, :, :, 64:80], v[:, :, :, 80:96], tmp))
            tmp = [rope_tmp[:, i, 0:32].rearrange("p (m d) -> p m d", m=M) for i in range(4)]
            r1, r2, c_, s_ = lat[:, :, 384:400], lat[:, :, 400:416], cs[:, :, 0, 0:16], cs[:, :, 1, 0:16]
            for t_, (a_, b_) in zip(tmp, ((r1, c_), (r2, s_), (r2, c_), (r1, s_))):
                chain(e.tensor_tensor(t_, a_, b_, ALU.mult))
            wide = [t_.unsqueeze(2).to_broadcast([P, M, 8, 16]) for t_ in tmp]
            v = k_up.rearrange("p m (h d) -> p m h d", d=96)
            chain(e.tensor_tensor(v[:, :, :, 64:80], wide[0], wide[1], ALU.subtract))
            copied(e, "ukv")
            e.tensor_tensor(v[:, :, :, 80:96], wide[2], wide[3], ALU.add).then_inc(sem["mla_roped"], 1)
            for name, dst in (("mbqT", qT_mb), ("mbkT", kT_mb)):
                for i in range(2):
                    turn_out(name, i, plain(dst))
            attention("mb", 8)
            for i in range(8):
                turn_out("mlaT", i, plain(qk[:, 8:24, :], 96))
            attention("mla", 8)
            e.wait_ge(sem["z_sig"], 1)
            zz = act[:, 832:2880]
            chain(e.tensor_tensor(zz, zz, scrA[:, :, :].rearrange("p m n -> p (m n)"), ALU.mult))
            e.wait_ge(sem["o_taken"], plan.pt0["sel"])
            for a, name in enumerate(("z_mla", "z_mb")):
                o = o_blk[:, a]
                e.tensor_tensor(o, o, z[name], ALU.mult).then_inc(sem["u_ready"], 1)
            low_tiles("uT")
            follow_stage("w_o_mla")
            follow_stage("w_o_moba")
            low_tiles("yT")
            follow_stage("w_out")
            e.wait_ge(sem["rs_y"], 1)
            e.wait_ge(sem["x_in"], 16)
            for m in range(M):
                c = SS["y"] + m
                chain(e.scalar_tensor_tensor(out=scrA[:, m, :], in0=scrA[:, m, :], scalar=rstd[:, c:c + 1],
                                             in1=gate[:, 0, :], op0=ALU.mult, op1=ALU.mult))
                e.tensor_tensor(x[:, m, :], x[:, m, :], scrA[:, m, :], ALU.add).then_inc(sem["x_done0"], 1)

            norm_stage(1)
            follow_stage("nsa_in")
            copied(e, "nsa_in")
            for m in range(M):
                for c in range(2):
                    ins = e.tensor_copy(kv_dup[:, m, :, :, c, :].rearrange("p a g d -> p (a g) d"),
                                        nsa[:, m, 1024:1536].rearrange("p (b d) -> p b d", d=64))
            ins.then_inc(sem["kv_doubled"], 1)
            for m in range(M):
                gl = nsa[:, m, 2560:2608]
                e.tensor_tensor(gl, gl, b_gate, ALU.add).then_inc(sem["gl_biased"], 1)
            for m in range(M):
                e.wait_ge(sem["nsa_sq"], 2 * m + 2)
                c = SS["nsa"] + 16 * m
                e.tensor_reduce(ss[:, c:c + 16], scrA[:, m, :].rearrange("p (h d) -> p h d", d=64), AX.X, ALU.add)\
                    .then_inc(sem["ss_nsa"], 1)
                c = SS["nsa"] + 32 + 8 * m
                e.tensor_reduce(ss[:, c:c + 8], act[:, 7264 + 512 * m:7776 + 512 * m].rearrange("p (h d) -> p h d", d=64),
                                AX.X, ALU.add).then_inc(sem["ss_nsa"], 1)
            for i in range(4):
                w = works["cmpin"] + i
                a, g0 = i // 2, 2 * (i % 2)
                e.wait_ge(sem["work_ready"], w + 1)
                for half_ in range(2):
                    lo = 64 * half_
                    src = bank[4 + w % 2][lo:lo + 64, :].rearrange("p (g i t c) -> p g i t c", g=2, i=16, c=2)[:, :, :, :, half_]
                    for h in range(2):
                        for g in range(2):
                            pe0 = (C_PEK, C_PEV)[a] + 8 * h
                            pos = cols[lo:lo + 64, pe0:pe0 + 8].unsqueeze(1).to_broadcast([64, 16, 8])
                            ins = e.tensor_tensor(z_blk[lo:lo + 64, a, h, g0 + g], src[:, g], pos, ALU.add)
                ins.then_inc(sem["turned_dve"], 1)
            e.wait_ge(sem["rs_nsa"], 1)

            def scale_heads(v, c, heads, gain):
                r = rstd[:, c:c + heads].unsqueeze(2).to_broadcast([P, heads, 64])
                chain(e.tensor_tensor(v, v, r, ALU.mult))
                return e.tensor_tensor(v, v, gain.unsqueeze(1).to_broadcast([P, heads, 64]), ALU.mult)

            def hidden_cmp(a):
                w = works["hid"] + a
                e.wait_ge(sem["hid_sig"], a + 1)
                e.tensor_tensor(hid[:, a, :], bank[4 + w % 2][:, 0:60], stat[:, 64:124], ALU.mult)\
                    .then_inc(sem["turned_dve"], 1)
                e.wait_ge(sem["turned_dve"], plan.work_free[w][1])

            hidden_cmp(0)
            hidden_cmp(1)
            for f in range(2):
                src = hid[:, 1, 30 * f:30 * f + 30].rearrange("p (g c) -> p g c", g=2)
                ins = e.tensor_copy(hid_rep[:, f], src.unsqueeze(2).to_broadcast([P, 2, 4, 15]))
            ins.then_inc(sem["hid_ready"], 1)
            w = works["kv_cmp"]
            e.wait_ge(sem["work_ready"], w + 1)
            e.tensor_copy(k_cmp[0:60, :], bank[4 + w % 2][0:60, 0:64]).then_inc(sem["turned_dve"], 1)
            e.wait_ge(sem["turned_dve"], plan.work_free[w][1])
            chain(e.tensor_tensor(k_cmp2[0:60, 0, :], k_cmp[0:60, :], k_cmp[0:60, :], ALU.mult))
            c = SS["kc"]
            e.tensor_reduce(ss[0:60, c:c + 1], k_cmp2[0:60, 0, :], AX.X, ALU.add).then_inc(sem["ss_kc"], 1)
            w = works["kv_cmp"] + 1
            e.wait_ge(sem["work_ready"], w + 1)
            for f in range(2):
                src = bank[4 + w % 2][0:120, 64 * f:64 * f + 64].unsqueeze(1).to_broadcast([120, 8, 64])
                ins = e.tensor_tensor(blockV[0:120, f], src, own[:, :].unsqueeze(2).to_broadcast([120, 8, 64]), ALU.mult)
            ins.then_inc(sem["turned_dve"], 1)
            for m in range(M):
                ins = scale_heads(nsa[:, m, 0:D].rearrange("p (h d) -> p h d", d=64), SS["nsa"] + 16 * m, 16, q_gain)
                if m:
                    ins.then_inc(sem["q_normed"], 1)
                else:
                    chain(ins)
            e.wait_ge(sem["rs_kc"], 1)
            for a in range(2):
                ins = e.scalar_tensor_tensor(out=k_cmp2[0:60, a, :], in0=k_cmp[0:60, :], scalar=rstd[0:60, c:c + 1],
                                             in1=k_gain[0:60, 0, :], op0=ALU.mult, op1=ALU.mult)
            ins.then_inc(sem["k_cmp_ready"], 1)
            w = works["kcT"]
            e.wait_ge(sem["work_ready"], w + 1)
            e.tensor_copy(kcT[:, :], bank[4 + w % 2][:, 0:60]).then_inc(sem["turned_dve"], 1)
            for i in range(4):
                turn_out("qcT", i, plain(qcT))
            e.wait_ge(sem["gl_ready"], 1)
            wide_h = lambda ap, n: ap.unsqueeze(2).to_broadcast([P, 16, n])
            for m in range(M):
                p3 = pc[:, m, :].rearrange("p (h c) -> p h c", c=15)
                for odd in range(2):
                    w = works["cmpS"] + 2 * m + odd
                    e.wait_ge(sem["work_ready"], w + 1)
                    e.tensor_tensor(p3[:, odd:16:2], bank[4 + w % 2][:, 0:120].rearrange("p (h c) -> p h c", c=15),
                                    cmp_neg[:, m, :].unsqueeze(1).to_broadcast([P, 8, 15]), ALU.add)\
                        .then_inc(sem["turned_dve"], 1)
                    e.wait_ge(sem["turned_dve"], plan.work_free[w][1])
                chain(e.tensor_reduce(stat[:, 16 * m:16 * m + 16], p3, AX.X, ALU.max, negate=True))
                e.tensor_tensor(p3, p3, wide_h(stat[:, 16 * m:16 * m + 16], 15), ALU.add).then_inc(sem["pc_shifted"], 1)
            for m in range(M):
                p3 = pc[:, m, :].rearrange("p (h c) -> p h c", c=15)
                s_ = stat[:, 32 + 16 * m:48 + 16 * m]
                e.wait_ge(sem["pc_exp"], m + 1)
                chain(e.tensor_reduce(s_, p3, AX.X, ALU.add))
                e.tensor_tensor(p3, p3, cmp_keep[:, m, :].unsqueeze(1).to_broadcast([P, 16, 15]), ALU.mult)\
                    .then_inc(sem["pc_ready"], 1)
                chain(e.reciprocal(s_, s_))
                g = nsa[:, m, 2560:2608].rearrange("p (h b) -> p h b", b=3)[:, :, 0]
                chain(e.tensor_tensor(s_, s_, g, ALU.mult))
            chain(e.tensor_copy(q_rot[:, :, :], nsa[:, :, 0:D]))
            v = q_rot.rearrange("p m (h d) -> p m h d", d=64)
            tmp = [k_dup_tmp[:, i, :].rearrange("p (m h d) -> p m h d", m=M, h=16) for i in range(4)]
            rope(v[:, :, :, 0:8], v[:, :, :, 8:16], angles(0, 48, 56, 16), angles(1, 48, 56, 16),
                 v[:, :, :, 0:8], v[:, :, :, 8:16], tmp).then_inc(sem["q_roped"], 1)
            e.wait_ge(sem["q_roped"], 1)
            for b_, k0 in enumerate((1536, 2048)):
                for m in range(M):
                    v = nsa[:, m, k0:k0 + 256].rearrange("p (h d) -> p h d", d=64)
                    chain(scale_heads(v, SS["nsa"] + 32 + 8 * m + 4 * b_, 4, k_gain[:, 1 + b_, :]))
                v = nsa[:, :, k0:k0 + 256].rearrange("p m (h d) -> p m h d", d=64)
                tmp = [k_dup_tmp[:, i, 0:64].rearrange("p (m h d) -> p m h d", m=M, h=4) for i in range(4)]
                chain(rope(v[:, :, :, 0:8], v[:, :, :, 8:16], angles(0, 48, 56, 4), angles(1, 48, 56, 4),
                           v[:, :, :, 0:8], v[:, :, :, 8:16], tmp))
            for b_, k0 in enumerate((1536, 2048)):
                for m in range(M):
                    for c_ in range(2):
                        ins = e.tensor_copy(k_dup[:, m, b_, :, c_, :],
                                            nsa[:, m, k0:k0 + 256].rearrange("p (h d) -> p h d", d=64))
            ins.then_inc(sem["k_doubled"], 1)
            for m in range(M):
                for f in range(2):
                    w = works["cmpO"] + 2 * m + f
                    e.wait_ge(sem["work_ready"], w + 1)
                    s_ = stat[:, 32 + 16 * m + 8 * f:40 + 16 * m + 8 * f].unsqueeze(2).to_broadcast([P, 8, 64])
                    e.tensor_tensor(o_rows[:, m, 512 * f:512 * f + 512].rearrange("p (h d) -> p h d", d=64),
                                    bank[4 + w % 2][:, :].rearrange("p (h d) -> p h d", d=64), s_, ALU.mult)\
                        .then_inc(sem["turned_dve"], 1)
            for i in range(4):
                turn_out("qrT", i, plain(qrT))
            for i in range(4):
                turn_out("kT", i, plain(qk[:, 16:24, :]))
            attention("sel", 16)
            attention("win", 16)
            e.memset(stat[:, 126:127], 0.0).then_inc(sem["o_rows_done"], 1)
            low_tiles("o1T")
            follow_stage("nsa_out")
            norm_stage(2)
            follow_stage("mlp_in0")
            follow_stage("mlp_out0")

            norm_stage(3)
            follow_stage("diff_in")
            for m in range(M):
                for a in range(2):
                    e.wait_ge(sem["diff_sq"], 2 * m + a + 1)
                    src = scrA[:, m, :] if a == 0 else scrB[:, m * D:(m + 1) * D]
                    c = SS["diff"] + 32 * a + 16 * m
                    e.tensor_reduce(ss[:, c:c + 16], src.rearrange("p (h d) -> p h d", d=64), AX.X, ALU.add)\
                        .then_inc(sem["ss_diff"], 1)
            e.wait_ge(sem["rs_diff"], 1)
            tmp = [scrB[:, 256 * i:256 * i + 256].rearrange("p (m h d) -> p m h d", m=M, h=16) for i in range(4)]
            for a in range(2):
                for m in range(M):
                    v = dif[:, m, a * D:(a + 1) * D].rearrange("p (h d) -> p h d", d=64)
                    chain(scale_heads(v, SS["diff"] + 32 * a + 16 * m, 16, (dq_gain, dk_gain)[a]))
                v = dif[:, :, a * D:(a + 1) * D].rearrange("p m (h d) -> p m h d", d=64)
                rope(v[:, :, :, 0:8], v[:, :, :, 8:16], angles(0, 48, 56, 16), angles(1, 48, 56, 16),
                     v[:, :, :, 0:8], v[:, :, :, 8:16], tmp).then_inc(sem["dqk_roped"], 1)
                e.wait_ge(sem["dqk_roped"], a + 1)
            for name, dst in (("dqT", dqT), ("dkT", dkT)):
                for i in range(4):
                    turn_out(name, i, plain(dst))
            attention("diff", 8, comps=2)
            e.wait_ge(sem["o_taken"], plan.n_pt)
            for m in range(M):
                e.wait_ge(sem["sub_sq"], m + 1)
                c = SS["sub"] + 8 * m
                e.tensor_reduce(ss[:, c:c + 8], scrB[:, m * D:(m + 1) * D].rearrange("p (h d) -> p h d", d=P),
                                AX.X, ALU.add).then_inc(sem["ss_sub"], 1)
            e.wait_ge(sem["rs_sub"], 1)
            for m in range(M):
                c = SS["sub"] + 8 * m
                v = scrA[:, m, :].rearrange("p (h d) -> p h d", d=P)
                chain(e.tensor_tensor(v, v, rstd[:, c:c + 8].unsqueeze(2).to_broadcast([P, 8, P]), ALU.mult))
                e.tensor_tensor(v, v, sub_gain.unsqueeze(1).to_broadcast([P, 8, P]), ALU.mult)\
                    .then_inc(sem["d_rows_done"], 1)
            low_tiles("o2T")
            follow_stage("diff_out")
            norm_stage(4)
            follow_stage("mlp_in1")
            follow_stage("mlp_out1")
    return nc


NAMES = ["x", "c", "positions", "w_ada", "b_ada", "g_pre", "g_post", "w_in", "g_q_lat", "w_uq", "g_kv_lat", "w_ukv",
         "w_o_mla", "w_o_moba", "b_merge", "w_out", "c_2", "positions_2", "ln_mix_g_2", "ln_mlp_g_2", "w_ada_2",
         "b_ada_2", "w_mlp_in_2", "w_mlp_out_2", "nsa_w_in_2", "nsa_b_gate_2", "nsa_q_gain_2", "nsa_k_gain_2",
         "nsa_pe_k_2", "nsa_w_ck1_2", "nsa_w_ck2_2", "nsa_pe_v_2", "nsa_w_cv1_2", "nsa_w_cv2_2", "nsa_w_out_2",
         "diff_w_in_2", "diff_q_gain_2", "diff_k_gain_2", "diff_lq1_2", "diff_lk1_2", "diff_lq2_2", "diff_lk2_2",
         "diff_subln_g_2", "diff_w_out_2"]


def kernel(**inputs):
    import concourse.bacc as bacc
    from concourse.bass_utils import run_bass_kernel_spmd

    freq = [np.float32(10000.0) ** (-np.arange(h, dtype=np.float32) / np.float32(h)) for h in (16, 32)]
    freq.append(np.float32(500000.0) ** (-np.arange(0, 16, 2, dtype=np.float32) / np.float32(16)))
    arrays = {"inv_freq": np.concatenate(freq).astype(np.float32)}
    for name in NAMES:
        arrays[name] = np.ascontiguousarray(inputs[name])
    nc = bacc.Bacc("TRN2", target_bir_lowering=False, num_devices=1)
    t_in = {name: nc.dram_tensor("in_" + name, a.shape, mybir.dt.from_np(a.dtype), kind="ExternalInput").ap()
            for name, a in arrays.items()}
    out = nc.dram_tensor("out_x", (1, S, D), F32, kind="ExternalOutput").ap()
    build(nc, t_in, out)
    r = run_bass_kernel_spmd(nc, [{"in_" + k: v for k, v in arrays.items()}], core_ids=[0])
    return r.results[0]["out_x"]
```

```python
from contextlib import ExitStack
import math
import numpy as np

import concourse.bass as bass
from concourse import mybir
from concourse.alu_op_type import AluOpType as ALU

ACT = mybir.ActivationFunctionType
AX = mybir.AxisListType
F32 = mybir.dt.float32
F32R = mybir.dt.float32r
I32 = mybir.dt.int32

P = 128
S = 256
M = S // P
D = 1024
DT = D // P
EPS = 1e-6
NEG = -1e30
RING = 4
SLOT = 2048
PART = 1024
ATT_PIECES = range(12, 16)
WARM = {"x0": 0, "x1": 36, "x2": 26, "x3": 18, "x4": 18, "mb_roped": 24, "u_mb": 12, "u_mla": 18, "cmpin": 14,
        "cmpT": 14, "kT": 8, "diff": 18, "attention": 8, "diff_end": 16}
PARTS = 3
ADA_RING = 2
ADA_FIRST = 6
LAM_INIT = 0.8 - 0.6 * math.exp(-0.3)
MLA_SCALE = (64 + 32) ** -0.5
HEAD_SCALE = 64 ** -0.5

DVE_JOBS = ("merge", "w_o_mla", "w_o_moba", "nsa_out", "diff_out", "mlp_out0", "mlp_out1")



class Plan:
    def __init__(self):
        self.chunks = []
        self.jobs = []
        self.parts = []
        self.last_part = []
        self.pair_at = {}
        self.works = {}
        self.n_works = 0
        self.n_units = 0
        self.work_free = []
        self.turned = {"act": 0, "dve": 0}
        self.turned_after = {}
        self.pt_of_unit = []
        self.copied = {"act": 0, "dve": 0}
        self.copied_after = {}
        self.job_free = []
        self.job_done = []
        self.chunk_free = {}
        self.low_by, self.low_count = [], []

    def chunk(self, weight, k0, kt, c0, n):
        self.chunks.append((weight, k0, kt, c0, n))
        return len(self.chunks) - 1

    def pair(self, stage, weight, kt, c0, n, lhs="hT", lhs0=0, T=False, key=None):
        spec = dict(stage=stage, lhs=lhs, lhs0=lhs0, n=n, T=T, key=c0 if key is None else key, parts=[])
        for k0 in range(0, kt, 4):
            c = self.chunk(weight, k0, min(4, kt - k0), c0, n)
            for k in range(0, min(4, kt - k0), 2):
                spec["parts"].append(len(self.parts))
                self.parts.append((c, k, min(2, min(4, kt - k0) - k), k0 + k))
        self.last_part.append(len(self.parts) - 1)
        for half in range(2):
            self.jobs.append(dict(spec, half=half, m=half, c0=spec["key"]))
        self.pair_at[(stage, spec["key"])] = len(self.last_part) - 1

    def work(self, stage, n, by="both"):
        self.works[stage] = self.n_works
        for i in range(n):
            w = self.n_works + i
            if by == "units":
                self.n_units += 1
                self.work_free.append(("probs_ready", self.n_units))
                continue
            who = ("act", "dve")[w % 2] if by == "both" else by
            self.turned[who] += 1
            self.work_free.append(("turned_" + who, self.turned[who]))
        self.n_works += n
        self.turned_after[stage] = dict(self.turned)


def make_plan():
    p = Plan()
    p.pair("lat", "w_in", DT, 0, 416)
    for i, name in enumerate(("q_mb", "k_mb", "v_mb")):
        p.pair(name, "w_in", DT, 928 + 512 * i, 512, key=0)
    for n0, n in ((0, 512), (512, 256)):
        p.pair("uq", "w_uq", 2, n0, n, lhs="latT")
    for n0 in (0, 512):
        p.pair("ukv", "w_ukv", 1, n0, 512, lhs="latT", lhs0=2)
    for name, c0 in (("z_mla", 416), ("z_mb", 2464)):
        p.pair(name, "w_in", DT, c0, 512, key=0)
    for i in range(4):
        p.pair("merge", "w_in", DT, 2976 + 512 * i, 512, key=512 * i)
    for name, lhs0 in (("w_o_moba", 4), ("w_o_mla", 0)):
        for n0 in (0, 512):
            p.pair(name, name, 4, n0, 512, lhs0=lhs0)
    for n0 in (0, 512):
        p.pair("w_out", "w_out", DT, n0, 512)
    for layer, (first, n_first, mix_out) in enumerate((("nsa_in", 2608, "nsa_out"), ("diff_in", 3072, "diff_out"))):
        for n0 in (1024, 2560, 0, 512, 1536, 2048) if layer == 0 else range(0, n_first, 512):
            p.pair(first, first, DT, n0, min(512, n_first - n0))
        for n0 in (0, 512):
            p.pair(mix_out, mix_out, DT, n0, 512)
        for f in range(8):
            p.pair("mlp_in%d" % layer, "mlp_in%d" % layer, DT, 512 * f, 512, T=True)
        for n0 in (0, 512):
            p.pair("mlp_out%d" % layer, "mlp_out%d" % layer, 32, n0, 512, lhs="hidT")
    for stage, n, by in (
            ("cols", 1, "dve"), ("x0", 4, "act"), ("latT", 2, "dve"), ("mbqT", 2, "both"), ("mbkT", 2, "both"),
            ("mb", 8, "units"), ("mlaT", 8, "both"), ("mla", 8, "units"), ("uT", 4, "dve"), ("yT", 4, "dve"),
            ("x1", 4, "act"), ("cmpin", 4, "dve"), ("hid", 2, "dve"), ("kv_cmp", 2, "dve"), ("kcT", 1, "dve"),
            ("qcT", 4, "both"), ("cmpS", 4, "dve"), ("cmpT", 2, "act"), ("cmpO", 4, "dve"), ("qrT", 4, "both"),
            ("kT0", 2, "both"), ("sel", 16, "units"), ("kT1", 2, "both"), ("win", 16, "units"), ("o1T", 4, "dve"), ("x2", 4, "act"),
            ("x3", 4, "act"), ("dqT", 4, "both"), ("dkT", 4, "both"), ("diff", 16, "units"), ("o2T", 4, "dve"),
            ("x4", 4, "act")):
        p.work(stage, n, by)
    p.unit0, p.pt0, u, t = {}, {}, 0, 0
    for name, n, nt in (("mb", 8, 8), ("mla", 8, 8), ("sel", 16, 16), ("win", 16, 16), ("diff", 16, 8)):
        p.unit0[name], p.pt0[name] = u, t
        p.pt_of_unit += [t + i * nt // n for i in range(n)]
        u, t = u + n, t + nt
    p.n_pt = t
    for job in p.jobs:
        who = job["by"] = "dve" if job["stage"] in DVE_JOBS else "act"
        p.copied[who] += 1
        p.job_free.append(("copied_" + who, p.copied[who]))
        p.copied_after[job["stage"]] = dict(p.copied)
    for j in range(len(p.jobs)):
        p.job_done.append(("first_done", j // 2 + 1) if j % 2 == 0 else ("part_done", p.last_part[j // 2] + 1))
    n_low = {"dve": 0, "pool": 0}
    for q, (c, k, nk, k_w) in enumerate(p.parts):
        stage = next(p.jobs[2 * i]["stage"] for i, last in enumerate(p.last_part) if q <= last)
        key = next(p.jobs[2 * i]["key"] for i, last in enumerate(p.last_part) if q <= last)
        roots = stage.startswith("mlp_in") or (stage, key) in (("diff_in", 1024), ("diff_in", 2048))
        roots = roots or ((stage, key) == ("nsa_in", 1536) and k_w >= 4)
        roots = roots or (stage.startswith("mlp_out") and k_w < 6 and p.chunks[c][3] == 0)
        who = "pool" if q % 2 and not roots else "dve"
        n_low[who] += 1
        p.low_by.append(who)
        p.low_count.append(n_low[who])
        p.chunk_free.setdefault(c, {})["low_ready_" + who] = n_low[who]
    p.pieces = [("w_ada", 0, 512 * i) for i in range(6)]
    for layer in range(2):
        p.pieces += [("w_ada_2", layer, 512 * i) for i in range(12)]
    def spread(pieces, a, b):
        halves = [2 * n + h for n in pieces for h in range(2)]
        for i, h in enumerate(halves):
            p.half_after[h] = a + i * (b - a) // len(halves)

    def first_part(stage, key=0):
        q = p.pair_at[(stage, key)]
        return p.last_part[q - 1] + 1 if q else 0
    p.half_after = {}
    spread(range(4, 10), 5, first_part("w_out") - 3)
    spread(range(10, 12), first_part("nsa_in", 1024), first_part("nsa_out") - 6)
    spread(ATT_PIECES, first_part("nsa_out") - 1, first_part("nsa_out") - 1)
    spread(range(16, 30), first_part("nsa_out"), first_part("diff_in") - 6)
    p.piece_sum, p.piece_end = {}, {}
    for n in [n for n in range(4, 30) if n not in ATT_PIECES]:
        at = p.half_after[2 * n + 1] + 4
        p.piece_sum.setdefault(at, []).append(n)
        p.piece_end.setdefault(at + 1, []).append(n)
    last_of = {c: q for q, (c, _, _, _) in enumerate(p.parts)}
    after = {}
    for h in range(8, 60):
        taken = p.half_after.get(h - ADA_RING, 0)
        fit = [c for c in sorted(last_of) if c - RING in last_of and last_of[c - RING] <= p.half_after[h] + PARTS]
        late = [c for c in fit if last_of[c - RING] >= taken + PARTS]
        after.setdefault(late[0] if late else max(fit, default=0), []).append(h)
    at, moved = 0, {}
    for h in range(8, 60):
        at = max(at, next(c for c, hs in after.items() if h in hs))
        if 2 * ATT_PIECES[0] <= h < 2 * ATT_PIECES[-1] + 2 + ADA_RING:
            at = p.parts[first_part("nsa_out")][0] + RING - 1
        moved.setdefault(at, []).append(h)
    after = moved
    p.loads = [("ada", h) for h in range(2, 8)]
    for c in range(len(p.chunks)):
        p.loads.append(("w", c))
        p.loads += [("ada", h) for h in after.get(c, [])]
    return p


def build(nc, t_in, out):
    plan = make_plan()
    jobs, works = plan.jobs, plan.works
    with ExitStack() as ctx:
        def sb(name, shape, dt=F32):
            return ctx.enter_context(nc.sbuf_tensor(name, shape, dt))

        class Named(dict):
            def __missing__(self, name):
                self[name] = ctx.enter_context(nc.semaphore(name))
                return self[name]

        sem = Named()
        bank = [ctx.enter_context(nc.psum_tensor("bank%d" % i, [P, 512], F32)) for i in range(8)]

        ring = sb("ring", [P, RING, SLOT])
        high = sb("weight_high", [P, PARTS, PART], F32R)
        low = sb("weight_low", [P, PARTS, PART], F32R)
        ada_ring = sb("ada_ring", [P, ADA_RING, 4, 512])
        acc = sb("ada_acc", [P, 2, 512])
        x = sb("x_rows", [P, M, D])
        hT = [sb("hT_" + part, [P, DT, S], F32R) for part in ("high", "low")]
        A_ACT, A_QK, A_B = 9312, 24 * S, 2 * D
        base = nc.sbuf_base
        region = sb("region", [P, A_ACT + A_QK + A_B])
        act = region[:, 0:A_ACT]
        qk = region[:, A_ACT:A_ACT + A_QK].rearrange("p (a s) -> p a s", s=S)
        scrB = region[:, A_ACT + A_QK:]

        def over(name, shape, first):
            return nc.alloc_sbuf_tensor_at(name, shape, F32R, offset=base + 4 * first)
        hidT = [over("hidT_" + part, [P, 32, S], 32 * S * i) for i, part in enumerate(("high", "low"))]
        latT = [over("latT_" + part, [P, 3, S], A_ACT + (18 + 3 * i) * S) for i, part in enumerate(("high", "low"))]
        scrA = sb("scratch_a", [P, M, D])
        gate = sb("gates", [P, 3, D])
        probs = sb("probs", [P, 4, 384])
        probsT = sb("probsT", [P, 2, 384])
        ident = sb("ident", [P, P])
        ones = sb("ones", [P, P])
        causal = sb("causal", [P, P])
        cmp_neg = sb("cmp_neg", [P, M, 15])
        cmp_keep = sb("cmp_keep", [P, M, 15])
        own = sb("own_head", [120, 8])
        vec_rows = act[0:108, 0:128]
        vec_rows2 = act[0:64, 128:256]
        cols = sb("cols", [P, 192])
        silu_c = sb("silu_c", [P, 16])
        mod = sb("mod_cols", [P, 5, 2, 8])
        gs = sb("gain_scale", [P, 5, 8])
        tiny = sb("tiny", [P, 880])
        pos_i = sb("pos_i", [P, 2, M], I32)
        pos_f = sb("pos_f", [P, 2, M])
        cs = sb("cos_sin", [P, M, 2, 56])
        trig = scrA[:, 1, 0:224].rearrange("p (m a n) -> p m a n", m=M, a=2)
        neg_max = sb("neg_max", [P, 16])
        sums = sb("prob_sums", [P, 16])
        inv = sums
        ss = sb("sum_squares", [P, 160])
        rstd = ss
        half_neg = sb("minus_half", [P, 64])
        stat = sb("stat", [P, 128])

        q_gain, k_gain = tiny[:, 0:64], tiny[:, 64:256].rearrange("p (a d) -> p a d", d=64)
        dq_gain, dk_gain = tiny[:, 256:320], tiny[:, 320:384]
        b_gate, lqk = tiny[:, 512:560], tiny[:, 560:816].rearrange("p (a d) -> p a d", d=64)
        inv_freq = tiny[:, 816:872]
        lam_tmp = scrA[:, 1, 256:384].rearrange("p (a d) -> p a d", d=64)
        lam = tiny[:, 872:880]

        C_C, C_PRE, C_BADA, C_MIX, C_MLP, C_GQ, C_GKV, C_SUB, C_PEK, C_PEV, C_BADA2 = \
            0, 16, 24, 40, 56, 72, 74, 75, 76, 92, 128

        lat = act[:, 0:832].rearrange("p (m n) -> p m n", m=M)
        v_mla = scrA[:, 0, :].rearrange("p (m h d) -> p m h d", m=M, h=8)
        z = {"z_mla": act[:, 832:1856].rearrange("p (m n) -> p m n", m=M),
             "z_mb": act[:, 1856:2880].rearrange("p (m n) -> p m n", m=M)}
        merge = act[:, 2880:6976].rearrange("p (m n) -> p m n", m=M)
        qk_mb = act[:, 6976:9024].rearrange("p (a m n) -> p a m n", a=2, m=M)
        y_rows = qk[:, 0:8, :].rearrange("p a s -> p (a s)").rearrange("p (m n) -> p m n", m=M)
        y_gated = act[:, 2880:4928].rearrange("p (m n) -> p m n", m=M)
        v_mb = scrA[:, 1, :].rearrange("p (m h d) -> p m h d", m=M, h=8)
        qT_mb, kT_mb = qk[:, 0:4, :], qk[:, 4:8, :]
        qT_mla, kT_mla = qk[:, 8:16, :], qk[:, 16:24, :]
        b_merge = scrB
        q_up = act[:, 2880:4416].rearrange("p (m n) -> p m n", m=M)
        k_up = act[:, 4416:5952].rearrange("p (m n) -> p m n", m=M)
        rope_tmp = act[:, 832:2880].rearrange("p (a n) -> p a n", a=4)
        mla_tmp = qk[:, 8:16, :].rearrange("p a s -> p (a s)").rearrange("p (a n) -> p a n", a=4)
        o_blk = act[:, 6976:9024].rearrange("p (a m n) -> p a m n", a=2, m=M)

        nsa = act[:, 0:5216].rearrange("p (m n) -> p m n", m=M)
        q_rot = act[:, 5216:7264].rearrange("p (m n) -> p m n", m=M)
        k_dup = act[:, 7264:9312].rearrange("p (m a g c d) -> p m a g c d", m=M, a=2, g=4, c=2)
        kv_dup = q_rot.rearrange("p m (a g c d) -> p m a g c d", a=2, g=4, c=2)
        qcT, qrT, kselT, kwinT = qk[:, 0:8, :], qk[:, 8:16, :], qk[:, 16:20, :], qk[:, 20:24, :]
        z_blk = scrB[:, :].rearrange("p (w h g i t) -> p w h g i t", w=2, h=2, g=4, i=16)
        small = qk[:, 20:24, :].rearrange("p a s -> p (a s)")
        hid = small[:, 0:120].rearrange("p (a n) -> p a n", a=2)
        hid_rep = small[:, 128:368].rearrange("p (f g r c) -> p f g r c", f=2, g=2, r=4)
        k_cmp = small[:, 384:448]
        k_cmp2 = small[:, 448:576].rearrange("p (a d) -> p a d", a=2)
        kcT = small[:, 576:636]
        w_c2 = sb("w_c2", [P, 2, 64])
        w_c1 = [v.rearrange("p (t n) -> p t n", n=P) for v in
                (act[:, 7264:9312], qk[:, 8:16, :].rearrange("p a s -> p (a s)"))]
        blockV = scrB[:, 0:1024].rearrange("p (f h d) -> p f h d", f=2, h=8)
        pcT = scrB[:, 1024:1536].rearrange("p (m f q) -> p m f q", m=M, f=2)
        pc = scrB[:, 1536:2016].rearrange("p (m n) -> p m n", m=M)
        o_rows = scrA
        k_dup_tmp = scrA[:, 0, :].rearrange("p (a n) -> p a n", a=4)
        o_tmp = scrB[:, 0:256].rearrange("p (a m d) -> p a m d", a=2, m=M)

        k_squares = [act[:, 7776:8288], act[:, 8800:9312]]

        dif = act[:, 0:6144].rearrange("p (m n) -> p m n", m=M)
        dqT, dkT = qk[:, 0:8, :], qk[:, 8:16, :]

        whole = probs[:, :, :].rearrange("p a n -> p (a n)").rearrange("p (a n) -> p a n", n=512)
        operand = {"hT": hT, "latT": latT, "hidT": hidT}

        def slot(c):
            w, k0, kt, c0, n = plan.chunks[c]
            return ring[:, c % RING, 0:kt * n].rearrange("p (k n) -> p k n", k=kt)

        def part_words(q):
            c, k, nk, _ = plan.parts[q]
            n = plan.chunks[c][4]
            return ring[:, c % RING, k * n:(k + nk) * n], nk * n

        weights = {k: t_in[k][0].rearrange("(t p) n -> p t n", p=P) for k in
                   ("w_in", "w_uq", "w_ukv", "w_o_mla", "w_o_moba", "w_out", "w_ada")}
        for name, src, i in (("nsa_in", "nsa_w_in_2", 0), ("nsa_out", "nsa_w_out_2", 0), ("diff_in", "diff_w_in_2", 0),
                             ("diff_out", "diff_w_out_2", 0), ("ck1", "nsa_w_ck1_2", 0), ("cv1", "nsa_w_cv1_2", 0),
                             ("mlp_in0", "w_mlp_in_2", 0), ("mlp_in1", "w_mlp_in_2", 1),
                             ("mlp_out0", "w_mlp_out_2", 0), ("mlp_out1", "w_mlp_out_2", 1)):
            weights[name] = t_in[src][i].rearrange("(t p) n -> p t n", p=P)
        ada2 = [t_in["w_ada_2"][i].rearrange("(t p) n -> p t n", p=P) for i in range(2)]

        def ada_slot(h):
            if h < ADA_FIRST:
                return region[:, 1024 + SLOT * h:1024 + SLOT * (h + 1)].rearrange("p (k n) -> p k n", k=4)
            return ada_ring[:, h % 2]

        def ada_arrived(h):
            return ("ada_first%d" % h, 16) if h < ADA_FIRST else ("ada_in%d" % (h % 2), 16 * ((h - ADA_FIRST) // 2 + 1))

        def piece_source(n):
            w, layer, c0 = plan.pieces[n]
            return (weights["w_ada"] if w == "w_ada" else ada2[layer]), c0

        def piece_use(n):
            if n < 6:
                part, half = n // 2, n % 2
                return ("gate", 0, 512 * half) if part == 2 else ("col", 0, part, 4 * half, C_BADA + 4 * n)
            layer, q = (n - 6) // 12, (n - 6) % 12
            part, half = q // 2, q % 2
            if part in (2, 5):
                return "gate", (1 + 2 * layer + part // 5) % 3, 512 * half
            norm = 1 + 2 * layer + part // 3
            return "col", norm, part % 3, 4 * half, C_BADA2 + 32 * layer + 16 * (part // 3) + 4 * (q % 6)

        class Chain:
            def __init__(self, eng, name):
                self.eng, self.sem, self.n = eng, sem[name], 0

            def __call__(self, ins):
                self.n += 1
                ins.then_inc(self.sem, 1)
                self.eng.wait_ge(self.sem, self.n)

        def turned(eng, stage):
            for who in ("act", "dve"):
                eng.wait_ge(sem["turned_" + who], plan.turned_after[stage][who])

        def copied(eng, stage):
            for who in ("act", "dve"):
                if plan.copied_after[stage][who]:
                    eng.wait_ge(sem["copied_" + who], plan.copied_after[stage][who])

        def pair_copied(eng, stage, key):
            name, value = plan.job_free[2 * plan.pair_at[(stage, key)] + 1]
            eng.wait_ge(sem[name], value)

        pair_of = [p for p, q in enumerate(plan.last_part) for _ in range(q - (plan.last_part[p - 1] if p else -1))]

        def stage_parts(stage, key=None, a=None, b=None):
            return [q for q, p in enumerate(pair_of) if jobs[2 * p]["stage"] == stage and
                    (key is None or jobs[2 * p]["key"] == key)][a:b]

        def beside_parts(name, step):
            parts = {"mb": stage_parts("z_mla") + stage_parts("z_mb"), "mla": stage_parts("merge")}.get(name, [])
            per = -(-len(parts) // 10)
            mine = parts[per * step:per * (step + 1)]
            return mine[:1], mine[1:]

        def multiply_tile(e, chain, n, k):
            h = 2 * n + k // 4
            if k % 4 == 0:
                name, value = ada_arrived(h)
                e.wait_ge(sem[name], value)
            if k == 0 and n >= 2:
                e.wait_ge(sem["piece_summed"], n - 1)
            w = ada_slot(h)[:, k % 4, :]
            c = (0 if n < 6 else 8) + k
            s_ = silu_c[:, c:c + 1]
            if k == 0:
                ins = e.tensor_scalar(acc[:, n % 2, :], w, s_, None, ALU.mult)
            elif e is nc.gpsimd:
                chain(e.tensor_scalar(w, w, s_, None, ALU.mult))
                ins = e.tensor_tensor(acc[:, n % 2, :], acc[:, n % 2, :], w, ALU.add)
            else:
                ins = e.scalar_tensor_tensor(out=acc[:, n % 2, :], in0=w, scalar=s_, in1=acc[:, n % 2, :],
                                             op0=ALU.mult, op1=ALU.add)
            if k % 4 < 3:
                chain(ins)
            else:
                ins.then_inc(sem["ada_used"], 1)
                e.wait_ge(sem["ada_used"], h + 1)

        NORM_X = ["x0", "x1", "x2", "x3", "x4"]
        block = ctx.enter_context(nc.Block())

        @block.sync
        def _(sp):
            def half_piece(h):
                src, c0 = piece_source(h // 2)
                k = 4 * (h % 2)
                sp.dma_start(ada_slot(h), src[:, k:k + 4, c0:c0 + 512]).then_inc(sem[ada_arrived(h)[0]], 16)

            half_piece(0)
            r = 0
            for src in (t_in["c"][0], t_in["c_2"][0], t_in["g_pre"][0], t_in["b_ada"][0, 0:2048],
                        t_in["ln_mix_g_2"].rearrange("a n -> (a n)"), t_in["ln_mlp_g_2"].rearrange("a n -> (a n)"),
                        t_in["g_q_lat"][0], t_in["g_kv_lat"][0], t_in["diff_subln_g_2"][0]):
                n = src.shape[0] // P
                sp.dma_start(vec_rows[r:r + n, :], src.rearrange("(r n) -> r n", n=P)).then_inc(sem["rows_in"], 16)
                r += n
            half_piece(1)
            for name in ("nsa_pe_k_2", "nsa_pe_v_2"):
                sp.dma_start(vec_rows[r:r + 16, :], t_in[name][0].rearrange("(r a) d -> r (a d)", a=2))\
                    .then_inc(sem["rows_in"], 16)
                r += 16
            for layer in range(2):
                for half_ in range(2):
                    q = 32 * layer + 16 * half_
                    sp.dma_start(vec_rows2[q:q + 16, :], t_in["b_ada_2"][layer, 3072 * half_:3072 * half_ + 2048]
                                .rearrange("(r n) -> r n", n=P)).then_inc(sem["rows_in"], 16)
            for kind, n in plan.loads:
                if kind == "w":
                    w, k0, kt, c0, cn = plan.chunks[n]
                    if n >= RING:
                        for name, value in plan.chunk_free[n - RING].items():
                            sp.wait_ge(sem[name], value)
                    sp.dma_start(slot(n), weights[w][:, k0:k0 + kt, c0:c0 + cn]).then_inc(
                        sem["chunk_in%d" % (n % RING)], 16)
                else:
                    if n == 4:
                        sp.dma_start(x[:, :, :], t_in["x"][0].rearrange("(m p) n -> p m n", p=P))\
                            .then_inc(sem["x_in"], 16)
                    if n >= ADA_FIRST + ADA_RING:
                        sp.wait_ge(sem["ada_used"], n - ADA_RING + 1)
                    half_piece(n)
            for m in range(M):
                sp.wait_ge(sem["x_done4"], m + 1)
                sp.dma_start(out[0, m * P:(m + 1) * P, :], x[:, m, :]).then_inc(sem["stored"], 16)
            sp.wait_ge(sem["stored"], 16 * M)

        @block.tensor
        def _(pe):
            def reduce_piece(n):
                pe.wait_ge(sem["ada_used"], 2 * n + 2)
                if n >= 1:
                    pe.wait_ge(sem["mod_taken"], n)
                use = piece_use(n)
                if use[0] == "gate":
                    mm = pe.matmul(bank[3][:, :], ones[:, :], acc[:, n % 2, :], start=True, stop=True)
                else:
                    for i in range(4):
                        mm = pe.matmul(bank[3][:, i:i + 1], acc[:, n % 2, i * P:(i + 1) * P], ones[:, 0:1],
                                       start=True, stop=True)
                mm.then_inc(sem["piece_summed"], 1)

            n_taken = [0]

            def keep_warm(n):
                if n_taken[0]:
                    pe.wait_ge(sem["pt_taken"], n_taken[0])
                for _ in range(n):
                    pe.matmul(bank[6][:, 384:512], ones[:, :], ones[:, :], start=True, stop=True)

            def bank_for(j):
                if j >= 3:
                    name, value = plan.job_free[j - 3]
                    pe.wait_ge(sem[name], value)
                return bank[j % 3]

            def run_part(q):
                c, _, nk, k_w = plan.parts[q]
                p = pair_of[q]
                first, last = q == 0 or pair_of[q - 1] != p, q == plan.last_part[p]
                job = jobs[2 * p]
                n = job["n"]
                pe.wait_ge(sem["low_ready_" + plan.low_by[q]], plan.low_count[q])
                wh, wl = [buf[:, q % PARTS, 0:nk * n].rearrange("p (k n) -> p k n", k=nk) for buf in (high, low)]
                ah, al = operand[job["lhs"]]
                for half in range(2):
                    j = 2 * p + half
                    b = bank_for(j) if first else bank[j % 3]
                    for k in range(nk):
                        a = job["lhs0"] + k_w + k
                        begin, end = first and k == 0, last and k == nk - 1
                        if job["T"]:
                            for i in range(2):
                                f = (2 * half + i) * P
                                for s_, (w, v) in enumerate(((wh, ah), (wh, al), (wl, ah))):
                                    mm = pe.matmul(b[:, i * S:(i + 1) * S], w[:, k, f:f + P], v[:, a, :],
                                                   start=begin and i == 0 and s_ == 0, stop=end and s_ == 2,
                                                   skip_group_check=True)
                        else:
                            t = slice(half * P, (half + 1) * P)
                            for s_, (v, w) in enumerate(((ah, wh), (ah, wl), (al, wh))):
                                mm = pe.matmul(b[:, 0:n], v[:, a, t], w[:, k, :],
                                               start=begin and s_ == 0, stop=end and s_ == 2)
                    if half == 0 and last:
                        mm.then_inc(sem["first_done"], 1)
                mm.then_inc(sem["part_done"], 1)
                for n_ in plan.piece_sum.get(q, []):
                    reduce_piece(n_)

            def run_stage(*which, after=None):
                for k, q in enumerate(stage_parts(*which)):
                    if after is not None and pair_of[q] == pair_of[stage_parts(*which)[0]]:
                        name, value = after(k)
                        pe.wait_ge(sem[name], value)
                    run_part(q)

            def split_x(i):
                return lambda k: ("x_split", 4 * i + k + 1)

            def low_of(stage, first=0):
                return lambda k: plan.work_free[works[stage] + first + k]

            def work_bank(w):
                if w >= 2:
                    name, value = plan.work_free[w - 2]
                    pe.wait_ge(sem[name], value)
                return bank[4 + w % 2]

            def turn(stage, src, n_tiles, ready=None, per=2, rows=P):
                for i in range(0, n_tiles, per):
                    w = works[stage] + i // per
                    b = work_bank(w)
                    for k in range(i, min(i + per, n_tiles)):
                        for m in range(M):
                            if ready is not None and m + (i > 0) * M < M and k == i:
                                pe.wait_ge(sem[ready], m + 1)
                            s = src(k, m)
                            o = (k - i) * S + m * P
                            mm = pe.transpose(b[0:s.shape[-1], o:o + P], s, ident[:, :])
                    mm.then_inc(sem["work_ready"], 1)

            def scores(name, i, q, kk):
                w = works[name] + i
                b = work_bank(w)
                pe.matmul(b[:, 0:P], q[:, 0:P], kk[:, 0:P], start=True, stop=False)
                pe.matmul(b[:, 0:P], ident[:, :], causal[:, :], start=False, stop=True)
                pe.matmul(b[:, P:384], q[:, P:S], kk[:, 0:S], start=True, stop=False)
                pe.matmul(b[:, 256:384], ident[:, :], causal[:, :], start=False, stop=True)\
                    .then_inc(sem["work_ready"], 1)

            def turn_probs(name, i, u):
                t = plan.pt0[name] + i
                if t >= 1:
                    pe.wait_ge(sem["pt_taken"], t)
                if name == "diff":
                    pe.wait_ge(sem["diff_mixed"], i + 1)
                else:
                    pe.wait_ge(sem["probs_ready"], u + 1)
                for a in range(3):
                    mm = pe.transpose(bank[6][:, a * P:(a + 1) * P], probs[:, u % 4, a * P:(a + 1) * P], ident[:, :])
                mm.then_inc(sem["pt_ready"], 1)
                n_taken[0] = t + 1

            def values(name, i, v, d):
                t = plan.pt0[name] + i
                pe.wait_ge(sem["pt_taken"], t + 1)
                if t >= 1:
                    pe.wait_ge(sem["o_taken"], t)
                r = (t % 2) * 256
                pT = probsT[:, t % 2, :]
                pe.matmul(bank[7][:, r:r + d], pT[:, 0:P], v(0), start=True, stop=True)
                pe.matmul(bank[7][:, r + d:r + 2 * d], pT[:, P:2 * P], v(0), start=True, stop=False)
                pe.matmul(bank[7][:, r + d:r + 2 * d], pT[:, 2 * P:384], v(1), start=False, stop=True)\
                    .then_inc(sem["o_ready"], 1)

            def attention(name, heads, q, kk, v, d=64, comps=1):
                u0 = plan.unit0[name]
                for i in range(heads + 2):
                    if i < heads:
                        for c in range(comps):
                            scores(name, comps * i + c, q(i, c), kk(i, c))
                    one, two = beside_parts(name, i)
                    for q_ in one:
                        run_part(q_)
                    if i == 1:
                        keep_warm(WARM["attention"])
                    if i == heads and name == "diff":
                        keep_warm(WARM["diff_end"])
                    if 1 <= i <= heads:
                        turn_probs(name, i - 1, u0 + comps * (i - 1))
                    for q_ in two:
                        run_part(q_)
                    n = ATT_PIECES[0] + (i + heads * (name == "win")) // DT
                    if name in ("sel", "win") and i < heads and i % DT == 4 and n > ATT_PIECES[0]:
                        reduce_piece(n - 1)
                    if i >= 2:
                        values(name, i - 2, v(i - 2), d)

            pe.wait_ge(sem["const_ready"], 1)
            pe.wait_ge(sem["rows_in"], 16 * 15)
            pe.transpose(bank[4][:, 0:108], vec_rows[:, :], ident[0:108, 0:108])
            pe.transpose(bank[4][:, 128:192], vec_rows2[:, :], ident[0:64, 0:64]).then_inc(sem["work_ready"], 1)
            for n in range(4):
                reduce_piece(n)

            pe.wait_ge(sem["masks_ready"], 1)

            def norm_turn(i):
                keep_warm(WARM["x%d" % i])
                turn(NORM_X[i], lambda k, m: scrA[:, m, k * P:(k + 1) * P], DT, ready="xs_ready%d" % i)

            norm_turn(0)
            run_stage("lat", after=split_x(0))
            run_stage("q_mb")
            run_stage("k_mb")
            pe.wait_ge(sem["lat_normed"], 1)
            turn("latT", lambda k, m: lat[:, m, k * P:(k + 1) * P], 3)
            run_stage("v_mb")
            turned(pe, "latT")
            run_stage("uq")
            run_stage("ukv")
            keep_warm(WARM["mb_roped"])
            for a, name in enumerate(("mbqT", "mbkT")):
                pe.wait_ge(sem["mb_roped"], a + 1)
                turn(name, lambda k, m: qk_mb[:, a, m, k * P:(k + 1) * P], 4)
            turned(pe, "mbkT")

            def half(buf, h):
                lo = 64 * (h % 2)
                return buf[lo:lo + 64, h // 2, :]

            attention("mb", 8, lambda h, c: half(qT_mb, h), lambda h, c: half(kT_mb, h),
                      lambda h: (lambda a: v_mb[:, a, h, :]))
            pe.wait_ge(sem["mla_roped"], 1)
            turn("mlaT", lambda k, m: (q_up, k_up)[k // 8][:, m, 96 * (k % 8):96 * (k % 8) + 96], 16)
            turned(pe, "mlaT")
            attention("mla", 8, lambda h, c: qT_mla[0:96, h, :], lambda h, c: kT_mla[0:96, h, :],
                      lambda h: (lambda a: v_mla[:, a, h, :]))
            for n, (a, name) in enumerate(((1, "w_o_moba"), (0, "w_o_mla"))):
                keep_warm(WARM[("u_mb", "u_mla")[n]])
                pe.wait_ge(sem["u_ready"], n + 1)
                for i in range(2):
                    b = work_bank(works["uT"] + 2 * n + i)
                    for k in range(2):
                        for m in range(M):
                            mm = pe.transpose(b[:, k * S + m * P:k * S + (m + 1) * P],
                                              o_blk[:, a, m, (2 * i + k) * P:(2 * i + k + 1) * P], ident[:, :])
                    mm.then_inc(sem["work_ready"], 1)
                run_stage(name, after=low_of("uT", 2 * n))
            pe.wait_ge(sem["y_ready"], 4)
            turn("yT", lambda k, m: y_rows[:, m, k * P:(k + 1) * P], DT)
            run_stage("w_out", after=low_of("yT"))

            norm_turn(1)
            run_stage("nsa_in", 1024, after=split_x(1))
            run_stage("nsa_in", 2560)
            run_stage("nsa_in", 0, 0, 3)
            keep_warm(WARM["cmpin"])
            for a in range(2):
                pe.wait_ge(sem["kv_doubled"], 1)
                for i in range(2):
                    w = works["cmpin"] + 2 * a + i
                    b = work_bank(w)
                    for g in range(2):
                        for m in range(M):
                            mm = pe.transpose(b[:, g * S + m * P:g * S + (m + 1) * P],
                                              kv_dup[:, m, a, 2 * i + g].rearrange("p c d -> p (c d)"), ident[:, :])
                    mm.then_inc(sem["work_ready"], 1)
            run_stage("nsa_in", 0, 3, 4)
            run_stage("nsa_in", 512, 0, 2)
            for a in range(2):
                pe.wait_ge(sem["turned_dve"], plan.work_free[works["cmpin"] + 2 * a + 1][1])
                pe.wait_ge(sem["w_c1_in%d" % a], 16)
                w1 = w_c1[a]
                w = works["hid"] + a
                b = work_bank(w)
                for t in range(16):
                    h, i0 = t // 8, t // 8
                    mm = pe.matmul(b[:, 0:60], w1[:, t, :], z_blk[:, a, h, :, i0:i0 + 15, t % 8],
                                   start=t == 0, stop=t == 15)
                mm.then_inc(sem["work_ready"], 1)
            run_stage("nsa_in", 512, 2, 3)
            pe.wait_ge(sem["turned_dve"], plan.work_free[works["hid"]][1])
            pe.wait_ge(sem["w_c2_in"], 32)
            b = work_bank(works["kv_cmp"])
            pe.matmul(b[0:60, 0:64], hid[:, 0, :], w_c2[:, 0, :], start=True, stop=True).then_inc(sem["work_ready"], 1)
            pe.wait_ge(sem["hid_ready"], 1)
            b = work_bank(works["kv_cmp"] + 1)
            for f in range(2):
                mm = pe.matmul(b[0:120, f * 64:(f + 1) * 64], hid_rep[:, f].rearrange("p g r c -> p (g r c)"),
                               w_c2[:, 1, :], start=True, stop=True)
            mm.then_inc(sem["work_ready"], 1)
            run_stage("nsa_in", 512, 3, 4)
            run_stage("nsa_in", 1536, 0, 3)
            pe.wait_ge(sem["k_cmp_ready"], 1)
            b = work_bank(works["kcT"])
            pe.transpose(b[:, 0:60], k_cmp2[0:60].rearrange("p a d -> p (a d)"), ident[0:60, 0:60])\
                .then_inc(sem["work_ready"], 1)
            run_stage("nsa_in", 1536, 3, 4)
            run_stage("nsa_in", 2048, 0, 1)
            pe.wait_ge(sem["q_normed"], 1)
            turn("qcT", lambda k, m: nsa[:, m, k * P:(k + 1) * P], 8)
            run_stage("nsa_in", 2048, 1, 3)
            turned(pe, "kcT")
            turned(pe, "qcT")
            for m in range(M):
                for odd in range(2):
                    b = work_bank(works["cmpS"] + 2 * m + odd)
                    lo = 64 * odd
                    for h in range(8):
                        mm = pe.matmul(b[:, 15 * h:15 * h + 15], qcT[lo:lo + 64, h, m * P:(m + 1) * P],
                                       kcT[lo:lo + 64, 15 * (h // 2):15 * (h // 2) + 15], start=True, stop=True)
                    mm.then_inc(sem["work_ready"], 1)
            run_stage("nsa_in", 2048, 3, 4)
            keep_warm(WARM["cmpT"])
            for m in range(M):
                pe.wait_ge(sem["pc_ready"], m + 1)
                b = work_bank(works["cmpT"] + m)
                for f in range(2):
                    mm = pe.transpose(b[0:120, f * P:(f + 1) * P], pc[:, m, 120 * f:120 * (f + 1)], ident[:, :])
                mm.then_inc(sem["work_ready"], 1)
            for m in range(M):
                pe.wait_ge(sem["turned_act"], plan.work_free[works["cmpT"] + m][1])
                pe.wait_ge(sem["turned_dve"], plan.work_free[works["kv_cmp"] + 1][1])
                for f in range(2):
                    b = work_bank(works["cmpO"] + 2 * m + f)
                    pe.matmul(b[:, :], pcT[0:120, m, f, :], blockV[0:120, f].rearrange("p h d -> p (h d)"),
                              start=True, stop=True).then_inc(sem["work_ready"], 1)
            pe.wait_ge(sem["q_roped"], 1)
            turn("qrT", lambda k, m: q_rot[:, m, k * P:(k + 1) * P], 8)
            for a, (name, kT, v0) in enumerate((("sel", kselT, 1792), ("win", kwinT, 2304))):
                keep_warm(WARM["kT"])
                pe.wait_ge(sem["k_doubled"], a + 1)
                turn("kT%d" % a, lambda k, m: k_dup[:, m, a, k].rearrange("p c d -> p (c d)"), 4)
                turned(pe, "kT%d" % a)
                attention(name, 16, lambda h, c: half(qrT, h),
                          lambda h, c: kT[64 * (h % 2):64 * (h % 2) + 64, h // 4, :],
                          lambda h: (lambda a: nsa[:, a, v0 + 64 * (h // 4):v0 + 64 * (h // 4) + 64]))
            pe.wait_ge(sem["o_rows_done"], 1)
            turn("o1T", lambda k, m: scrA[:, m, k * P:(k + 1) * P], DT)
            run_stage("nsa_out", 0, 0, 2, after=low_of("o1T"))
            reduce_piece(ATT_PIECES[-1])
            run_stage("nsa_out", 0, 2, 4, after=low_of("o1T", 2))
            run_stage("nsa_out", 512)

            def mlp(layer, norm):
                norm_turn(norm)
                run_stage("mlp_in%d" % layer, after=split_x(norm))
                run_stage("mlp_out%d" % layer, after=lambda k: ("hidden", 16 * layer + k + 1))

            mlp(0, 2)
            norm_turn(3)
            run_stage("diff_in", 0, after=split_x(3))
            for key in (512, 1024, 1536, 2048):
                run_stage("diff_in", key)
            for a, name in enumerate(("dqT", "dkT")):
                if a:
                    run_stage("diff_in", 2560)
                keep_warm(WARM["diff"])
                pe.wait_ge(sem["dqk_roped"], a + 1)
                turn(name, lambda k, m: dif[:, m, a * D + k * P:a * D + (k + 1) * P], 8)
            turned(pe, "dkT")
            attention("diff", 8, lambda h, c: dqT[64 * c:64 * c + 64, h, :], lambda h, c: dkT[64 * c:64 * c + 64, h, :],
                      lambda h: (lambda a: dif[:, a, 2048 + h * P:2048 + (h + 1) * P]), d=P, comps=2)
            for half_ in range(2):
                pe.wait_ge(sem["d_rows_done"], half_ + 1)
                for i in (2 * half_, 2 * half_ + 1):
                    b = work_bank(works["o2T"] + i)
                    for k in range(2):
                        for m in range(M):
                            mm = pe.transpose(b[:, k * S + m * P:k * S + (m + 1) * P],
                                              scrA[:, m, (2 * i + k) * P:(2 * i + k + 1) * P], ident[:, :])
                    mm.then_inc(sem["work_ready"], 1)
                if half_ == 0:
                    pe.wait_ge(sem["turned_dve"], plan.work_free[works["o2T"] + 1][1])
                    run_stage("diff_out", 0, 0, 1)
            run_stage("diff_out", 0, 1, 2)
            run_stage("diff_out", 0, 2, 4, after=lambda k: low_of("o2T")(k + 2))
            run_stage("diff_out", 512)
            mlp(1, 4)

        SS = {"x0": 0, "lat": 2, "y": 6, "x1": 8, "nsa": 10, "kc": 58, "x2": 59, "x3": 61, "diff": 63,
              "sub": 127, "x4": 143, "y2": 145}

        @block.scalar
        def _(act_e):
            e = act_e
            e.wait_ge(sem["turned_dve"], 1)
            e.activation(stat[:, 0:16], cols[:, 0:16], ACT.Sigmoid).then_inc(sem["sig_c"], 1)

            def turn_out(stage, i, put):
                w = works[stage] + i
                if w % 2 == 0:
                    e.wait_ge(sem["work_ready"], w + 1)
                    put(i, bank[4 + w % 2]).then_inc(sem["turned_act"], 1)

            def plain(dst, rows=P):
                def put(i, b):
                    return e.activation(dst[0:rows, 2 * i:2 * i + 2, :].rearrange("p a s -> p (a s)"),
                                        b[0:rows, :], ACT.Copy)
                return put

            def high_out(stage, i, dst, scale=1.0):
                w = works[stage] + i
                e.wait_ge(sem["work_ready"], w + 1)
                n = len(dst)
                b = bank[4 + w % 2]
                for k, d in enumerate(dst):
                    s_ = scale if isinstance(scale, float) else scale[:, k:k + 1]
                    wd = 512 // n if n > 1 or d.shape[-1] == 512 else S
                    ins = e.activation(d, b[:, k * wd:(k + 1) * wd], ACT.Copy, scale=s_)
                ins.then_inc(sem["turned_high"], 1)

            def high_tiles(stage, a=0, b=4, scale=1.0, first=0):
                for i in range(a, b):
                    t = 2 * (first + i)
                    high_out(stage, i, [hT[0][:, t:t + 2, :].rearrange("p a s -> p (a s)")], scale)

            def split_high(q):
                if q >= len(plan.parts):
                    return
                c = plan.parts[q][0]
                e.wait_ge(sem["chunk_in%d" % (c % RING)], 16 * (c // RING + 1))
                if q >= PARTS:
                    e.wait_ge(sem["part_done"], q - PARTS + 1)
                src, n = part_words(q)
                e.activation(high[:, q % PARTS, 0:n], src, ACT.Copy).then_inc(sem["high_ready"], 1)

            def follow(q):
                p = pair_of[q]
                if q == plan.last_part[p]:
                    take_job(2 * p)
                    take_job(2 * p + 1)
                split_high(q + PARTS)

            def follow_stage(*which):
                for q in stage_parts(*which):
                    follow(q)

            def norm_stage(i, ready):
                for m in range(M):
                    e.wait_ge(sem[ready], (16 if ready == "x_in" else m + 1))
                    c = SS["x%d" % i] + m
                    e.activation(scrA[:, m, :], x[:, m, :], ACT.Square, accum_out=ss[:, c:c + 1])\
                        .then_inc(sem["ss_x%d" % i], 1)
                if i == 0:
                    for q in range(PARTS):
                        split_high(q)
                e.wait_ge(sem["gs_ready"], i + 1)
                for t in range(4):
                    w = works["x%d" % i] + t
                    e.wait_ge(sem["work_ready"], w + 1)
                    n = 4 * i + t
                    if n % 4 == 3:
                        e.wait_ge(sem["x_split"], n - 2)
                    for k in range(2):
                        f = 2 * t + k
                        ins = e.activation(whole[:, t % 3, k * S:(k + 1) * S], bank[4 + w % 2][:, k * S:(k + 1) * S],
                                           ACT.Identity, scale=gs[:, i, f:f + 1], bias=mod[:, i, 0, f:f + 1])
                    ins.then_inc(sem["turned_act"], 1)

            hidden = [0]

            def take_job(j):
                job = jobs[j]
                if job["by"] != "act":
                    return
                name, value = plan.job_done[j]
                e.wait_ge(sem[name], value)
                b, m, c0, stage = bank[j % 3], job["half"], job["c0"], job["stage"]
                n = job.get("n")
                if stage == "lat":
                    ins = e.activation(lat[:, m, :], b[:, 0:416], ACT.Copy)
                elif stage in ("q_mb", "k_mb"):
                    ins = e.activation(qk_mb[:, int(stage == "k_mb"), m, :], b[:, :], ACT.Copy,
                                       scale=HEAD_SCALE if stage == "q_mb" else 1.0)
                elif stage == "v_mb":
                    ins = e.activation(v_mb[:, m, :, :].rearrange("p h d -> p (h d)"), b[:, :], ACT.Copy)
                elif stage == "uq":
                    ins = e.activation(q_up[:, m, c0:c0 + n], b[:, 0:n], ACT.Copy, scale=MLA_SCALE)
                elif stage == "ukv":
                    h0 = c0 // P
                    src = b[:, :].rearrange("p (h d) -> p h d", d=P)
                    dst = k_up[:, m, :].rearrange("p (h d) -> p h d", d=96)
                    e.activation(dst[:, h0:h0 + 4, 0:64], src[:, :, 0:64], ACT.Copy)
                    ins = e.activation(v_mla[:, m, h0:h0 + 4, :], src[:, :, 64:128], ACT.Copy)
                elif stage in ("z_mla", "z_mb"):
                    ins = e.activation(z[stage][:, m, :], b[:, :], ACT.Copy)
                elif stage == "w_out":
                    e.activation(scrA[:, m, c0:c0 + n], b[:, 0:n], ACT.Copy).then_inc(sem["y_copied"], 1)
                    c = SS["y2"] + 2 * (c0 // 512) + m
                    ins = e.activation(scrB[:, m * D + c0:m * D + c0 + 512], b[:, 0:n], ACT.Square,
                                       accum_out=ss[:, c:c + 1])
                elif stage == "nsa_in":
                    ins = e.activation(nsa[:, m, c0:c0 + n], b[:, 0:n], ACT.Copy)
                elif stage == "diff_in":
                    ins = e.activation(dif[:, m, c0:c0 + n], b[:, 0:n], ACT.Copy)
                else:
                    h, f = hidden[0], c0 // P + 2 * m
                    hidden[0] += 1
                    if h >= 3:
                        e.wait_ge(sem["hidden"], h - 2)
                    e.activation(whole[:, h % 3, :], b[:, :], ACT.Relu).then_inc(sem["copied_act"], 1)
                    e.wait_ge(sem["copied_act"], plan.job_free[j][1])
                    e.activation(hidT[0][:, f:f + 2, :].rearrange("p a s -> p (a s)"), whole[:, h % 3, :], ACT.Square)\
                        .then_inc(sem["hidden_high"], 1)
                    return
                ins.then_inc(sem["copied_act"], 1)

            def exps(name, i):
                u, w = plan.unit0[name] + i, works[name] + i
                e.wait_ge(sem["neg_max"], u + 1)
                if u >= 4:
                    e.wait_ge(sem["pt_ready"], plan.pt_of_unit[u - 4] + 1)
                b = bank[4 + w % 2]
                e.activation(probs[:, u % 4, 0:P], b[:, 0:P], ACT.Exp, bias=neg_max[:, 2 * (u % 8):2 * (u % 8) + 1],
                             accum_out=sums[:, 2 * (u % 8):2 * (u % 8) + 1])
                e.activation(probs[:, u % 4, P:384], b[:, P:384], ACT.Exp, bias=neg_max[:, 2 * (u % 8) + 1:2 * (u % 8) + 2],
                             accum_out=sums[:, 2 * (u % 8) + 1:2 * (u % 8) + 2]).then_inc(sem["probs_ready"], 1)

            def sub_squares(h):
                e.wait_ge(sem["o_taken"], plan.pt0["diff"] + h + 1)
                for m in range(M):
                    c = SS["sub"] + 8 * (h // 4) + 4 * m + h % 4
                    ins = e.activation(scrB[:, m * D + h * P:m * D + (h + 1) * P], scrA[:, m, h * P:(h + 1) * P], ACT.Square,
                                       accum_out=ss[:, c:c + 1])
                ins.then_inc(sem["ss_sub%d" % (h // 4)], 1)

            def attention(name, heads, comps=1):
                for i in range(heads + 2):
                    if name == "diff" and i >= 5:
                        sub_squares(i - 5)
                    if i < heads:
                        for c in range(comps):
                            exps(name, comps * i + c)
                    one, two = beside_parts(name, i)
                    for q in one:
                        follow(q)
                    if name == "mla" and i == heads:
                        copied(e, "merge")
                        e.activation(scrB[:, :], act[:, 832:2880], ACT.Sigmoid).then_inc(sem["z_sig"], 1)
                    if 1 <= i <= heads:
                        t = plan.pt0[name] + i - 1
                        e.wait_ge(sem["pt_ready"], t + 1)
                        if t >= 2:
                            e.wait_ge(sem["o_ready"], t - 1)
                        e.activation(probsT[:, t % 2, :], bank[6][:, 0:384], ACT.Copy).then_inc(sem["pt_taken"], 1)
                    for q in two:
                        follow(q)

            norm_stage(0, "x_in")
            follow_stage("lat")
            e.dma_start(gate[:, 2, :], t_in["g_post"][0].partition_broadcast(P)).then_inc(sem["g_post_in"], 16)
            e.dma_start(gate[:, 0, :], t_in["b_ada"][0, 2048:3072].partition_broadcast(P)).then_inc(sem["gate_in0"], 16)
            copied(e, "lat")
            for m in range(M):
                c = SS["lat"] + m
                e.activation(scrA[:, 0, 512 * m:512 * m + 256], lat[:, m, 0:256], ACT.Square, accum_out=ss[:, c:c + 1])\
                    .then_inc(sem["ss_lat"], 1)
                e.activation(scrA[:, 0, 512 * m + 256:512 * m + 384], lat[:, m, 256:384], ACT.Square, accum_out=ss[:, c + 2:c + 3])\
                    .then_inc(sem["ss_lat"], 1)
            follow_stage("q_mb")
            e.wait_ge(sem["angles"], 1)
            e.activation(cs[:, :, :, :], trig[:, :, :, :], ACT.Sin).then_inc(sem["cos_sin"], 1)
            e.wait_ge(sem["lam_sums"], 1)
            e.activation(lam[:, 2:4], lam[:, 0:2], ACT.Exp).then_inc(sem["lam_exp"], 1)
            follow_stage("k_mb")
            high_out("latT", 0, [latT[0][:, k, :] for k in range(2)], cols[:, C_GQ:C_GQ + 2])
            high_out("latT", 1, [latT[0][:, 2, :]], cols[:, C_GKV:C_GKV + 1])
            e.dma_start(b_merge[:, :], t_in["b_merge"][0].partition_broadcast(P)).then_inc(sem["b_merge_in"], 16)
            follow_stage("v_mb")
            e.dma_start(gate[:, 1, :], t_in["b_ada_2"][0, 2048:3072].partition_broadcast(P)).then_inc(sem["gate_in1"], 16)
            for a, name in enumerate(("nsa_w_ck2_2", "nsa_w_cv2_2")):
                e.dma_start(w_c2[:, a, :], t_in[name][0]).then_inc(sem["w_c2_in"], 16)

            follow_stage("uq")
            follow_stage("ukv")
            for name, dst in (("mbqT", qT_mb), ("mbkT", kT_mb)):
                for i in range(2):
                    turn_out(name, i, plain(dst))
            attention("mb", 8)
            for i in range(8):
                turn_out("mlaT", i, plain(qk[:, 8:24, :], 96))
            attention("mla", 8)
            e.activation(merge[:, :, :].rearrange("p m n -> p (m n)"), merge[:, :, :].rearrange("p m n -> p (m n)"),
                         ACT.Sigmoid).then_inc(sem["merge_sig"], 1)
            high_tiles("uT", 0, 2, first=2)
            follow_stage("w_o_moba")
            high_tiles("uT", 2, 4, first=-2)
            follow_stage("w_o_mla")
            high_tiles("yT")
            follow_stage("w_out")

            norm_stage(1, "x_done0")
            follow_stage("nsa_in", 1024)
            follow_stage("nsa_in", 2560)
            e.wait_ge(sem["gl_biased"], 2)
            e.activation(nsa[:, :, 2560:2608], nsa[:, :, 2560:2608], ACT.Sigmoid).then_inc(sem["gl_ready"], 1)
            def key_squares(b_):
                pair_copied(e, "nsa_in", 1536 + 512 * b_)
                e.activation(k_squares[b_].rearrange("p (m n) -> p m n", m=M),
                             nsa[:, :, 1536 + 512 * b_:1792 + 512 * b_], ACT.Square).then_inc(sem["nsa_k_sq"], 1)

            follow_stage("nsa_in", 0)
            follow_stage("nsa_in", 512, 0, 2)
            for a in range(2):
                e.wait_ge(sem["work_ready"], works["hid"] + a + 1)
                if a:
                    e.wait_ge(sem["turned_dve"], plan.work_free[works["hid"]][1])
                e.activation(stat[:, 64:124], bank[4 + (works["hid"] + a) % 2][:, 0:60], ACT.Sigmoid)\
                    .then_inc(sem["hid_sig"], 1)
            follow_stage("nsa_in", 512, 2, 4)
            pair_copied(e, "nsa_in", 512)
            for m in range(M):
                e.activation(scrA[:, m, :], nsa[:, m, 0:D], ACT.Square).then_inc(sem["nsa_q_sq"], 1)
            follow_stage("nsa_in", 1536)
            key_squares(0)
            follow_stage("nsa_in", 2048, 0, 1)
            for i in range(4):
                turn_out("qcT", i, plain(qcT))
            follow_stage("nsa_in", 2048, 1, 3)
            for m in range(M):
                e.wait_ge(sem["pc_shifted"], m + 1)
                e.activation(pc[:, m, :], pc[:, m, :], ACT.Exp).then_inc(sem["pc_exp"], 1)
            follow_stage("nsa_in", 2048, 3, 4)
            key_squares(1)
            for m in range(M):
                w = works["cmpT"] + m
                e.wait_ge(sem["work_ready"], w + 1)
                e.activation(pcT[0:120, m].rearrange("p f q -> p (f q)"), bank[4 + w % 2][0:120, 0:256], ACT.Copy)\
                    .then_inc(sem["turned_act"], 1)
            for i in range(4):
                turn_out("qrT", i, plain(qrT))
            for a, name in enumerate(("sel", "win")):
                for i in range(2):
                    turn_out("kT%d" % a, i, plain(qk[:, 16 + 4 * a:20 + 4 * a, :]))
                attention(name, 16)
            high_tiles("o1T")
            follow_stage("nsa_out")
            norm_stage(2, "x_done1")
            follow_stage("mlp_in0")
            follow_stage("mlp_out0")
            norm_stage(3, "x_done2")
            for a in range(2):
                follow_stage("diff_in", D * a)
                follow_stage("diff_in", D * a + 512)
                pair_copied(e, "diff_in", D * a + 512)
                for m in range(M):
                    e.activation((scrA[:, m, :], scrB[:, m * D:(m + 1) * D])[a], dif[:, m, a * D:(a + 1) * D],
                                 ACT.Square).then_inc(sem["diff_sq"], 1)
            follow_stage("diff_in", 2048)
            for i in range(4):
                turn_out("dqT", i, plain(dqT))
            follow_stage("diff_in", 2560)
            for i in range(4):
                turn_out("dkT", i, plain(dkT))
            attention("diff", 8, comps=2)
            for h in range(5, 8):
                sub_squares(h)
            high_tiles("o2T", 0, 2, cols[:, C_SUB:C_SUB + 1])
            follow_stage("diff_out", 0, 0, 1)
            high_tiles("o2T", 2, 4, cols[:, C_SUB:C_SUB + 1])
            follow_stage("diff_out", 0, 1, 4)
            follow_stage("diff_out", 512)
            norm_stage(4, "x_done3")
            follow_stage("mlp_in1")
            follow_stage("mlp_out1")

        @block.gpsimd
        def _(pool):
            e = pool
            chain = Chain(e, "pool_chain")
            chain(e.memset(ident[:, :], 0.0))
            chain(e.affine_select(out=ident[:, :], in_=ident[:, :], compare_op=ALU.not_equal, fill=1.0, base=0,
                                  pattern=[[-1, P]], channel_multiplier=1))
            e.memset(ones[:, :], 1.0).then_inc(sem["const_ready"], 1)
            chain(e.memset(half_neg[:, :], -0.5))
            chain(e.memset(causal[:, :], 0.0))
            chain(e.affine_select(out=causal[:, :], in_=causal[:, :], compare_op=ALU.is_ge, fill=NEG, base=0,
                                  pattern=[[-1, P]], channel_multiplier=1))
            for buf, inside, outside in ((cmp_neg, 0.0, NEG), (cmp_keep, 1.0, 0.0)):
                chain(e.memset(buf[:, :, :], inside))
                chain(e.affine_select(out=buf[:, :, :], in_=buf[:, :, :], compare_op=ALU.is_ge, fill=outside,
                                      base=-31, pattern=[[P, M], [-16, 15]], channel_multiplier=1))
            chain(e.memset(own[:, :], 1.0))
            chain(e.affine_select(out=own[:, :], in_=own[:, :], compare_op=ALU.is_ge, fill=0.0, base=0,
                                  pattern=[[-15, 8]], channel_multiplier=1))
            chain(e.affine_select(out=own[:, :], in_=own[:, :], compare_op=ALU.is_ge, fill=0.0, base=14,
                                  pattern=[[15, 8]], channel_multiplier=-1))
            e.memset(stat[:, 127:128], 0.0).then_inc(sem["masks_ready"], 1)
            def split_low(q):
                if q < len(plan.parts) and plan.low_by[q] == "pool":
                    e.wait_ge(sem["high_ready"], q + 1)
                    src, n = part_words(q)
                    e.tensor_tensor(low[:, q % PARTS, 0:n], src, high[:, q % PARTS, 0:n].bitcast(F32), ALU.subtract)\
                        .then_inc(sem["low_ready_pool"], 1)

            def follow_pairs(stage, keys):
                for key in keys:
                    for q in stage_parts(stage, key):
                        split_low(q + PARTS)

            def follow_stage(*stages):
                for q in range(len(plan.parts)):
                    if jobs[2 * pair_of[q]]["stage"] in stages:
                        split_low(q + PARTS)

            def root(name, groups, count, p=P):
                if count is not None:
                    e.wait_ge(sem["ss_" + name], count)
                for c, n, elements in groups:
                    chain(e.tensor_scalar(rstd[0:p, c:c + n], ss[0:p, c:c + n], 1.0 / elements, EPS, ALU.mult, ALU.add))
                for g, (c, n, _) in enumerate(groups):
                    e.tensor_tensor(rstd[0:p, c:c + n], rstd[0:p, c:c + n], half_neg[0:p, 0:n], ALU.pow)\
                        .then_inc(sem["rs_" + name], 1)

            root("x0", [(SS["x0"], 2, D)], 2)
            for o, name in enumerate(("positions", "positions_2")):
                e.dma_start(pos_i[:, o, :], t_in[name][0].rearrange("(m p) -> p m", p=P),
                            allow_slow_non_contiguous=True).then_inc(sem["tiny_in"], 16)
            for dst, src in ((q_gain, t_in["nsa_q_gain_2"][0]), (tiny[:, 64:256], t_in["nsa_k_gain_2"].rearrange("l a d -> (l a d)")),
                             (dq_gain, t_in["diff_q_gain_2"][0]), (dk_gain, t_in["diff_k_gain_2"][0]),
                             (b_gate, t_in["nsa_b_gate_2"][0]),
                             (lqk[:, 0, :], t_in["diff_lq1_2"][0]), (lqk[:, 1, :], t_in["diff_lk1_2"][0]),
                             (lqk[:, 2, :], t_in["diff_lq2_2"][0]), (lqk[:, 3, :], t_in["diff_lk2_2"][0]),
                             (inv_freq, t_in["inv_freq"])):
                e.dma_start(dst, src.partition_broadcast(P)).then_inc(sem["tiny_in"], 16)

            for q in range(PARTS):
                split_low(q)
            follow_stage("lat")
            root("lat", [(SS["lat"], 2, 256), (SS["lat"] + 2, 2, 128)], 4)
            follow_stage("q_mb", "k_mb", "v_mb", "uq", "ukv", "z_mla", "z_mb", "merge")
            e.wait_ge(sem["gg_ready"], 1)
            e.dma_start(gate[:, 2, :], t_in["b_ada_2"][0, 5120:6144].partition_broadcast(P)).then_inc(sem["gate_in2"], 16)
            follow_stage("w_o_moba", "w_o_mla", "w_out")
            copied(e, "w_out")
            c = SS["y2"]
            chain(e.tensor_tensor(ss[:, SS["y"]:SS["y"] + 2], ss[:, c:c + 2], ss[:, c + 2:c + 4], ALU.add))
            root("y", [(SS["y"], 2, D)], None)
            e.wait_ge(sem["x_done0"], 2)
            e.dma_start(gate[:, 0, :], t_in["b_ada_2"][1, 2048:3072].partition_broadcast(P)).then_inc(sem["gate_in3"], 16)
            root("x1", [(SS["x1"], 2, D)], 2)
            turned(e, "yT")
            for a, name in enumerate(("ck1", "cv1")):
                e.dma_start(w_c1[a], weights[name]).then_inc(sem["w_c1_in%d" % a], 16)
            follow_pairs("nsa_in", (1024, 2560, 0, 512))
            root("kc", [(SS["kc"], 1, 64)], 1, 60)
            root("nsa_q", [(SS["nsa"], 32, 64)], 2)
            follow_pairs("nsa_in", (1536,))
            for q in stage_parts("nsa_in", 2048, 0, 1):
                split_low(q + PARTS)
            root("nsa_k0", [(SS["nsa"] + 32, 8, 64)], 1)
            for q in stage_parts("nsa_in", 2048, 1, 4):
                split_low(q + PARTS)
            root("nsa_k1", [(SS["nsa"] + 40, 8, 64)], 1)
            e.wait_ge(sem["ada_used"], 2 * ATT_PIECES[0])
            for n in ATT_PIECES:
                for k in range(DT):
                    multiply_tile(e, chain, n, k)
            follow_stage("nsa_out")
            e.wait_ge(sem["x_done1"], 2)
            e.dma_start(gate[:, 1, :], t_in["b_ada_2"][1, 5120:6144].partition_broadcast(P)).then_inc(sem["gate_in4"], 16)

            def square_hidden(layer):
                for i in range(16 * layer, 16 * layer + 16):
                    f = 2 * (i % 16)
                    e.wait_ge(sem["hidden_high"], i + 1)
                    v = whole[:, i % 3, :]
                    chain(e.tensor_tensor(v, v, v, ALU.mult))
                    e.tensor_tensor(hidT[1][:, f:f + 2, :].rearrange("p a s -> p (a s)"), v,
                                    hidT[0][:, f:f + 2, :].bitcast(F32).rearrange("p a s -> p (a s)"), ALU.subtract)\
                        .then_inc(sem["hidden"], 1)

            root("x2", [(SS["x2"], 2, D)], 2)
            square_hidden(0)
            follow_stage("mlp_in0", "mlp_out0")
            root("x3", [(SS["x3"], 2, D)], 2)
            for a in range(2):
                follow_pairs("diff_in", (D * a, D * a + 512))
                root("diff%d" % a, [(SS["diff"] + 32 * a, 32, 64)], 2)
            follow_pairs("diff_in", (2048, 2560))
            for half_ in range(2):
                root("sub%d" % half_, [(SS["sub"] + 8 * half_, 8, P)], 4)
            follow_stage("diff_out")
            root("x4", [(SS["x4"], 2, D)], 2)
            square_hidden(1)
            follow_stage("mlp_in1", "mlp_out1")

        @block.vector
        def _(dve):
            e = dve
            chain = Chain(e, "dve_chain")

            e.wait_ge(sem["work_ready"], 1)
            e.tensor_copy(cols[:, 0:108], bank[4][:, 0:108])
            e.tensor_copy(cols[:, 128:192], bank[4][:, 128:192]).then_inc(sem["turned_dve"], 1)
            e.wait_ge(sem["turned_dve"], 1)
            sub = cols[:, C_SUB:C_SUB + 1]
            chain(e.tensor_scalar(sub, sub, 1.0 - LAM_INIT, None, ALU.mult))
            e.wait_ge(sem["sig_c"], 1)
            chain(e.tensor_tensor(silu_c[:, :], stat[:, 0:16], cols[:, 0:16], ALU.mult))

            def ada_tile(n, k):
                if k == 0 and n == ATT_PIECES[-1] + 1:
                    e.wait_ge(sem["ada_used"], 2 * n)
                multiply_tile(e, chain, n, k)

            def half_piece(h):
                for k in range(4):
                    ada_tile(h // 2, 4 * (h % 2) + k)

            def piece_end(n):
                e.wait_ge(sem["piece_summed"], n + 1)
                use = piece_use(n)
                if use[0] == "col":
                    _, norm, part, c0, b0 = use
                    e.tensor_tensor(mod[:, norm, part, c0:c0 + 4], bank[3][:, 0:4], cols[:, b0:b0 + 4], ALU.add)\
                        .then_inc(sem["mod_taken"], 1)
                else:
                    g = 0 if n < 6 else 1 + (n - 6) // 12 * 2 + ((n - 6) % 12) // 6
                    e.wait_ge(sem["gate_in%d" % g], 16)
                    dst = gate[:, use[1], use[2]:use[2] + 512]
                    e.tensor_tensor(dst, bank[3][:, :], dst, ALU.add).then_inc(sem["mod_taken"], 1)
                if n == 5:
                    e.wait_ge(sem["mod_taken"], 6)
                    e.wait_ge(sem["g_post_in"], 16)
                    e.tensor_tensor(gate[:, 0, :], gate[:, 0, :], gate[:, 2, :], ALU.mult).then_inc(sem["gg_ready"], 1)

            def turn_out(stage, i, put):
                w = works[stage] + i
                if w % 2 == 1:
                    e.wait_ge(sem["work_ready"], w + 1)
                    put(i, bank[5]).then_inc(sem["turned_dve"], 1)

            def plain(dst, rows=P):
                def put(i, b):
                    return e.tensor_copy(dst[0:rows, 2 * i:2 * i + 2, :].rearrange("p a s -> p (a s)"), b[0:rows, :])
                return put

            GAIN = [C_PRE, C_MIX, C_MLP, C_MIX + 8, C_MLP + 8]
            LAST_PIECE = [4, 10, 16, 22, 28]

            def scale_rows(i):
                e.wait_ge(sem["rs_x%d" % i], 1)
                for m in range(M):
                    c = SS["x%d" % i] + m
                    e.tensor_scalar(scrA[:, m, :], x[:, m, :], rstd[:, c:c + 1], None, ALU.mult)\
                        .then_inc(sem["xs_ready%d" % i], 1)

            def norm_stage(i):
                e.wait_ge(sem["mod_taken"], LAST_PIECE[i])
                e.scalar_tensor_tensor(out=gs[:, i, :], in0=mod[:, i, 1, :], scalar=1.0,
                                       in1=cols[:, GAIN[i]:GAIN[i] + 8], op0=ALU.add, op1=ALU.mult)\
                    .then_inc(sem["gs_ready"], 1)
                if i:
                    scale_rows(i)
                if i == 0:
                    for q in range(PARTS):
                        split_low(q)
                for t in range(4):
                    w = works["x%d" % i] + t
                    e.wait_ge(sem["turned_act"], plan.work_free[w][1])
                    hi = hT[0][:, 2 * t:2 * t + 2, :].rearrange("p a s -> p (a s)")
                    chain(e.tensor_copy(hi, whole[:, t % 3, :]))
                    e.tensor_tensor(hT[1][:, 2 * t:2 * t + 2, :].rearrange("p a s -> p (a s)"), whole[:, t % 3, :],
                                    hT[0][:, 2 * t:2 * t + 2, :].bitcast(F32).rearrange("p a s -> p (a s)"),
                                    ALU.subtract).then_inc(sem["x_split"], 1)

            turned_low = [0]

            def low_out(stage, i, lows, highs, scale=None):
                w = works[stage] + i
                turned_low[0] += 1
                e.wait_ge(sem["turned_high"], turned_low[0])
                b = bank[4 + w % 2]
                for k, (lo, hi) in enumerate(zip(lows, highs)):
                    n = hi.shape[-1]
                    src = b[:, k * n:(k + 1) * n]
                    if scale is None:
                        ins = e.tensor_tensor(lo, src, hi, ALU.subtract)
                    else:
                        ins = e.scalar_tensor_tensor(out=lo, in0=src, scalar=scale[:, k:k + 1], in1=hi, op0=ALU.mult,
                                                     op1=ALU.subtract)
                ins.then_inc(sem["turned_dve"], 1)

            def low_tiles(stage, a=0, b=4, scale=None, first=0):
                for i in range(a, b):
                    t = 2 * (first + i)
                    low_out(stage, i, [hT[1][:, t:t + 2, :].rearrange("p a s -> p (a s)")],
                            [hT[0][:, t:t + 2, :].bitcast(F32).rearrange("p a s -> p (a s)")], scale)

            def split_low(q):
                if q >= len(plan.parts) or plan.low_by[q] != "dve":
                    return
                e.wait_ge(sem["high_ready"], q + 1)
                src, n = part_words(q)
                e.tensor_tensor(low[:, q % PARTS, 0:n], src, high[:, q % PARTS, 0:n].bitcast(F32), ALU.subtract)\
                    .then_inc(sem["low_ready_dve"], 1)

            def follow(q):
                p = pair_of[q]
                if q == plan.last_part[p]:
                    take_job(2 * p)
                    take_job(2 * p + 1)
                split_low(q + PARTS)
                for h, at in plan.half_after.items():
                    if at == q and h // 2 not in ATT_PIECES:
                        half_piece(h)
                for n in plan.piece_end.get(q, []):
                    piece_end(n)

            def follow_stage(*which):
                for q in stage_parts(*which):
                    follow(q)

            def rope(x1, x2, c, s, o1, o2, tmp):
                e.tensor_tensor(tmp[0], x1, c, ALU.mult)
                e.tensor_tensor(tmp[1], x2, s, ALU.mult)
                e.tensor_tensor(tmp[2], x2, c, ALU.mult)
                chain(e.tensor_tensor(tmp[3], x1, s, ALU.mult))
                e.tensor_tensor(o1, tmp[0], tmp[1], ALU.subtract)
                return e.tensor_tensor(o2, tmp[2], tmp[3], ALU.add)

            def angles(kind, a, b, heads):
                return cs[:, :, kind, a:b].unsqueeze(2).to_broadcast([P, M, heads, b - a])

            def take_job(j):
                job = jobs[j]
                if job["stage"] == "w_out":
                    m, c0 = job["half"], job["c0"]
                    e.wait_ge(sem["y_copied"], 2 * (c0 // 512) + m + 1)
                    e.tensor_tensor(y_gated[:, m, c0:c0 + 512], scrA[:, m, c0:c0 + 512], gate[:, 0, c0:c0 + 512],
                                    ALU.mult).then_inc(sem["y_gated"], 1)
                if job["by"] == "dve":
                    b, m, c0, stage = bank[j % 3], job["half"], job["c0"], job["stage"]
                    name, value = plan.job_done[j]
                    e.wait_ge(sem[name], value)
                    t = scrB[:, D + (j % 2) * 512:D + (j % 2) * 512 + 512]
                    if stage == "merge":
                        e.wait_ge(sem["b_merge_in"], 16)
                        e.tensor_tensor(merge[:, m, c0:c0 + 512], b[:, :], b_merge[:, c0:c0 + 512], ALU.add)\
                            .then_inc(sem["copied_dve"], 1)
                    elif stage == "w_o_moba":
                        e.wait_ge(sem["merge_sig"], 1)
                        e.tensor_tensor(y_rows[:, m, c0:c0 + 512], b[:, :], merge[:, m, D + c0:D + c0 + 512], ALU.mult)\
                            .then_inc(sem["copied_dve"], 1)
                    elif stage == "w_o_mla":
                        e.tensor_tensor(t, b[:, :], merge[:, m, c0:c0 + 512], ALU.mult)\
                            .then_inc(sem["copied_dve"], 1)
                        e.wait_ge(sem["copied_dve"], plan.job_free[j][1])
                        y = y_rows[:, m, c0:c0 + 512]
                        e.tensor_tensor(y, y, t, ALU.add).then_inc(sem["y_ready"], 1)
                    else:
                        k = {"nsa_out": 1, "mlp_out0": 2, "diff_out": 3, "mlp_out1": 4}[stage]
                        g = gate[:, k % 3, c0:c0 + 512]
                        e.tensor_tensor(t, b[:, :], g, ALU.mult).then_inc(sem["copied_dve"], 1)
                        e.wait_ge(sem["copied_dve"], plan.job_free[j][1])
                        r = x[:, m, c0:c0 + 512]
                        ins = e.tensor_tensor(r, r, t, ALU.add)
                        if c0 == 512:
                            ins.then_inc(sem["x_done%d" % k], 1)

            def maxima(name, i):
                u, w = plan.unit0[name] + i, works[name] + i
                b = bank[4 + w % 2]
                e.wait_ge(sem["work_ready"], w + 1)
                e.tensor_reduce(neg_max[:, 2 * (u % 8):2 * (u % 8) + 1], b[:, 0:P], AX.X, ALU.max, negate=True)
                e.tensor_reduce(neg_max[:, 2 * (u % 8) + 1:2 * (u % 8) + 2], b[:, P:384], AX.X, ALU.max, negate=True)\
                    .then_inc(sem["neg_max"], 1)

            def outputs(name, i):
                t = plan.pt0[name] + i
                u = plan.unit0[name] + i
                r = (t % 2) * 256
                if name == "diff":
                    e.wait_ge(sem["o_ready"], t + 1)
                    o = bank[7][:, r:r + 256].rearrange("p (m d) -> p m d", m=M)
                    e.tensor_copy(scrA[:, :, i * P:(i + 1) * P], o).then_inc(sem["o_taken"], 1)
                    return
                e.wait_ge(sem["probs_ready"], u + 1)
                chain(e.reciprocal(inv[:, 2 * (u % 8):2 * (u % 8) + 2], sums[:, 2 * (u % 8):2 * (u % 8) + 2]))
                if name in ("sel", "win"):
                    g = nsa[:, :, 2560 + 3 * i + (1 if name == "sel" else 2)]
                    chain(e.tensor_tensor(inv[:, 2 * (u % 8):2 * (u % 8) + 2], inv[:, 2 * (u % 8):2 * (u % 8) + 2], g, ALU.mult))
                e.wait_ge(sem["o_ready"], t + 1)
                o = bank[7][:, r:r + P].rearrange("p (m d) -> p m d", m=M)
                w = inv[:, 2 * (u % 8):2 * (u % 8) + 2].unsqueeze(2).to_broadcast([P, M, 64])
                if name in ("mb", "mla"):
                    dst = o_blk[:, int(name == "mb"), :, 64 * i:64 * i + 64]
                    e.tensor_tensor(dst, o, w, ALU.mult).then_inc(sem["o_taken"], 1)
                else:
                    tmp = o_tmp[:, t % 2, :, :]
                    e.tensor_tensor(tmp, o, w, ALU.mult).then_inc(sem["o_taken"], 1)
                    e.wait_ge(sem["o_taken"], t + 1)
                    dst = scrA[:, :, 64 * i:64 * i + 64]
                    chain(e.tensor_tensor(dst, dst, tmp, ALU.add))

            def mla_rope_q():
                copied(e, "uq")
                tmp = [mla_tmp[:, i, 0:256].rearrange("p (m h d) -> p m h d", m=M, h=8) for i in range(4)]
                v = q_up.rearrange("p m (h d) -> p m h d", d=96)
                chain(rope(v[:, :, :, 64:80], v[:, :, :, 80:96], angles(0, 0, 16, 8), angles(1, 0, 16, 8),
                           v[:, :, :, 64:80], v[:, :, :, 80:96], tmp))

            def mla_rope_k():
                tmp = [mla_tmp[:, i, 0:32].rearrange("p (m d) -> p m d", m=M) for i in range(4)]
                r1, r2, c_, s_ = lat[:, :, 384:400], lat[:, :, 400:416], cs[:, :, 0, 0:16], cs[:, :, 1, 0:16]
                for t_, (a_, b_) in zip(tmp, ((r1, c_), (r2, s_), (r2, c_), (r1, s_))):
                    chain(e.tensor_tensor(t_, a_, b_, ALU.mult))
                wide = [t_.unsqueeze(2).to_broadcast([P, M, 8, 16]) for t_ in tmp]
                v = k_up.rearrange("p m (h d) -> p m h d", d=96)
                chain(e.tensor_tensor(v[:, :, :, 64:80], wide[0], wide[1], ALU.subtract))
                copied(e, "ukv")
                e.tensor_tensor(v[:, :, :, 80:96], wide[2], wide[3], ALU.add).then_inc(sem["mla_roped"], 1)

            def gated(name):
                a = ("z_mla", "z_mb").index(name)
                e.wait_ge(sem["z_sig"], 1)
                e.wait_ge(sem["o_taken"], plan.pt0["mla" if a else "sel"])
                v = act[:, 832 + D * a:832 + D * (a + 1)]
                chain(e.tensor_tensor(v, v, scrB[:, D * a:D * (a + 1)], ALU.mult))
                o = o_blk[:, a]
                e.tensor_tensor(o, o, z[name], ALU.mult).then_inc(sem["u_ready"], 1)

            def mix(i):
                u = plan.unit0["diff"] + 2 * i
                e.wait_ge(sem["probs_ready"], u + 2)
                chain(e.reciprocal(inv[:, 2 * (u % 8):2 * (u % 8) + 4], sums[:, 2 * (u % 8):2 * (u % 8) + 4]))
                chain(e.tensor_scalar(inv[:, 2 * (u % 8) + 2:2 * (u % 8) + 4], inv[:, 2 * (u % 8) + 2:2 * (u % 8) + 4], lam[:, 5:6], None, ALU.mult))
                for m, (a, b) in enumerate(((0, P), (P, 384))):
                    p1 = probs[:, (u + 1) % 4, a:b]
                    ins = e.tensor_scalar(p1, p1, inv[:, 2 * (u % 8) + 2 + m:2 * (u % 8) + 3 + m], None, ALU.mult)
                chain(ins)
                for m, (a, b) in enumerate(((0, P), (P, 384))):
                    p0 = probs[:, u % 4, a:b]
                    ins = e.scalar_tensor_tensor(out=p0, in0=p0, scalar=inv[:, 2 * (u % 8) + m:2 * (u % 8) + m + 1],
                                                 in1=probs[:, (u + 1) % 4, a:b], op0=ALU.mult, op1=ALU.add)
                ins.then_inc(sem["diff_mixed"], 1)

            def norm_heads(half_):
                e.wait_ge(sem["rs_sub%d" % half_], 1)
                v = scrA[:, :, 512 * half_:512 * half_ + 512].rearrange("p m (h d) -> p m h d", d=P)
                c = SS["sub"] + 8 * half_
                r = rstd[:, c:c + 8].rearrange("p (m h) -> p m h", m=M).unsqueeze(3).to_broadcast([P, M, 4, P])
                e.tensor_tensor(v, v, r, ALU.mult).then_inc(sem["d_rows_done"], 1)

            def attention(name, heads, comps=1):
                for i in range(heads + 2):
                    if name == "diff" and i == 9:
                        norm_heads(0)
                    if i < heads:
                        for c in range(comps):
                            maxima(name, comps * i + c)
                        if comps == 2:
                            mix(i)
                    one, two = beside_parts(name, i)
                    for q in one + two:
                        follow(q)
                    if name == "sel" and i in (2, 4, 6):
                        {2: key_norm, 4: key_rope, 6: key_double}[i](1)
                    if name == "mb" and i in (2, 5):
                        (mla_rope_q if i == 2 else mla_rope_k)()
                    if name in ("sel", "win") and i < heads:
                        n, k = ATT_PIECES[0] + (i + heads * (name == "win")) // DT, i % DT
                        if k == 5 and n > ATT_PIECES[0]:
                            piece_end(n - 1)
                    if i >= 2:
                        outputs(name, i - 2)

            e.wait_ge(sem["masks_ready"], 1)
            for n in range(4):
                half_piece(2 * n)
                half_piece(2 * n + 1)
                if n == 2:
                    scale_rows(0)
                if n:
                    piece_end(n - 1)
            piece_end(3)
            norm_stage(0)
            follow_stage("lat")
            e.wait_ge(sem["rs_lat"], 2)
            for m in range(M):
                c = SS["lat"] + m
                chain(e.tensor_scalar(lat[:, m, 0:256], lat[:, m, 0:256], rstd[:, c:c + 1], None, ALU.mult))
                ins = e.tensor_scalar(lat[:, m, 256:384], lat[:, m, 256:384], rstd[:, c + 2:c + 3], None, ALU.mult)
                if m:
                    ins.then_inc(sem["lat_normed"], 1)
                else:
                    chain(ins)
            e.wait_ge(sem["tiny_in"], 16 * 12)
            chain(e.tensor_copy(pos_f[:, :, :], pos_i[:, :, :]))
            for m in range(M):
                for o, (a, b) in enumerate(((0, 48), (48, 56))):
                    for kind in range(2):
                        chain(e.tensor_scalar(trig[:, m, kind, a:b], inv_freq[:, a:b], pos_f[:, o, m:m + 1], None, ALU.mult))
            TURN = 2 * math.pi
            C1, C2 = 6.28125, 2029 / 2 ** 20
            C3 = TURN - C1 - C2
            MAGIC = 1.5 * 2 ** 23
            turns = cs
            for kind, quarter in ((0, 0.25), (1, 0.0)):
                chain(e.tensor_scalar(turns[:, :, kind, :], trig[:, :, kind, :], 1 / TURN, quarter, ALU.mult, ALU.add))
            chain(e.tensor_scalar(turns[:, :, :, :], turns[:, :, :, :], MAGIC, None, ALU.add))
            chain(e.tensor_scalar(turns[:, :, :, :], turns[:, :, :, :], -MAGIC, None, ALU.add))
            for c in (C1, C2, C3):
                chain(e.scalar_tensor_tensor(out=trig[:, :, :, :], in0=turns[:, :, :, :], scalar=-c,
                                             in1=trig[:, :, :, :], op0=ALU.mult, op1=ALU.add))
            chain(e.tensor_scalar(trig[:, :, 0, :], trig[:, :, 0, :], math.pi / 2, None, ALU.add))
            LIMIT = 3.1415925
            e.tensor_scalar(trig[:, :, :, :], trig[:, :, :, :], LIMIT, -LIMIT, ALU.min, ALU.max)\
                .then_inc(sem["angles"], 1)
            chain(e.tensor_tensor(lam_tmp[:, :, :], lqk[:, 0:4:2, :], lqk[:, 1:4:2, :], ALU.mult))
            e.tensor_reduce(lam[:, 0:2], lam_tmp[:, :, :], AX.X, ALU.add).then_inc(sem["lam_sums"], 1)
            chain(e.tensor_scalar(q_gain, q_gain, HEAD_SCALE, None, ALU.mult))
            chain(e.tensor_scalar(dq_gain, dq_gain, HEAD_SCALE, None, ALU.mult))
            def mb_rope(a, stage):
                copied(e, stage)
                v = qk_mb[:, a].rearrange("p m (h d) -> p m h d", d=64)
                tmp = [rope_tmp[:, i, :].rearrange("p (m h d) -> p m h d", m=M, h=8) for i in range(4)]
                rope(v[:, :, :, 0:32], v[:, :, :, 32:64], angles(0, 16, 48, 8), angles(1, 16, 48, 8),
                     v[:, :, :, 0:32], v[:, :, :, 32:64], tmp).then_inc(sem["mb_roped"], 1)
                e.wait_ge(sem["mb_roped"], a + 1)

            follow_stage("q_mb")
            follow_stage("k_mb", 0, 0, 2)
            e.wait_ge(sem["cos_sin"], 1)
            mb_rope(0, "q_mb")
            follow_stage("k_mb", 0, 2, 4)
            for i, (k0, nk, g) in enumerate(((0, 2, C_GQ), (2, 1, C_GKV))):
                low_out("latT", i, [latT[1][:, k, :] for k in range(k0, k0 + nk)],
                        [latT[0][:, k, :].bitcast(F32) for k in range(k0, k0 + nk)], cols[:, g:g + nk])
            follow_stage("v_mb", 0, 0, 2)
            mb_rope(1, "k_mb")
            e.wait_ge(sem["lam_exp"], 1)
            chain(e.tensor_tensor(lam[:, 4:5], lam[:, 2:3], lam[:, 3:4], ALU.subtract))
            chain(e.tensor_scalar(lam[:, 5:6], lam[:, 4:5], LAM_INIT, -1.0, ALU.add, ALU.mult))
            follow_stage("v_mb", 0, 2, 4)
            follow_stage("uq")
            follow_stage("ukv")
            for name, dst in (("mbqT", qT_mb), ("mbkT", kT_mb)):
                for i in range(2):
                    turn_out(name, i, plain(dst))
            attention("mb", 8)
            for i in range(8):
                turn_out("mlaT", i, plain(qk[:, 8:24, :], 96))
            attention("mla", 8)
            gated("z_mb")
            low_tiles("uT", 0, 2, first=2)
            follow_stage("w_o_moba")
            gated("z_mla")
            low_tiles("uT", 2, 4, first=-2)
            follow_stage("w_o_mla")
            low_tiles("yT")
            follow_stage("w_out")
            e.wait_ge(sem["rs_y"], 1)
            e.wait_ge(sem["y_gated"], 4)
            e.wait_ge(sem["x_in"], 16)
            for m in range(M):
                c = SS["y"] + m
                e.scalar_tensor_tensor(out=x[:, m, :], in0=y_gated[:, m, :], scalar=rstd[:, c:c + 1],
                                       in1=x[:, m, :], op0=ALU.mult, op1=ALU.add).then_inc(sem["x_done0"], 1)

            norm_stage(1)
            def scale_heads(v, c, heads, gain):
                r = rstd[:, c:c + heads].unsqueeze(2).to_broadcast([P, heads, 64])
                chain(e.tensor_tensor(v, v, r, ALU.mult))
                return e.tensor_tensor(v, v, gain.unsqueeze(1).to_broadcast([P, heads, 64]), ALU.mult)

            def hidden_cmp(a):
                w = works["hid"] + a
                e.wait_ge(sem["hid_sig"], a + 1)
                e.tensor_tensor(hid[:, a, :], bank[4 + w % 2][:, 0:60], stat[:, 64:124], ALU.mult)\
                    .then_inc(sem["turned_dve"], 1)
                e.wait_ge(sem["turned_dve"], plan.work_free[w][1])

            follow_stage("nsa_in", 1024)
            pair_copied(e, "nsa_in", 1024)
            for m in range(M):
                for c in range(2):
                    ins = e.tensor_copy(kv_dup[:, m, :, :, c, :].rearrange("p a g d -> p (a g) d"),
                                        nsa[:, m, 1024:1536].rearrange("p (b d) -> p b d", d=64))
            ins.then_inc(sem["kv_doubled"], 1)
            follow_stage("nsa_in", 2560)
            pair_copied(e, "nsa_in", 2560)
            for m in range(M):
                gl = nsa[:, m, 2560:2608]
                e.tensor_tensor(gl, gl, b_gate, ALU.add).then_inc(sem["gl_biased"], 1)
            def key_sums(b_):
                e.wait_ge(sem["nsa_k_sq"], b_ + 1)
                c = SS["nsa"] + 32 + 8 * b_
                e.tensor_reduce(ss[:, c:c + 8], k_squares[b_].rearrange("p (h d) -> p h d", d=64), AX.X, ALU.add)\
                    .then_inc(sem["ss_nsa_k%d" % b_], 1)

            def keys_of(b_):
                k0 = 1536 + 512 * b_
                return nsa[:, :, k0:k0 + 256].rearrange("p m (h d) -> p m h d", d=64)

            def key_norm(b_):
                e.wait_ge(sem["rs_nsa_k%d" % b_], 1)
                v, c = keys_of(b_), SS["nsa"] + 32 + 8 * b_
                r = rstd[:, c:c + 8].rearrange("p (m h) -> p m h", m=M).unsqueeze(3).to_broadcast([P, M, 4, 64])
                chain(e.tensor_tensor(v, v, r, ALU.mult))
                chain(e.tensor_tensor(v, v, k_gain[:, 1 + b_, :].unsqueeze(1).unsqueeze(1).to_broadcast([P, M, 4, 64]),
                                      ALU.mult))

            def key_rope(b_):
                v = keys_of(b_)
                t = (scrA[:, 0, 0:256], scrB[:, 512:768])[b_]
                tmp = [t[:, 64 * i:64 * i + 64].rearrange("p (m h d) -> p m h d", m=M, h=4) for i in range(4)]
                chain(rope(v[:, :, :, 0:8], v[:, :, :, 8:16], angles(0, 48, 56, 4), angles(1, 48, 56, 4),
                           v[:, :, :, 0:8], v[:, :, :, 8:16], tmp))

            def key_double(b_):
                v = keys_of(b_)
                for c_ in range(2):
                    ins = e.tensor_copy(k_dup[:, :, b_, :, c_, :], v)
                ins.then_inc(sem["k_doubled"], 1)

            follow_stage("nsa_in", 0, 0, 3)
            for i in range(4):
                w = works["cmpin"] + i
                a, g0 = i // 2, 2 * (i % 2)
                e.wait_ge(sem["work_ready"], w + 1)
                for half_ in range(2):
                    lo = 64 * half_
                    src = bank[4 + w % 2][lo:lo + 64, :].rearrange("p (g i t c) -> p g i t c", g=2, i=16, c=2)[:, :, :, :, half_]
                    for h in range(2):
                        for g in range(2):
                            pe0 = (C_PEK, C_PEV)[a] + 8 * h
                            pos = cols[lo:lo + 64, pe0:pe0 + 8].unsqueeze(1).to_broadcast([64, 16, 8])
                            ins = e.tensor_tensor(z_blk[lo:lo + 64, a, h, g0 + g], src[:, g], pos, ALU.add)
                ins.then_inc(sem["turned_dve"], 1)
            follow_stage("nsa_in", 0, 3, 4)
            follow_stage("nsa_in", 512, 0, 2)
            hidden_cmp(0)
            hidden_cmp(1)
            for f in range(2):
                src = hid[:, 1, 30 * f:30 * f + 30].rearrange("p (g c) -> p g c", g=2)
                ins = e.tensor_copy(hid_rep[:, f], src.unsqueeze(2).to_broadcast([P, 2, 4, 15]))
            ins.then_inc(sem["hid_ready"], 1)
            follow_stage("nsa_in", 512, 2, 3)
            w = works["kv_cmp"]
            e.wait_ge(sem["work_ready"], w + 1)
            e.tensor_copy(k_cmp[0:60, :], bank[4 + w % 2][0:60, 0:64]).then_inc(sem["turned_dve"], 1)
            e.wait_ge(sem["turned_dve"], plan.work_free[w][1])
            chain(e.tensor_tensor(k_cmp2[0:60, 0, :], k_cmp[0:60, :], k_cmp[0:60, :], ALU.mult))
            c = SS["kc"]
            e.tensor_reduce(ss[0:60, c:c + 1], k_cmp2[0:60, 0, :], AX.X, ALU.add).then_inc(sem["ss_kc"], 1)
            w = works["kv_cmp"] + 1
            e.wait_ge(sem["work_ready"], w + 1)
            for f in range(2):
                src = bank[4 + w % 2][0:120, 64 * f:64 * f + 64].unsqueeze(1).to_broadcast([120, 8, 64])
                ins = e.tensor_tensor(blockV[0:120, f], src, own[:, :].unsqueeze(2).to_broadcast([120, 8, 64]), ALU.mult)
            ins.then_inc(sem["turned_dve"], 1)
            follow_stage("nsa_in", 512, 3, 4)
            for m in range(M):
                e.wait_ge(sem["nsa_q_sq"], m + 1)
                c = SS["nsa"] + 16 * m
                e.tensor_reduce(ss[:, c:c + 16], scrA[:, m, :].rearrange("p (h d) -> p h d", d=64), AX.X, ALU.add)\
                    .then_inc(sem["ss_nsa_q"], 1)
            follow_stage("nsa_in", 1536, 0, 2)
            e.wait_ge(sem["rs_kc"], 1)
            for a in range(2):
                ins = e.scalar_tensor_tensor(out=k_cmp2[0:60, a, :], in0=k_cmp[0:60, :], scalar=rstd[0:60, SS["kc"]:SS["kc"] + 1],
                                             in1=k_gain[0:60, 0, :], op0=ALU.mult, op1=ALU.mult)
            ins.then_inc(sem["k_cmp_ready"], 1)
            e.wait_ge(sem["rs_nsa_q"], 1)
            for m in range(M):
                ins = scale_heads(nsa[:, m, 0:D].rearrange("p (h d) -> p h d", d=64), SS["nsa"] + 16 * m, 16, q_gain)
                if m:
                    ins.then_inc(sem["q_normed"], 1)
                else:
                    chain(ins)
            follow_stage("nsa_in", 1536, 2, 3)
            w = works["kcT"]
            e.wait_ge(sem["work_ready"], w + 1)
            e.tensor_copy(kcT[:, :], bank[4 + w % 2][:, 0:60]).then_inc(sem["turned_dve"], 1)
            follow_stage("nsa_in", 1536, 3, 4)
            key_sums(0)
            follow_stage("nsa_in", 2048, 0, 1)
            for i in range(4):
                turn_out("qcT", i, plain(qcT))
            follow_stage("nsa_in", 2048, 1, 2)
            key_norm(0)
            key_rope(0)
            key_double(0)
            follow_stage("nsa_in", 2048, 2, 3)
            e.wait_ge(sem["gl_ready"], 1)
            wide_h = lambda ap, n: ap.unsqueeze(2).to_broadcast([P, 16, n])
            for m in range(M):
                p3 = pc[:, m, :].rearrange("p (h c) -> p h c", c=15)
                for odd in range(2):
                    w = works["cmpS"] + 2 * m + odd
                    e.wait_ge(sem["work_ready"], w + 1)
                    e.tensor_tensor(p3[:, odd:16:2], bank[4 + w % 2][:, 0:120].rearrange("p (h c) -> p h c", c=15),
                                    cmp_neg[:, m, :].unsqueeze(1).to_broadcast([P, 8, 15]), ALU.add)\
                        .then_inc(sem["turned_dve"], 1)
                    e.wait_ge(sem["turned_dve"], plan.work_free[w][1])
                chain(e.tensor_reduce(stat[:, 16 * m:16 * m + 16], p3, AX.X, ALU.max, negate=True))
                e.tensor_tensor(p3, p3, wide_h(stat[:, 16 * m:16 * m + 16], 15), ALU.add).then_inc(sem["pc_shifted"], 1)
            chain(e.tensor_copy(q_rot[:, :, :], nsa[:, :, 0:D]))
            v = q_rot.rearrange("p m (h d) -> p m h d", d=64)
            tmp = [k_dup_tmp[:, i, :].rearrange("p (m h d) -> p m h d", m=M, h=16) for i in range(4)]
            rope(v[:, :, :, 0:8], v[:, :, :, 8:16], angles(0, 48, 56, 16), angles(1, 48, 56, 16),
                 v[:, :, :, 0:8], v[:, :, :, 8:16], tmp).then_inc(sem["q_roped"], 1)
            e.wait_ge(sem["q_roped"], 1)
            follow_stage("nsa_in", 2048, 3, 4)
            for m in range(M):
                p3 = pc[:, m, :].rearrange("p (h c) -> p h c", c=15)
                s_ = stat[:, 32 + 16 * m:48 + 16 * m]
                e.wait_ge(sem["pc_exp"], m + 1)
                chain(e.tensor_reduce(s_, p3, AX.X, ALU.add))
                e.tensor_tensor(p3, p3, cmp_keep[:, m, :].unsqueeze(1).to_broadcast([P, 16, 15]), ALU.mult)\
                    .then_inc(sem["pc_ready"], 1)
                chain(e.reciprocal(s_, s_))
                g = nsa[:, m, 2560:2608].rearrange("p (h b) -> p h b", b=3)[:, :, 0]
                chain(e.tensor_tensor(s_, s_, g, ALU.mult))
            key_sums(1)
            for m in range(M):
                for f in range(2):
                    w = works["cmpO"] + 2 * m + f
                    e.wait_ge(sem["work_ready"], w + 1)
                    s_ = stat[:, 32 + 16 * m + 8 * f:40 + 16 * m + 8 * f].unsqueeze(2).to_broadcast([P, 8, 64])
                    e.tensor_tensor(o_rows[:, m, 512 * f:512 * f + 512].rearrange("p (h d) -> p h d", d=64),
                                    bank[4 + w % 2][:, :].rearrange("p (h d) -> p h d", d=64), s_, ALU.mult)\
                        .then_inc(sem["turned_dve"], 1)
            for i in range(4):
                turn_out("qrT", i, plain(qrT))
            for a, name in enumerate(("sel", "win")):
                for i in range(2):
                    turn_out("kT%d" % a, i, plain(qk[:, 16 + 4 * a:20 + 4 * a, :]))
                attention(name, 16)
            e.memset(stat[:, 126:127], 0.0).then_inc(sem["o_rows_done"], 1)
            low_tiles("o1T")
            follow_stage("nsa_out", 0, 0, 3)
            piece_end(ATT_PIECES[-1])
            follow_stage("nsa_out", 0, 3, 4)
            follow_stage("nsa_out", 512)
            norm_stage(2)
            follow_stage("mlp_in0")
            follow_stage("mlp_out0")

            norm_stage(3)
            tmp = [scrA[:, 1, 256 * i:256 * i + 256].rearrange("p (m h d) -> p m h d", m=M, h=16) for i in range(4)]

            def diff_squares(a):
                for m in range(M):
                    e.wait_ge(sem["diff_sq"], 2 * a + m + 1)
                    src = scrA[:, m, :] if a == 0 else scrB[:, m * D:(m + 1) * D]
                    c = SS["diff"] + 32 * a + 16 * m
                    e.tensor_reduce(ss[:, c:c + 16], src.rearrange("p (h d) -> p h d", d=64), AX.X, ALU.add)\
                        .then_inc(sem["ss_diff%d" % a], 1)

            def diff_norm(a, m):
                v = dif[:, m, a * D:(a + 1) * D].rearrange("p (h d) -> p h d", d=64)
                e.wait_ge(sem["rs_diff%d" % a], 1)
                chain(scale_heads(v, SS["diff"] + 32 * a + 16 * m, 16, (dq_gain, dk_gain)[a]))

            def diff_rope(a):
                v = dif[:, :, a * D:(a + 1) * D].rearrange("p m (h d) -> p m h d", d=64)
                rope(v[:, :, :, 0:8], v[:, :, :, 8:16], angles(0, 48, 56, 16), angles(1, 48, 56, 16),
                     v[:, :, :, 0:8], v[:, :, :, 8:16], tmp).then_inc(sem["dqk_roped"], 1)
                e.wait_ge(sem["dqk_roped"], a + 1)

            follow_stage("diff_in", 0)
            follow_stage("diff_in", 512)
            diff_squares(0)
            follow_stage("diff_in", 1024)
            diff_norm(0, 0)
            follow_stage("diff_in", 1536, 0, 2)
            diff_norm(0, 1)
            follow_stage("diff_in", 1536, 2, 4)
            diff_rope(0)
            diff_squares(1)
            follow_stage("diff_in", 2048)
            diff_norm(1, 0)
            for i in range(4):
                turn_out("dqT", i, plain(dqT))
            follow_stage("diff_in", 2560, 0, 2)
            diff_norm(1, 1)
            follow_stage("diff_in", 2560, 2, 4)
            diff_rope(1)
            for i in range(4):
                turn_out("dkT", i, plain(dkT))
            attention("diff", 8, comps=2)
            low_tiles("o2T", 0, 2, cols[:, C_SUB:C_SUB + 1])
            norm_heads(1)
            follow_stage("diff_out", 0, 0, 1)
            low_tiles("o2T", 2, 4, cols[:, C_SUB:C_SUB + 1])
            follow_stage("diff_out", 0, 1, 4)
            follow_stage("diff_out", 512)
            norm_stage(4)
            follow_stage("mlp_in1")
            follow_stage("mlp_out1")
    return nc


NAMES = ["x", "c", "positions", "w_ada", "b_ada", "g_pre", "g_post", "w_in", "g_q_lat", "w_uq", "g_kv_lat", "w_ukv",
         "w_o_mla", "w_o_moba", "b_merge", "w_out", "c_2", "positions_2", "ln_mix_g_2", "ln_mlp_g_2", "w_ada_2",
         "b_ada_2", "w_mlp_in_2", "w_mlp_out_2", "nsa_w_in_2", "nsa_b_gate_2", "nsa_q_gain_2", "nsa_k_gain_2",
         "nsa_pe_k_2", "nsa_w_ck1_2", "nsa_w_ck2_2", "nsa_pe_v_2", "nsa_w_cv1_2", "nsa_w_cv2_2", "nsa_w_out_2",
         "diff_w_in_2", "diff_q_gain_2", "diff_k_gain_2", "diff_lq1_2", "diff_lk1_2", "diff_lq2_2", "diff_lk2_2",
         "diff_subln_g_2", "diff_w_out_2"]


def kernel(**inputs):
    import concourse.bacc as bacc
    from concourse.bass_utils import run_bass_kernel_spmd

    freq = [np.float32(10000.0) ** (-np.arange(h, dtype=np.float32) / np.float32(h)) for h in (16, 32)]
    freq.append(np.float32(500000.0) ** (-np.arange(0, 16, 2, dtype=np.float32) / np.float32(16)))
    arrays = {"inv_freq": np.concatenate(freq).astype(np.float32)}
    for name in NAMES:
        arrays[name] = np.ascontiguousarray(inputs[name])
    nc = bacc.Bacc("TRN2", target_bir_lowering=False, num_devices=1)
    t_in = {name: nc.dram_tensor("in_" + name, a.shape, mybir.dt.from_np(a.dtype), kind="ExternalInput").ap()
            for name, a in arrays.items()}
    out = nc.dram_tensor("out_x", (1, S, D), F32, kind="ExternalOutput").ap()
    build(nc, t_in, out)
    r = run_bass_kernel_spmd(nc, [{"in_" + k: v for k, v in arrays.items()}], core_ids=[0])
    return r.results[0]["out_x"]
```
